# Optimizing a Trainium2 kernel written in Bass

```python
import math
import jax, jax.numpy as jnp
from jax import lax
import numpy as np

D_MODEL = 1024
BATCH = 1
SEQ = 256
DEPTH = 1

CHUNK = 64
N_META = 16
Q_BLOCK = 128
SB_HEADS = 8
SB_HEAD_DIM = 64
SB_WIDTH = SB_HEADS * SB_HEAD_DIM
MLA_HEADS = 8
MLA_Q_LORA = 384
MLA_KV_LORA = 256
MLA_NOPE = 64
MLA_ROPE = 32
MLA_V = 64
MLA_WIDTH = MLA_HEADS * MLA_V
ROPE_THETA = 10000.0
N_BRANCH = 2
IN_COLS = 3 * SB_WIDTH + MLA_Q_LORA + MLA_KV_LORA + MLA_ROPE + N_BRANCH * D_MODEL
D_FF = 2816
EPS = 1e-6
NEG_INF = -1e30
PAD_CHUNK_ID = 2 ** 30


def rmsnorm(x, g):
    xf = x.astype(jnp.float32)
    y = xf * lax.rsqrt(jnp.mean(xf * xf, axis=-1, keepdims=True) + EPS)
    return (y * g.astype(jnp.float32)).astype(x.dtype)

def swiglu(h, w_gate, w_up, w_down):
    return (jax.nn.silu(h @ w_gate) * (h @ w_up)) @ w_down

def rope(x, pos):
    half = x.shape[-1] // 2
    inv = ROPE_THETA ** (-jnp.arange(half, dtype=jnp.float32) / half)
    ang = pos[:, None] * inv[None, :]
    cos = jnp.cos(ang).astype(x.dtype)
    sin = jnp.sin(ang).astype(x.dtype)
    x1, x2 = x[..., :half], x[..., half:]
    return jnp.concatenate([x1 * cos - x2 * sin, x1 * sin + x2 * cos], axis=-1)

def to_heads(t, n_heads):
    b, l, _ = t.shape
    return t.reshape(b, l, n_heads, -1).transpose(0, 2, 1, 3)

def from_heads(t):
    b, h, l, d = t.shape
    return t.transpose(0, 2, 1, 3).reshape(b, l, h * d)

def chunk_end(pos):
    if pos < N_META:
        return N_META
    return N_META + ((pos - N_META) // CHUNK + 1) * CHUNK

def stick_breaking_attention(q, k, v):
    lp, d = q.shape[2], q.shape[3]
    scale = d ** -0.5
    outs = []
    for blk in range(lp // Q_BLOCK):
        q0, q1 = blk * Q_BLOCK, (blk + 1) * Q_BLOCK
        z = jnp.einsum('bhtd,bhsd->bhts', q[:, :, q0:q1], k[:, :, :q1]).astype(jnp.float32) * scale
        strict = jnp.arange(q1)[None, :] < jnp.arange(q0, q1)[:, None]
        log_1m = jnp.where(strict, jax.nn.log_sigmoid(-z), 0.0)
        csum = jnp.cumsum(log_1m, axis=-1)
        log_a = jax.nn.log_sigmoid(z) + csum[..., -1:] - csum
        a = jnp.where(strict, jnp.exp(log_a), 0.0)
        outs.append(jnp.einsum('bhts,bhsd->bhtd', a.astype(v.dtype), v[:, :, :q1]))
    return jnp.concatenate(outs, axis=2)

def latent_attention(q_nope, q_rope, k_nope, k_rope, v, cid):
    lp = q_nope.shape[2]
    scale = (MLA_NOPE + MLA_ROPE) ** -0.5
    outs = []
    for blk in range(lp // Q_BLOCK):
        q0, q1 = blk * Q_BLOCK, (blk + 1) * Q_BLOCK
        kend = min(lp, chunk_end(q1 - 1))
        s = (jnp.einsum('bhtd,bhsd->bhts', q_nope[:, :, q0:q1], k_nope[:, :, :kend])
             + jnp.einsum('bhtd,bsd->bhts', q_rope[:, :, q0:q1], k_rope[:, :kend]))
        s = s.astype(jnp.float32) * scale
        mask = cid[None, :kend] <= cid[q0:q1, None]
        p = jax.nn.softmax(jnp.where(mask, s, NEG_INF), axis=-1)
        outs.append(jnp.einsum('bhts,bhsd->bhtd', p.astype(v.dtype), v[:, :, :kend]))
    return jnp.concatenate(outs, axis=2)

def hybrid_mixer(u, w_in, b_gate, q_norm_g, w_uq, kv_norm_g, w_ukv, w_sb_o, w_mla_o, w_out):
    bsz, l, _ = u.shape
    lp = -(-l // Q_BLOCK) * Q_BLOCK
    up = jnp.pad(u, ((0, 0), (0, lp - l), (0, 0)))
    proj = up @ w_in
    sizes = [SB_WIDTH, SB_WIDTH, SB_WIDTH, MLA_Q_LORA, MLA_KV_LORA, MLA_ROPE, N_BRANCH * D_MODEL]
    idx = np.cumsum(sizes)[:-1].tolist()
    sb_q, sb_k, sb_v, c_q, c_kv, k_r, gate_pre = jnp.split(proj, idx, axis=-1)

    pos = jnp.arange(lp)
    cid = jnp.where(pos < N_META, 0, 1 + (pos - N_META) // CHUNK)
    cid = jnp.where(pos < l, cid, PAD_CHUNK_ID)
    posf = pos.astype(jnp.float32)

    y_sb = stick_breaking_attention(to_heads(sb_q, SB_HEADS), to_heads(sb_k, SB_HEADS),
                                    to_heads(sb_v, SB_HEADS))
    y_sb = from_heads(y_sb) @ w_sb_o

    q = jnp.einsum('bld,dhe->bhle', rmsnorm(c_q, q_norm_g), w_uq)
    q_nope, q_rope = q[..., :MLA_NOPE], rope(q[..., MLA_NOPE:], posf)
    kv = jnp.einsum('bld,dhe->bhle', rmsnorm(c_kv, kv_norm_g), w_ukv)
    k_nope, v = kv[..., :MLA_NOPE], kv[..., MLA_NOPE:]
    k_rope = rope(k_r, posf)
    y_mla = latent_attention(q_nope, q_rope, k_nope, k_rope, v, cid)
    y_mla = from_heads(y_mla) @ w_mla_o

    g = jax.nn.sigmoid(gate_pre + b_gate)
    g_sb, g_mla = g[..., :D_MODEL], g[..., D_MODEL:]
    out = (g_sb * y_sb + g_mla * y_mla) @ w_out
    return out[:, :l]

def first_inputs(seed: int = 0) -> dict:
    key = jax.random.key(seed)
    ks = jax.random.split(key, 24)

    def w(k, shape, fan_in):
        return jax.random.normal(k, shape, jnp.float32) * fan_in ** -0.5

    def gain(k, n):
        return 1.0 + 0.02 * jax.random.normal(k, (DEPTH, n), jnp.float32)

    return {
        "x": jax.random.normal(ks[0], (BATCH, SEQ, D_MODEL), jnp.float32),
        "meta_tokens": jax.random.normal(ks[1], (N_META, D_MODEL), jnp.float32),
        "ffn1_pre_g": gain(ks[2], D_MODEL),
        "ffn1_w_gate": w(ks[3], (DEPTH, D_MODEL, D_FF), D_MODEL),
        "ffn1_w_up": w(ks[4], (DEPTH, D_MODEL, D_FF), D_MODEL),
        "ffn1_w_down": w(ks[5], (DEPTH, D_FF, D_MODEL), D_FF),
        "ffn1_post_g": gain(ks[6], D_MODEL),
        "mix_pre_g": gain(ks[7], D_MODEL),
        "w_in": w(ks[8], (DEPTH, D_MODEL, IN_COLS), D_MODEL),
        "b_gate": 0.02 * jax.random.normal(ks[9], (DEPTH, N_BRANCH * D_MODEL), jnp.float32),
        "q_norm_g": gain(ks[10], MLA_Q_LORA),
        "w_uq": w(ks[11], (DEPTH, MLA_Q_LORA, MLA_HEADS, MLA_NOPE + MLA_ROPE), MLA_Q_LORA),
        "kv_norm_g": gain(ks[12], MLA_KV_LORA),
        "w_ukv": w(ks[13], (DEPTH, MLA_KV_LORA, MLA_HEADS, MLA_NOPE + MLA_V), MLA_KV_LORA),
        "w_sb_o": w(ks[14], (DEPTH, SB_WIDTH, D_MODEL), SB_WIDTH),
        "w_mla_o": w(ks[15], (DEPTH, MLA_WIDTH, D_MODEL), MLA_WIDTH),
        "w_out": w(ks[16], (DEPTH, D_MODEL, D_MODEL), D_MODEL),
        "mix_post_g": gain(ks[17], D_MODEL),
        "ffn2_pre_g": gain(ks[18], D_MODEL),
        "ffn2_w_gate": w(ks[19], (DEPTH, D_MODEL, D_FF), D_MODEL),
        "ffn2_w_up": w(ks[20], (DEPTH, D_MODEL, D_FF), D_MODEL),
        "ffn2_w_down": w(ks[21], (DEPTH, D_FF, D_MODEL), D_FF),
        "ffn2_post_g": gain(ks[22], D_MODEL),
    }

def first_block(x, meta_tokens, ffn1_pre_g, ffn1_w_gate, ffn1_w_up, ffn1_w_down, ffn1_post_g,
              mix_pre_g, w_in, b_gate, q_norm_g, w_uq, kv_norm_g, w_ukv, w_sb_o, w_mla_o,
              w_out, mix_post_g, ffn2_pre_g, ffn2_w_gate, ffn2_w_up, ffn2_w_down, ffn2_post_g):
    bsz = x.shape[0]
    meta = jnp.broadcast_to(meta_tokens[None].astype(x.dtype), (bsz, N_META, x.shape[-1]))
    h = jnp.concatenate([meta, x], axis=1)
    for l in range(DEPTH):
        f = swiglu(rmsnorm(h, ffn1_pre_g[l]), ffn1_w_gate[l], ffn1_w_up[l], ffn1_w_down[l])
        h = h + 0.5 * rmsnorm(f, ffn1_post_g[l])
        m = hybrid_mixer(rmsnorm(h, mix_pre_g[l]), w_in[l], b_gate[l], q_norm_g[l], w_uq[l],
                         kv_norm_g[l], w_ukv[l], w_sb_o[l], w_mla_o[l], w_out[l])
        h = h + rmsnorm(m, mix_post_g[l])
        f = swiglu(rmsnorm(h, ffn2_pre_g[l]), ffn2_w_gate[l], ffn2_w_up[l], ffn2_w_down[l])
        h = h + 0.5 * rmsnorm(f, ffn2_post_g[l])
    return h[:, N_META:]


N_HEADS = 8
HEAD_DIM = 64
ATTN_WIDTH = N_HEADS * HEAD_DIM
CONV_WIDTH = D_MODEL // 2
CONV_KERNEL = 31
N_EXPERTS = 32
TOP_K = 4
D_EXPERT = D_MODEL
SWIGLU_LIMIT = 7.0
SWIGLU_ALPHA = 1.702
MOE_BLOCK = 128
RMS_EPS = 1e-5
LN_EPS = 1e-5
N_MOD = 6
COL_SIZES = (CONV_WIDTH, CONV_WIDTH,
             ATTN_WIDTH, ATTN_WIDTH, ATTN_WIDTH,
             N_HEADS,
             D_MODEL, D_MODEL)
IN_COLS_2 = sum(COL_SIZES)


def rms_norm(x, g):
    xf = x.astype(jnp.float32)
    y = xf * lax.rsqrt(jnp.mean(xf * xf, axis=-1, keepdims=True) + RMS_EPS)
    return (y * g.astype(jnp.float32)).astype(x.dtype)

def layer_norm(x, g, b):
    xf = x.astype(jnp.float32)
    mu = jnp.mean(xf, axis=-1, keepdims=True)
    var = jnp.mean(jnp.square(xf - mu), axis=-1, keepdims=True)
    y = (xf - mu) * lax.rsqrt(var + LN_EPS)
    return (y * g.astype(jnp.float32) + b.astype(jnp.float32)).astype(x.dtype)

def conv_module(u_val, u_gate, conv_w, conv_b, ln_g, ln_b, w_proj):
    a = u_val * jax.nn.sigmoid(u_gate)
    a = lax.conv_general_dilated(
        a, conv_w[:, None, :].astype(a.dtype), window_strides=(1,),
        padding=[(CONV_KERNEL - 1, 0)],
        dimension_numbers=('NWC', 'WIO', 'NWC'),
        feature_group_count=CONV_WIDTH) + conv_b
    a = jax.nn.silu(layer_norm(a, ln_g, ln_b))
    return a @ w_proj

def forgetting_attention(q, k, v, f_logit):
    B, S = q.shape[0], q.shape[1]
    n_blocks = S // Q_BLOCK
    log_f = jax.nn.log_sigmoid(f_logit.astype(jnp.float32))
    F = jnp.cumsum(log_f, axis=1).transpose(0, 2, 1)
    kh = k.transpose(0, 2, 1, 3)
    vh = v.transpose(0, 2, 1, 3)
    q_blocks = q.transpose(0, 2, 1, 3).reshape(B, N_HEADS, n_blocks, Q_BLOCK, HEAD_DIM).transpose(2, 0, 1, 3, 4)
    F_blocks = F.reshape(B, N_HEADS, n_blocks, Q_BLOCK).transpose(2, 0, 1, 3)
    k_pos = jnp.arange(S)
    scale = HEAD_DIM ** -0.5

    def one_block(args):
        qi, Fi, bi = args
        q_pos = bi * Q_BLOCK + jnp.arange(Q_BLOCK)
        s = jnp.einsum('bhqd,bhkd->bhqk', qi, kh).astype(jnp.float32) * scale
        s = s + Fi[..., :, None] - F[:, :, None, :]
        s = jnp.where(k_pos[None, :] <= q_pos[:, None], s, -jnp.inf)
        p = jax.nn.softmax(s, axis=-1)
        return jnp.einsum('bhqk,bhkd->bhqd', p.astype(vh.dtype), vh)

    out = lax.map(one_block, (q_blocks, F_blocks, jnp.arange(n_blocks)))
    return out.transpose(1, 0, 3, 2, 4).reshape(B, S, ATTN_WIDTH)

def moe_ffn(h, w_router, b_router, w1, b1, w2, b2):
    B, S, D = h.shape
    T = B * S
    A = T * TOP_K
    hf = h.reshape(T, D)
    logits = (hf @ w_router + b_router).astype(jnp.float32)
    top_v, top_e = lax.top_k(logits, TOP_K)
    gates = jax.nn.softmax(top_v, axis=-1)

    flat_e = top_e.reshape(A).astype(jnp.int32)
    flat_tok = (jnp.arange(A, dtype=jnp.int32) // TOP_K)
    flat_gate = gates.reshape(A)
    order = jnp.argsort(flat_e)
    se, stok, sg = flat_e[order], flat_tok[order], flat_gate[order]
    counts = jnp.bincount(flat_e, length=N_EXPERTS)
    padded = (counts + MOE_BLOCK - 1) // MOE_BLOCK * MOE_BLOCK
    pend = jnp.cumsum(padded)
    pstart = pend - padded
    ustart = jnp.cumsum(counts) - counts
    dest = pstart[se] + jnp.arange(A, dtype=jnp.int32) - ustart[se]
    P = A + N_EXPERTS * MOE_BLOCK
    n_blocks = P // MOE_BLOCK
    tok_buf = jnp.zeros((P,), jnp.int32).at[dest].set(stok)
    gate_buf = jnp.zeros((P,), jnp.float32).at[dest].set(sg)
    block_e = jnp.clip(jnp.searchsorted(pend, jnp.arange(n_blocks) * MOE_BLOCK, side='right'), 0, N_EXPERTS - 1)
    xb = hf[tok_buf].reshape(n_blocks, MOE_BLOCK, D)

    def expert_block(args):
        xi, e = args
        hc = xi @ w1[e] + b1[e]
        g, u = hc[:, :D_EXPERT], hc[:, D_EXPERT:]
        g = jnp.minimum(g, SWIGLU_LIMIT)
        u = jnp.clip(u, -SWIGLU_LIMIT, SWIGLU_LIMIT)
        hm = (u + 1.0) * (g * jax.nn.sigmoid(SWIGLU_ALPHA * g))
        return hm @ w2[e] + b2[e]

    yb = lax.map(expert_block, (xb, block_e)).reshape(P, D)
    y = jax.ops.segment_sum(yb.astype(jnp.float32) * gate_buf[:, None], tok_buf, num_segments=T)
    return y.astype(h.dtype).reshape(B, S, D)

def second_inputs(seed: int = 0) -> dict:
    key = jax.random.key(seed)
    ks = jax.random.split(key, 24)
    f32 = jnp.float32
    L, D = DEPTH, D_MODEL

    def nrm(k, shape, fan_in, mult=1.0):
        return jax.random.normal(k, shape, f32) * (mult * fan_in ** -0.5)

    return {
        "x": jax.random.normal(ks[0], (BATCH, SEQ, D), f32),
        "c": jax.random.normal(ks[1], (BATCH, D), f32),
        "w_ada": nrm(ks[2], (L, D, N_MOD * D), D, 0.5),
        "b_ada": 0.02 * jax.random.normal(ks[3], (L, N_MOD * D), f32),
        "norm1_g": 1.0 + 0.05 * jax.random.normal(ks[4], (L, D), f32),
        "w_in": nrm(ks[5], (L, D, IN_COLS_2), D),
        "b_forget": jax.random.uniform(ks[6], (L, N_HEADS), f32, 1.0, 4.0),
        "conv_w": nrm(ks[7], (L, CONV_KERNEL, CONV_WIDTH), CONV_KERNEL),
        "conv_b": 0.02 * jax.random.normal(ks[8], (L, CONV_WIDTH), f32),
        "conv_ln_g": 1.0 + 0.05 * jax.random.normal(ks[9], (L, CONV_WIDTH), f32),
        "conv_ln_b": 0.02 * jax.random.normal(ks[10], (L, CONV_WIDTH), f32),
        "w_conv_out": nrm(ks[11], (L, CONV_WIDTH, D), CONV_WIDTH),
        "w_attn_out": nrm(ks[12], (L, ATTN_WIDTH, D), ATTN_WIDTH),
        "w_out": nrm(ks[13], (L, D, D), D),
        "norm2_g": 1.0 + 0.05 * jax.random.normal(ks[14], (L, D), f32),
        "w_router": nrm(ks[15], (L, D, N_EXPERTS), D),
        "b_router": 0.01 * jax.random.normal(ks[16], (L, N_EXPERTS), f32),
        "w_exp_in": nrm(ks[17], (L, N_EXPERTS, D, 2 * D_EXPERT), D),
        "b_exp_in": 0.02 * jax.random.normal(ks[18], (L, N_EXPERTS, 2 * D_EXPERT), f32),
        "w_exp_out": nrm(ks[19], (L, N_EXPERTS, D_EXPERT, D), D_EXPERT),
        "b_exp_out": 0.02 * jax.random.normal(ks[20], (L, N_EXPERTS, D), f32),
        "final_g": 1.0 + 0.05 * jax.random.normal(ks[21], (D,), f32),
    }

def second_block(x, c, w_ada, b_ada, norm1_g, w_in, b_forget, conv_w, conv_b, conv_ln_g, conv_ln_b,
              w_conv_out, w_attn_out, w_out, norm2_g, w_router, b_router, w_exp_in, b_exp_in,
              w_exp_out, b_exp_out, final_g):
    B, S, D = x.shape
    offs = np.cumsum(COL_SIZES)[:-1].tolist()
    for l in range(DEPTH):
        mod = (jax.nn.silu(c) @ w_ada[l] + b_ada[l]).reshape(B, N_MOD, D)
        sh1, sc1, g1, sh2, sc2, g2 = (mod[:, i, None, :] for i in range(N_MOD))

        h = rms_norm(x, norm1_g[l]) * (1.0 + sc1) + sh1
        z = h @ w_in[l]
        u_val, u_gate, q, k, v, f_logit, gate_c, gate_a = jnp.split(z, offs, axis=-1)
        conv_out = conv_module(u_val, u_gate, conv_w[l], conv_b[l], conv_ln_g[l], conv_ln_b[l], w_conv_out[l])
        attn = forgetting_attention(q.reshape(B, S, N_HEADS, HEAD_DIM),
                                    k.reshape(B, S, N_HEADS, HEAD_DIM),
                                    v.reshape(B, S, N_HEADS, HEAD_DIM),
                                    f_logit + b_forget[l])
        attn_out = attn @ w_attn_out[l]
        mixed = jax.nn.sigmoid(gate_c) * conv_out + jax.nn.sigmoid(gate_a) * attn_out
        x = x + g1 * (mixed @ w_out[l])

        h2 = rms_norm(x, norm2_g[l]) * (1.0 + sc2) + sh2
        x = x + g2 * moe_ffn(h2, w_router[l], b_router[l], w_exp_in[l], b_exp_in[l], w_exp_out[l], b_exp_out[l])
    return rms_norm(x, final_g)


def setup_inputs(seed=0):
    out = dict(first_inputs(seed))
    for name, value in second_inputs(seed + 1).items():
        if name != "x":
            out[name + "_2"] = value
    return out


def reference(
    x, meta_tokens, ffn1_pre_g, ffn1_w_gate, ffn1_w_up, ffn1_w_down, ffn1_post_g, mix_pre_g,
    w_in, b_gate, q_norm_g, w_uq, kv_norm_g, w_ukv, w_sb_o, w_mla_o, w_out, mix_post_g,
    ffn2_pre_g, ffn2_w_gate, ffn2_w_up, ffn2_w_down, ffn2_post_g, c_2, w_ada_2, b_ada_2,
    norm1_g_2, w_in_2, b_forget_2, conv_w_2, conv_b_2, conv_ln_g_2, conv_ln_b_2, w_conv_out_2,
    w_attn_out_2, w_out_2, norm2_g_2, w_router_2, b_router_2, w_exp_in_2, b_exp_in_2,
    w_exp_out_2, b_exp_out_2, final_g_2,
):
    x = first_block(
        x, meta_tokens, ffn1_pre_g, ffn1_w_gate, ffn1_w_up, ffn1_w_down, ffn1_post_g, mix_pre_g,
        w_in, b_gate, q_norm_g, w_uq, kv_norm_g, w_ukv, w_sb_o, w_mla_o, w_out, mix_post_g,
        ffn2_pre_g, ffn2_w_gate, ffn2_w_up, ffn2_w_down, ffn2_post_g,
    )
    return second_block(
        x, c_2, w_ada_2, b_ada_2, norm1_g_2, w_in_2, b_forget_2, conv_w_2, conv_b_2,
        conv_ln_g_2, conv_ln_b_2, w_conv_out_2, w_attn_out_2, w_out_2, norm2_g_2, w_router_2,
        b_router_2, w_exp_in_2, b_exp_in_2, w_exp_out_2, b_exp_out_2, final_g_2,
    )


_drawn_inputs = setup_inputs


def setup_inputs(seed=0):
    import zlib

    import numpy as np

    out = dict(_drawn_inputs(seed))
    spreads = {}
    factors = {'ffn1_pre_g': 3.162,
     'ffn1_post_g': 4.167,
     'mix_pre_g': 2.759,
     'b_gate': 7.509,
     'q_norm_g': 8.0,
     'kv_norm_g': 8.0,
     'mix_post_g': 3.677,
     'ffn2_pre_g': 5.335,
     'ffn2_post_g': 7.506,
     'b_ada_2': 3.853,
     'norm1_g_2': 8.0,
     'conv_b_2': 55.12,
     'conv_ln_g_2': 38.978,
     'conv_ln_b_2': 64.0,
     'norm2_g_2': 3.195,
     'b_router_2': 29.313,
     'b_exp_in_2': 23.69,
     'b_exp_out_2': 64.0}
    for name, (base, spread) in spreads.items():
        noise = np.random.default_rng([zlib.crc32(name.encode()), seed]).standard_normal(out[name].shape)
        drawn = base * np.exp(spread * noise) if base else spread * noise
        out[name] = __import__('jax').numpy.asarray(drawn.astype(out[name].dtype))
    for name, factor in factors.items():
        out[name] = (out[name] * factor).astype(out[name].dtype)
    return out
```

```python
import concourse.bass as bass
from concourse import mybir
from concourse.alu_op_type import AluOpType as ALU
from contextlib import ExitStack
import numpy as np

P = 128
D = 1024
KD = D // P
SEQ = 256
META = 16
TOK = SEQ + META
FF = 2816
NF = FF // P
HEADS = 8
E = 32
TOPK = 4
EPS1 = 1e-6
EPS2 = 1e-5
MLA_SCALE = 96 ** -0.5
CONV_K = 31
CT = 4
PIECE = 2048
BLK = 16
RING = 11
SLOTS = 12
SLOT_TOK = 64
NEG = -1e30

FFN_PIECES = NF + NF // 2
MIX1_BLOCKS = 448
MIX2_BLOCKS = 416
MIX1_PIECES = MIX1_BLOCKS // BLK
MIX2_PIECES = MIX2_BLOCKS // BLK


def padded(n):
    return -(-n // RING) * RING


FFN1_AT = 0
MIX1_AT = FFN_PIECES + padded(MIX1_PIECES) - MIX1_PIECES
FFN2_AT = MIX1_AT + MIX1_PIECES
MIX2_AT = FFN2_AT + FFN_PIECES + padded(MIX2_PIECES) - MIX2_PIECES
DENSE = MIX2_AT + MIX2_PIECES
PAD1 = MIX1_AT - FFN_PIECES
PAD2 = MIX2_AT - FFN2_AT - FFN_PIECES


def real_piece(p):
    return not (FFN_PIECES <= p < MIX1_AT or FFN2_AT + FFN_PIECES <= p < MIX2_AT)


def stored(p):
    return sum(real_piece(q) for q in range(p))


def loads_of(p):
    return sum(real_piece(q) for q in range(p % RING, p + 1, RING))


COLS = {}


def _columns():
    at = 0
    for name, n in (("f1_pre", 8), ("f1_post", 8), ("mix_pre", 8), ("b_gate", 16), ("q_g", 3), ("kv_g", 2),
                    ("mix_post", 8), ("f2_pre", 8), ("f2_post", 8), ("b_ada", 48), ("n1_g", 8),
                    ("conv_b", 4), ("ln_g", 4), ("ln_b", 4), ("n2_g", 8), ("final_g", 8),
                    ("conv_w", CT * CONV_K), ("w_f", KD * HEADS), ("w_router", KD * E),
                    ("b_router", E), ("b_forget", 1)):
        COLS[name] = (at, n)
        at += n
    return at


NCOLS = _columns()

CONST = {}


def _const_columns():
    at = 0
    for name, n in (("ident", 128), ("ones", 128), ("neg_ones", 128), ("neg_tri_ge", 128), ("tri_le", 128),
                    ("strict", 128), ("cap", 128), ("mla_mask", 416), ("causal", 128), ("iota", 256),
                    ("cos", TOK), ("sin", TOK), ("sel", HEADS * 128), ("eps1", 1), ("eps2", 1), ("one", 1)):
        CONST[name] = (at, n)
        at += n
    return at


NCONST = _const_columns()


def shape_constants():
    c = np.zeros((P, NCONST), np.float32)

    def put(name, a):
        at, n = CONST[name]
        c[: a.shape[0], at:at + n] = a

    i, j = np.arange(128)[:, None], np.arange(128)[None, :]
    put("ident", np.eye(128))
    put("ones", np.ones((128, 128)))
    put("neg_ones", -np.ones((128, 128)))
    put("neg_tri_ge", -(i >= j).astype(np.float32))
    put("tri_le", (i <= j).astype(np.float32))
    put("strict", (i < j).astype(np.float32))
    put("cap", np.where(i < j, 3e38, NEG))
    later = np.where((i < 64) & (np.arange(64)[None, :] >= 0), NEG, 0.0)
    mask = np.zeros((128, 416))
    mask[:, META + 64:144] = later
    mask[:, 144 + META + 192:] = later
    put("mla_mask", mask)
    put("causal", np.where(j <= i, 0.0, NEG))
    put("iota", np.tile(np.arange(256), (128, 1)))
    inv = 10000.0 ** (-np.arange(16, dtype=np.float32) / 16)
    ang = (np.arange(TOK, dtype=np.float32)[None, :] * inv.astype(np.float32)[:, None]).astype(np.float32)
    put("cos", np.tile(np.concatenate([np.cos(ang), np.cos(ang)]), (4, 1)))
    put("sin", np.tile(np.concatenate([-np.sin(ang), np.sin(ang)]), (4, 1)))
    sel = np.zeros((HEADS, HEADS * 128))
    for h in range(HEADS):
        sel[h, h * 128:(h + 1) * 128] = 1.0
    put("sel", sel)
    put("eps1", np.full((128, 1), EPS1))
    put("eps2", np.full((128, 1), EPS2))
    put("one", np.ones((128, 1)))
    return c


def build(nc, xT_in, stream, ada, c_in, cols_in, const_in, w_exp_in, w_exp_out, b_exp, out):
    ENG = mybir.EngineType
    f32, i32, u32 = mybir.dt.float32, mybir.dt.int32, mybir.dt.uint32
    ACT = mybir.ActivationFunctionType
    AX = mybir.AxisListType
    PE_, ACT_, DVE_, SP_ = (ENG.PE, ENG.Activation, ENG.DVE, ENG.SP)
    ctx = ExitStack()
    with ctx:
        def sb(name, shape, dt=f32):
            return ctx.enter_context(nc.sbuf_tensor(name, shape, dt))

        def sem(name):
            return ctx.enter_context(nc.semaphore(name))

        ring = sb("ring", [P, SLOTS, PIECE])
        res = sb("res", [P, KD, TOK])
        nrm = sb("nrm", [P, KD, TOK])
        cst = sb("cst", [P, NCONST])
        col = sb("col", [P, NCOLS])
        small = sb("small", [P, 512])
        sq = sb("sq", [P, KD, TOK])
        rstd = sb("rstd", [P, TOK])
        rtmp = sb("rtmp", [P, TOK])
        count_i = sb("count_i", [1, E], i32)
        idx_u = sb("idx_u", [P, 2, 8], u32)
        ARENA = 16896
        arena = sb("arena", [P, ARENA])
        bank = [ctx.enter_context(nc.psum_tensor(f"bank{i}", [P, 512], f32)) for i in range(8)]

        def const(name, lo=0, hi=None, rows=P):
            at, n = CONST[name]
            return cst[0:rows, at + lo:at + (n if hi is None else hi)]

        def vec(name, i=0, n=1, rows=P):
            at, _ = COLS[name]
            return col[0:rows, at + i:at + i + n]

        class Area:

            def __init__(self, whole, at=0):
                self.whole, self.at = whole, at

            def take(self, *shape):
                n = int(np.prod(shape))
                v = self.whole[:, self.at:self.at + n]
                self.at += n
                assert self.at <= self.whole.shape[1], (self.at, self.whole.shape)
                if len(shape) == 2:
                    v = v.rearrange("p (a b) -> p a b", a=shape[0])
                if len(shape) == 3:
                    v = v.rearrange("p (a b c) -> p a b c", a=shape[0], b=shape[1])
                return v

        sm_area = Area(small)
        half_f1 = sm_area.take(8)
        half_f2 = sm_area.take(8)
        mod = sm_area.take(48)
        ada_acc = sm_area.take(2 * RING)
        g1s = sm_area.take(8)
        g2s = sm_area.take(8)
        c_col = sm_area.take(8)
        top = sm_area.take(2, 8)
        topi = sm_area.take(2, 8)
        tope = sm_area.take(2, 8)
        tops = sm_area.take(2, 2)
        smx = sm_area.take(2, 2)
        ssum = sm_area.take(2, 2)
        srec = sm_area.take(2, 2)
        gate = sm_area.take(2, E)
        slot = sm_area.take(2, E)
        csum = sm_area.take(E)
        ctmp = sm_area.take(E)

        a = Area(arena)
        hid = a.take(NF, TOK)
        sig = a.take(2, TOK)
        ada_w = a.take(2, D)
        c_all = a.take(D)
        ada_t = a.take(D)

        a = Area(arena)
        lat = a.take(7, TOK)
        sb_q = a.take(4, SEQ)
        sb_k = a.take(4, TOK)
        sb_v = a.take(3, 512)
        graw = a.take(16, SEQ)
        uq = a.take(8, SEQ)
        kn = a.take(4, TOK)
        v2 = a.take(3, 512)
        t_e = a.take(2, 640)
        t_sp = a.take(2, 640)
        flat_sq = sq[:, :, :].rearrange("p a b -> p (a b)")
        t_a = flat_sq[:, 0:1280].rearrange("p (a b) -> p a b", a=2)
        qr = uq[:, 4:6, :]
        kr = lat[:, 5, :]
        a2 = Area(arena, a.at - 2560)
        p_sb = a2.take(2, 416)
        pt_sb = a2.take(2, 640)
        y_area = ring[:, RING, :]
        y_sb = y_area[:, 0:1024].rearrange("p (a b) -> p a b", a=4)
        y_mla = y_area[:, 1024:2048].rearrange("p (a b) -> p a b", a=4)
        mix_o = graw[:, 0:8, :]
        mtmp = flat_sq[:, 1280:1792].rearrange("p (a b) -> p a b", a=2)

        a = Area(arena)
        ca = a.take(CT, SEQ + CONV_K - 1)
        cv = a.take(CT, SEQ)
        csg = a.take(2, SEQ)
        q2 = a.take(4, SEQ)
        k2 = a.take(4, SEQ)
        w2v = a.take(2, 512)
        lf = a.take(SEQ)
        lft = a.take(SEQ)
        lfn = a.take(2, HEADS)
        fcum = a.take(2, HEADS)
        neg_f = a.take(SEQ)
        graw2 = a.take(16, SEQ)
        p2 = a.take(2, 384)
        pt2 = a.take(2, 384)
        y2 = a.take(4, SEQ)
        lnm = a.take(SEQ)
        mt2 = a.take(2, SEQ)

        a = Area(arena)
        h2n = a.take(2, D)
        acc = a.take(KD, SEQ)
        lgt = a.take(2, E)
        msk = a.take(2, E)
        b_all = a.take(3 * D)
        S = a.take(2, SLOT_TOK)
        SG = a.take(2, 2, SLOT_TOK)
        onehot = a.take(SLOT_TOK)
        xg = a.take(512)
        xT = a.take(4, 2, SLOT_TOK)
        ST = a.take(2, P)
        gl = a.take(512)
        ul = a.take(512)
        eg = a.take(512)
        hmT = a.take(4, 2, SLOT_TOK)
        ye = a.take(512)
        fin = a.take(KD, SEQ)

        inputs_in = sem("inputs_in")
        slot_in = [sem(f"slot_in{s}") for s in range(SLOTS)]
        freed = sem("freed")
        ada_in = [sem(f"ada_in{i}") for i in range(2)]
        ada_used = sem("ada_used")
        ada_copied = sem("ada_copied")
        bias_in = sem("bias_in")
        stored_out = sem("stored_out")
        act_chain = sem("act_chain")
        dve_chain = sem("dve_chain")
        n_sq = sem("norm_squares")
        n_sum = sem("norm_sum")
        n_rs = sem("norm_rstd")
        n_out = sem("normed")
        proj = sem("projected")

        def bases(*parts):
            at, found = 0, {}
            for name, n in parts:
                found[name] = at
                at += n
            return found

        AT = {
            n_sq: bases(("f1_pre", 8), ("f1_post", 8), ("mix_pre", 8), ("cq", 3), ("ckv", 2), ("mix_post", 8),
                        ("f2_pre", 8), ("f2_post", 8), ("n1", 8), ("ln_var", 4), ("n2", 8), ("final", 8)),
            n_sum: bases(*((n, 1) for n in ("f1_pre", "f1_post", "mix_pre", "cq", "ckv", "mix_post", "f2_pre",
                                            "f2_post", "n1", "ln_mean", "ln_var", "n2", "final"))),
            n_out: bases(("f1_pre", 8), ("mix_pre", 8), ("cq", 3), ("ckv", 2), ("f2_pre", 8), ("n1", 8),
                         ("ln_var", 4), ("n2", 8)),
            proj: bases(("lat", 7), ("qk", 8), ("v", 1), ("uq", 8), ("ukv", 5), ("gates", 16), ("o1", 8),
                        ("w1", 8), ("conv", 4), ("f", 1), ("qk2", 8), ("v2", 1), ("gates2", 16), ("o2", 8),
                        ("w2", 8)),
        }
        AT[n_rs] = AT[n_sum]
        updated = {n: sem(f"residual_{n}") for n in ("f1", "m1", "f2", "m2")}
        up_ready = sem("up_ready")
        exp_ready = sem("exp_ready")
        c_silu = sem("c_silu")
        fin_x = sem("fin_x")
        hid_ready = sem("hid_ready")
        down_ready = sem("down_ready")
        down_out = sem("down_out")
        evac = {n: sem(f"evac_{n}") for n in ("lat", "qk", "v", "uq", "ukv", "gates", "o1", "w1",
                                              "conv", "qk2", "v2", "f", "gates2", "o2", "w2")}
        roped = sem("roped")
        z_ready = sem("z_ready")
        e_done = sem("e_done")
        sp_done = sem("sp_done")
        la_ready = sem("la_ready")
        cap_done = sem("cap_done")
        at_done = sem("at_done")
        av_done = sem("av_done")
        y_out = sem("y_out")
        soft = {k: {n: sem(f"{n}_{k}") for n in ("scores", "maxed", "exped", "normed", "pt", "pt_v", "pt_a",
                                                 "pv", "y")} for k in ("mla", "fa")}
        gates_ready = sem("gates_ready")
        conv_sig = sem("conv_sig")
        conv_in = sem("conv_in")
        conv_done = sem("conv_done")
        ln_in = sem("ln_in")
        conv_silu = sem("conv_silu")
        logf_ready = sem("logf_ready")
        logf_t = sem("logf_t")
        logf_n = sem("logf_n")
        f_sums = sem("f_sums")
        f_out = sem("f_out")
        logits = sem("logits")
        top_max = sem("top_max")
        top_exp = sem("top_exp")
        masked = sem("masked")
        counted = sem("counted")
        counts_ready = sem("counts_ready")
        nat = sem("nat")
        nat_out = sem("nat_out")
        m_sel = sem("m_sel")
        m_gath = sem("m_gath")
        m_xg = sem("m_xg")
        m_xt = sem("m_xt")
        m_xts = sem("m_xts")
        m_sts = sem("m_sts")
        m_hc = sem("m_hc")
        m_gl = sem("m_gl")
        m_eg = sem("m_eg")
        m_hm = sem("m_hm")
        m_hmt = sem("m_hmt")
        m_hms = sem("m_hms")
        m_y = sem("m_y")
        m_ys = sem("m_ys")
        m_comb = sem("m_comb")
        m_acc = sem("m_acc")
        moe_dve = sem("moe_dve")
        fin_ready = sem("fin_ready")

        def real(x):
            return x[:, META:TOK]

        block = ctx.enter_context(nc.Block())

        @block.sync
        def _(sp):
            sp.dma_start(cst[:, :], const_in).then_inc(inputs_in, 16)
            sp.dma_start(col[:, :], cols_in).then_inc(inputs_in, 16)
            sp.dma_start(res[:, :, :], xT_in.rearrange("(k p) t -> p k t", p=P)).then_inc(inputs_in, 16)

            def load_rounds(first, rounds, offset=0):
                with sp.Fori(0, rounds) as it:
                    for j in range(RING):
                        sp.wait_ge(freed, it * RING + (first + j + 1))
                        sp.dma_start(ring[:, j, :],
                                     stream[bass.ds(it * RING + (stored(first) + j), 1), :, :]
                                     .rearrange("o p n -> p (o n)")).then_inc(slot_in[j], 16)

            def load_piece(p):
                sp.wait_ge(freed, p + 1)
                sp.dma_start(ring[:, p % RING, :], stream[stored(p), :, :]).then_inc(slot_in[p % RING], 16)

            load_rounds(FFN1_AT, 3)
            for p in range(MIX1_AT, FFN2_AT):
                load_piece(p)
            load_rounds(FFN2_AT, 3)
            for p in range(MIX2_AT, DENSE):
                load_piece(p)

            def expert_piece(e, j):
                if j < 8:
                    return ring[:, j, :], w_exp_in[bass.ds(e * 8 + j, 1), :, :].rearrange("o p n -> p (o n)")
                return (ring[:, j, :].rearrange("p (t n) -> p t n", t=2),
                        w_exp_out[bass.ds(e * 8 + (j - 8) * 2, 2), :, :].rearrange("t p n -> p t n"))

            for j in range(SLOTS):
                if j < RING:
                    sp.wait_ge(freed, DENSE + j + 1)
                dst, src = expert_piece(0, j)
                sp.dma_start(dst, src).then_inc(slot_in[j], 16)
            sp.wait_ge(counts_ready, 1)
            cum = sp.alloc_register("sp_cum")
            n0 = sp.value_load(count_i[0:1, 0:1], min_val=1, max_val=4)
            sp.reg_mov(cum, 0)
            sp.reg_add(cum, cum, n0)
            with sp.Fori(1, E) as e:
                before = nc.snap(cum, engines=[SP_])
                for j in range(SLOTS):
                    sp.wait_ge(freed, before * SLOTS + (DENSE + RING + 1 - SLOTS + j))
                    dst, src = expert_piece(e, j)
                    sp.dma_start(dst, src).then_inc(slot_in[j], 16)
                n = sp.value_load(count_i[0:1, bass.ds(e, 1)], min_val=1, max_val=4)
                sp.reg_add(cum, cum, n)
            sp.wait_ge(fin_ready, KD)
            sp.dma_start(out.rearrange("(k p) t -> p k t", p=P), fin[:, :, :]).then_inc(stored_out, 16)
            sp.wait_ge(stored_out, 16)

        @block.tensor
        def _(pe):
            mm = nc.tensor.matmul
            pe.wait_ge(inputs_in, 48)

            def norm_sum(n, tiles, width):
                for m in range(tiles):
                    pe.wait_ge(n_sq, AT[n_sq][n] + m + 1)
                    last = mm(bank[7][:, 0:width], const("ones"), sq[:, m, 0:width],
                              start=(m == 0), stop=(m == tiles - 1))
                last.then_inc(n_sum, 1)

            def gives_back(p):
                return 1 + (PAD1 if p == MIX1_AT else PAD2 if p == MIX2_AT else 0)

            def ffn(f, at, lo):
                w = TOK - lo
                base = f * NF
                pe.wait_ge(n_out, AT[n_out]["f1_pre" if f == 0 else "f2_pre"] + KD)
                with pe.Fori(0, 2) as it:
                    for j in range(RING):
                        pe.wait_ge(slot_in[j], it * 16 + 16 * loads_of(at + j))
                        pe.wait_ge(hid_ready, it * RING + (base + j + (2 if j == 0 else 1)))
                        for g in range(2):
                            for k in range(KD):
                                c0 = (g * KD + k) * P
                                last = mm(bank[2 * (j % 2) + g][:, 0:w], ring[:, j, c0:c0 + P],
                                          nrm[:, k, lo:TOK], start=(k == 0), stop=(k == KD - 1))
                                if g == 0 and k == 0:
                                    last.then_inc(freed, 1)
                        last.then_inc(up_ready, 1)
                pe.wait_ge(hid_ready, base + NF + 2)
                cur = Cursor(at + NF)
                for m in range(KD):
                    pe.wait_ge(down_out, f * KD + m + 1)
                    tile(cur, bank[4 + m % 2][:, 0:w], lambda k: hid[:, k, 0:w], NF, down_ready)

            class Cursor:

                def __init__(self, piece):
                    self.b = piece * BLK
                    self.owed = 0

                def take(self, n=1):
                    p, c = self.b // BLK, (self.b % BLK) * P
                    begins = self.b % BLK == 0
                    if begins:
                        pe.wait_ge(slot_in[p % RING], 16 * loads_of(p))
                    self.b += n
                    return ring[:, p % RING, c:c + n * P], gives_back(p) if begins else 0

            def tile(cur, out_, rhs, n_k, ready=None):
                for k in range(n_k):
                    w, back = cur.take()
                    last = mm(out_, w, rhs(k), start=(k == 0), stop=(k == n_k - 1))
                    cur.owed += back
                    if cur.owed and k < n_k - 1:
                        last.then_inc(freed, cur.owed)
                        cur.owed = 0
                if ready is not None:
                    last.then_inc(ready, 1)

            def natural(cur, n_k, parts, ready):
                for k in range(n_k):
                    w, back = cur.take(4)
                    for n, (o, lhs) in enumerate(parts):
                        last = mm(o, lhs(k), w, start=(k == 0), stop=(k == n_k - 1))
                        if n == 0 and back + cur.owed:
                            last.then_inc(freed, back + cur.owed)
                            cur.owed = 0
                last.then_inc(ready, 1)

            norm_sum("f1_pre", KD, TOK)
            ffn(0, FFN1_AT, 0)
            norm_sum("f1_post", KD, TOK)
            norm_sum("mix_pre", KD, TOK)
            cur = Cursor(MIX1_AT)
            pe.wait_ge(n_out, AT[n_out]["mix_pre"] + KD)
            for i in range(7):
                if i >= 2:
                    pe.wait_ge(evac["lat"], i - 1)
                tile(cur, bank[i % 2][:, 0:TOK], lambda k: nrm[:, k, :], KD, proj)
            for i in range(8):
                if i >= 2:
                    pe.wait_ge(evac["qk"], i - 1)
                lo = META if i < 4 else 0
                tile(cur, bank[2 + i % 2][:, 0:TOK - lo], lambda k: nrm[:, k, lo:TOK], KD, proj)
            pe.wait_ge(evac["lat"], 7)
            v_parts = ((META, P), (META + P, P), (0, META))
            natural(cur, KD, [(bank[4 + t][0:n, :], lambda k, c0=c0, n=n: nrm[:, k, c0:c0 + n])
                              for t, (c0, n) in enumerate(v_parts)], proj)
            norm_sum("cq", 3, SEQ)
            for m in range(2):
                pe.wait_ge(n_sq, AT[n_sq]["ckv"] + m + 1)
                last = mm(bank[0][:, 0:TOK], const("ones"), sq[:, 4 + m, :], start=(m == 0), stop=(m == 1))
            last.then_inc(n_sum, 1)
            pe.wait_ge(n_out, AT[n_out]["cq"] + 3)
            pe.wait_ge(evac["qk"], 8)
            for i in range(8):
                if i >= 2:
                    pe.wait_ge(evac["uq"], i - 1)
                tile(cur, bank[2 + i % 2][:, 0:SEQ], lambda k: lat[:, k, META:TOK], 3, proj)
            pe.wait_ge(n_out, AT[n_out]["ckv"] + 2)
            for i in range(4):
                if i >= 2:
                    pe.wait_ge(evac["ukv"], i - 1)
                tile(cur, bank[i % 2][:, 0:TOK], lambda k: lat[:, 3 + k, :], 2, proj)
            pe.wait_ge(evac["v"], 3)
            natural(cur, 2, [(bank[4 + t][0:n, :], lambda k, c0=c0, n=n: lat[:, 3 + k, c0:c0 + n])
                             for t, (c0, n) in enumerate(v_parts)], proj)
            pe.wait_ge(evac["uq"], 8)
            pe.wait_ge(evac["ukv"], 7)

            def gate_tile(i, which):
                if i >= 2:
                    pe.wait_ge(evac[which], i - 1)
                tile(cur, bank[6 + i % 2][:, 0:SEQ], lambda k: nrm[:, k, META:TOK] if which == "gates"
                     else nrm[:, k, 0:SEQ], KD, proj)

            def rows(x, j, n=64):
                return x[64 * j:64 * j + n]

            def z(h):
                m, j = h // 2, h % 2
                if h >= 2:
                    pe.wait_ge(at_done, h - 1)
                X, Y = bank[h % 2], bank[2 + h % 2]
                pos = (64 * j, 0)
                kk, qq = rows(sb_k[:, m, :], j), rows(sb_q[:, m, :], j)
                mm(X[:, 0:256], kk[:, META:META + P], qq, start=True, stop=False, tile_position=pos,
                   skip_group_check=True)
                mm(X[:, 256:384], kk[:, META + P:TOK], qq[:, P:SEQ], start=False, stop=False, tile_position=pos,
                   skip_group_check=True)
                mm(Y[0:META, 0:256], kk[:, 0:META], qq, start=True, stop=False, tile_position=pos,
                   skip_group_check=True).then_inc(z_ready, 1)

            def suffix(h):
                pe.wait_ge(sp_done, h + 1)
                X, Y, sp_ = bank[h % 2], bank[2 + h % 2], t_sp[:, h % 2, :]
                tri, no = const("neg_tri_ge"), const("neg_ones")
                kw = dict(start=False, skip_group_check=True)
                mm(X[:, 0:256], tri, sp_[:, 0:256], stop=False, **kw)
                mm(X[:, 128:256], no, sp_[:, 256:384], stop=False, **kw)
                mm(X[:, 256:384], tri, sp_[:, 256:384], stop=True, **kw)
                mm(Y[0:META, 0:256], no[:, 0:META], sp_[:, 0:256], stop=False, **kw)
                mm(Y[0:META, 128:256], no[:, 0:META], sp_[:, 256:384], stop=False, **kw)
                mm(Y[0:META, 0:256], const("neg_tri_ge", 0, META, META), sp_[0:META, 384:640], stop=True,
                   **kw).then_inc(la_ready, 1)

            def pv(h, v, ready, parts):
                j = h % 2
                pos = (0, 64 * j)
                o = bank[4 + h // 2 % 2][64 * j:64 * j + 64, 0:SEQ]
                for n, (vt, n_rows, ap, lo) in enumerate(parts):
                    last = mm(o[:, lo:SEQ], v[0:n_rows, vt, 64 * h:64 * h + 64], ap,
                              start=(n == 0), stop=(n == len(parts) - 1), tile_position=pos,
                              skip_group_check=True)
                last.then_inc(ready, 1)

            def av(h):
                pe.wait_ge(at_done, h + 1)
                if h % 2 == 0 and h >= 4:
                    pe.wait_ge(y_out, h // 2 - 1)
                t = t_a[:, h % 2, :]
                pv(h, sb_v, av_done,
                   ((0, P, t[:, 0:256], 0), (1, P, t[:, 256:384], P), (2, META, t[0:META, 384:640], 0)))

            gi = 0
            z(0)
            for h in range(HEADS):
                if h + 1 < HEADS:
                    z(h + 1)
                gate_tile(gi, "gates")
                gi += 1
                suffix(h)
                if h:
                    av(h - 1)
            av(HEADS - 1)

            def scores_mla(h):
                m, j = h // 2, h % 2
                if h >= 2:
                    pe.wait_ge(soft["mla"]["maxed"], h - 1)
                if h == 0:
                    pe.wait_ge(at_done, HEADS)
                    pe.wait_ge(roped, 2)
                Bk = bank[h % 2]
                r, g = h // 4, 32 * (h % 4)
                qn_, kn_ = rows(uq[:, m, :], j), rows(kn[:, m, :], j)
                qr_, kr_ = qr[g:g + 32, r, :], kr[g:g + 32, :]
                for t, (c0, n) in enumerate(((0, 144), (144, TOK))):
                    mm(Bk[:, c0:c0 + n], qn_[:, t * P:t * P + P], kn_[:, 0:n], start=True, stop=False,
                       tile_position=(64 * j, 0), skip_group_check=True)
                    last = mm(Bk[:, c0:c0 + n], qr_[:, t * P:t * P + P], kr_[:, 0:n], start=False, stop=True,
                              tile_position=(g, 0), skip_group_check=True)
                last.then_inc(soft["mla"]["scores"], 1)

            def transposes(kind, h, p, parts):
                s = soft[kind]
                pe.wait_ge(s["normed"], h + 1)
                if h:
                    pe.wait_ge(s["pt_v"], h)
                    if kind == "mla":
                        pe.wait_ge(s["pt_a"], h)
                for o, i in parts:
                    last = nc.tensor.transpose(o, i, const("ident"))
                last.then_inc(s["pt"], 1)

            def pt_mla(h):
                p = p_sb[:, h % 2, :]
                b2, b3 = bank[2], bank[3]
                transposes("mla", h, p, ((b3[0:META, 0:P], p[:, 0:META]), (b2[:, 0:P], p[:, META:144]),
                                         (b3[0:META, P:256], p[:, 144:160]), (b2[:, P:256], p[:, 160:288]),
                                         (b2[:, 256:384], p[:, 288:416])))

            def pv_mla(h):
                s = soft["mla"]
                pe.wait_ge(s["pt_v"], h + 1)
                pe.wait_ge(s["pt_a"], h + 1)
                if h in (0, 2):
                    pe.wait_ge(y_out, 3 + h // 2)
                if h % 2 == 0 and h >= 4:
                    pe.wait_ge(s["y"], h // 2 - 1)
                t = pt_sb[:, h % 2, :]
                pv(h, v2, s["pv"],
                   ((0, P, t[:, 0:256], 0), (1, P, t[:, 256:384], P), (2, META, t[0:META, 384:640], 0)))

            scores_mla(0)
            for h in range(HEADS):
                if h + 1 < HEADS:
                    scores_mla(h + 1)
                gate_tile(gi, "gates")
                gi += 1
                pt_mla(h)
                if h:
                    pv_mla(h - 1)
            pv_mla(HEADS - 1)

            def out_proj(n, ya, yb_, ready_a, ready_b):
                ready_a()
                for m in range(KD):
                    if m >= 2:
                        pe.wait_ge(evac[n], m - 1)
                    b0 = 2 * (m % 2)
                    tile(cur, bank[b0][:, 0:SEQ], lambda k: ya[:, k, :], 4)
                    if m == 0:
                        ready_b()
                    tile(cur, bank[b0 + 1][:, 0:SEQ], lambda k: yb_[:, k, :], 4, proj)

            out_proj("o1", y_sb, y_mla, lambda: pe.wait_ge(y_out, 4),
                     lambda: (pe.wait_ge(soft["mla"]["y"], 4)))
            pe.wait_ge(evac["o1"], KD)
            for m in range(KD):
                if m >= 2:
                    pe.wait_ge(evac["w1"], m - 1)
                tile(cur, bank[4 + m % 2][:, 0:SEQ], lambda k: nrm[:, k, 0:SEQ], KD, proj)
            norm_sum("mix_post", KD, SEQ)
            norm_sum("f2_pre", KD, SEQ)
            ffn(1, FFN2_AT, META)
            norm_sum("f2_post", KD, SEQ)

            norm_sum("n1", KD, SEQ)
            cur = Cursor(MIX2_AT)
            pe.wait_ge(n_out, AT[n_out]["n1"] + KD)
            x2 = lambda k: nrm[:, k, 0:SEQ]
            for m in range(CT):
                if m >= 2:
                    pe.wait_ge(evac["conv"], m - 1)
                tile(cur, bank[2 * (m % 2)][:, 0:SEQ], x2, KD)
                tile(cur, bank[2 * (m % 2) + 1][:, 0:SEQ], x2, KD, proj)
            for k in range(KD):
                last = mm(bank[6][0:HEADS, 0:SEQ], vec("w_f", k * HEADS, HEADS), x2(k),
                          start=(k == 0), stop=(k == KD - 1))
            last.then_inc(proj, 1)
            for i in range(8):
                if i >= 2:
                    pe.wait_ge(evac["qk2"], i - 1)
                tile(cur, bank[4 + i % 2][:, 0:SEQ], x2, KD, proj)
            pe.wait_ge(evac["conv"], CT)
            natural(cur, KD, [(bank[t][:, :], lambda k, t=t: nrm[:, k, t * P:t * P + P]) for t in range(2)],
                    proj)
            pe.wait_ge(logf_ready, 1)
            for t in range(2):
                last = nc.tensor.transpose(bank[2][:, t * 8:t * 8 + 8], lf[0:8, t * P:t * P + P],
                                           const("ident", 0, 8, 8))
            last.then_inc(logf_t, 1)
            pe.wait_ge(logf_n, 1)
            kw = dict(skip_group_check=True)
            mm(bank[3][:, 0:8], const("tri_le"), lfn[:, 0, :], start=True, stop=False, **kw)
            mm(bank[3][:, 8:16], const("ones"), lfn[:, 0, :], start=False, stop=False, **kw)
            mm(bank[3][:, 8:16], const("tri_le"), lfn[:, 1, :], start=False, stop=True, **kw)
            mm(bank[2][0:8, 256:384], lfn[:, 0, :], const("tri_le"), start=True, stop=False, **kw)
            mm(bank[2][0:8, 384:512], lfn[:, 0, :], const("ones"), start=False, stop=False, **kw)
            mm(bank[2][0:8, 384:512], lfn[:, 1, :], const("tri_le"), start=False, stop=True,
               **kw).then_inc(f_sums, 1)
            pe.wait_ge(evac["qk2"], 8)
            pe.wait_ge(evac["v2"], 2)
            pe.wait_ge(f_out, 2)

            def scores_fa(h):
                m, j = h // 2, h % 2
                if h >= 2:
                    pe.wait_ge(soft["fa"]["maxed"], h - 1)
                Bk = bank[h % 2]
                q_, k_ = rows(q2[:, m, :], j), rows(k2[:, m, :], j)
                for t, (c0, n) in enumerate(((0, P), (P, SEQ))):
                    mm(Bk[:, c0:c0 + n], q_[:, t * P:t * P + P], k_[:, 0:n], start=True, stop=False,
                       tile_position=(64 * j, 0), skip_group_check=True)
                    last = mm(Bk[:, c0:c0 + n], const("sel", h * P, h * P + P, HEADS), neg_f[0:8, 0:n],
                              start=False, stop=True, skip_group_check=True)
                last.then_inc(soft["fa"]["scores"], 1)

            def pt_fa(h):
                p = p2[:, h % 2, :]
                b2 = bank[2]
                transposes("fa", h, p, ((b2[:, 0:P], p[:, 0:P]), (b2[:, P:256], p[:, P:256]),
                                        (b2[:, 256:384], p[:, 256:384])))

            def pv_fa(h):
                s = soft["fa"]
                pe.wait_ge(s["pt_v"], h + 1)
                if h % 2 == 0 and h >= 4:
                    pe.wait_ge(s["y"], h // 2 - 1)
                t = pt2[:, h % 2, :]
                pv(h, w2v, s["pv"], ((0, P, t[:, 0:256], 0), (1, P, t[:, 256:384], P)))

            pe.wait_ge(evac["f"], 1)
            scores_fa(0)
            for h in range(HEADS):
                if h + 1 < HEADS:
                    scores_fa(h + 1)
                gate_tile(2 * h, "gates2")
                gate_tile(2 * h + 1, "gates2")
                pt_fa(h)
                if h:
                    pv_fa(h - 1)
            pv_fa(HEADS - 1)
            pe.wait_ge(soft["fa"]["y"], 3)
            for m in range(CT):
                pe.wait_ge(conv_done, m + 1)
                last = mm(bank[4][:, 0:SEQ], const("ones"), cv[:, m, :], start=(m == 0), stop=(m == CT - 1))
            last.then_inc(n_sum, 1)
            pe.wait_ge(evac["gates2"], 16)
            norm_sum("ln_var", CT, SEQ)
            out_proj("o2", cv, y2, lambda: pe.wait_ge(conv_silu, CT), lambda: pe.wait_ge(soft["fa"]["y"], 4))
            pe.wait_ge(evac["o2"], KD)
            for m in range(KD):
                if m >= 2:
                    pe.wait_ge(evac["w2"], m - 1)
                tile(cur, bank[4 + m % 2][:, 0:SEQ], x2, KD, proj)
            norm_sum("n2", KD, SEQ)

            pe.wait_ge(n_out, AT[n_out]["n2"] + KD)
            for t in range(2):
                for k in range(KD):
                    last = mm(bank[t][:, 0:E], nrm[:, k, t * P:t * P + P], vec("w_router", k * E, E),
                              start=(k == 0), stop=(k == KD - 1))
            last.then_inc(logits, 1)
            for t in range(2):
                for k in range(KD):
                    b = bank[2 + 2 * t + k // 4]
                    last = nc.tensor.transpose(b[:, (k % 4) * P:(k % 4 + 1) * P], nrm[:, k, t * P:t * P + P],
                                               const("ident"))
            last.then_inc(nat, 1)
            pe.wait_ge(masked, 1)
            mm(bank[6][:, 0:E], const("strict"), msk[:, 0, :], start=True, stop=False, **kw)
            mm(bank[6][:, E:2 * E], const("ones"), msk[:, 0, :], start=False, stop=False, **kw)
            mm(bank[6][:, E:2 * E], const("strict"), msk[:, 1, :], start=False, stop=False, **kw)
            mm(bank[6][:, 2 * E:3 * E], const("ones"), msk[:, 0, :], start=False, stop=False, **kw)
            mm(bank[6][:, 2 * E:3 * E], const("ones"), msk[:, 1, :], start=False, stop=True,
               **kw).then_inc(counted, 1)

            pe.wait_ge(nat_out, 4)
            pe.wait_ge(bias_in, 16)
            pe.wait_ge(counts_ready, 1)
            cum = pe.alloc_register("pe_cum")
            pe.reg_mov(cum, 0)
            base_loads = [16 * loads_of(DENSE - RING + s) if s < RING else 0 for s in range(SLOTS)]
            with pe.Fori(0, E) as e:
                n = pe.value_load(count_i[0:1, bass.ds(e, 1)], min_val=1, max_val=4)
                before = nc.snap(cum, engines=[PE_])
                with pe.Fori(0, n) as b:
                    g = before + b
                    halves = [(j, (0, 64 * j), slice(64 * j, 64 * j + 64)) for j in range(2)]
                    pe.wait_ge(m_sel, g + 1)
                    for t in range(2):
                        for j, pos, pr in halves:
                            last = mm(bank[0][pr, :], S[:, t, :], h2n[:, t, 512 * j:512 * j + 512],
                                      start=(t == 0), stop=(t == 1), tile_position=pos)
                    last.then_inc(m_gath, 1)
                    pe.wait_ge(m_xg, g + 1)
                    for c in range(4):
                        nc.tensor.transpose(bank[1][:, c * P:c * P + P], xg[:, c * P:c * P + P], const("ident"))
                    for t in range(2):
                        last = nc.tensor.transpose(bank[4][:, t * P:t * P + P],
                                                   SG[:, t, :, :].rearrange("p a b -> p (a b)"), const("ident"))
                    last.then_inc(m_xt, 1)
                    pe.wait_ge(m_xts, g + 1)
                    for k in range(KD):
                        pe.wait_ge(slot_in[k], e * 16 + (base_loads[k] + 16))
                        for gu in range(2):
                            for j, pos, pr in halves:
                                c0 = gu * D + j * 512
                                last = mm(bank[2 + gu][pr, :], xT[:, k % 4, k // 4, :],
                                          ring[:, k, c0:c0 + 512], start=(k == 0), stop=False,
                                          tile_position=pos)
                                if gu == 0 and j == 0:
                                    last.then_inc(freed, 1)
                    for gu in range(2):
                        for j, pos, pr in halves:
                            c0 = gu * D + j * 512
                            last = mm(bank[2 + gu][pr, :], onehot[0:E, :], b_all[0:E, c0:c0 + 512],
                                      start=False, stop=True, tile_position=pos)
                    last.then_inc(m_hc, 1)
                    pe.wait_ge(m_hm, g + 1)
                    pe.wait_ge(m_sts, g + 1)
                    for c in range(4):
                        last = nc.tensor.transpose(bank[4][:, c * P:c * P + P], gl[:, c * P:c * P + P],
                                                   const("ident"))
                    last.then_inc(m_hmt, 1)
                    pe.wait_ge(m_hms, g + 1)
                    for k in range(KD):
                        s = 8 + k // 2
                        if k % 2 == 0:
                            pe.wait_ge(slot_in[s], e * 16 + (base_loads[s] + 16))
                        for j, pos, pr in halves:
                            c0 = (k % 2) * D + j * 512
                            last = mm(bank[5][pr, :], hmT[:, k % 4, k // 4, :], ring[:, s, c0:c0 + 512],
                                      start=(k == 0), stop=False, tile_position=pos)
                            if k % 2 == 0 and j == 0:
                                last.then_inc(freed, 1)
                    for j, pos, pr in halves:
                        last = mm(bank[5][pr, :], onehot[0:E, :], b_all[0:E, 2 * D + 512 * j:2 * D + 512 * j + 512],
                                  start=False, stop=True, tile_position=pos)
                    last.then_inc(m_y, 1)
                    pe.wait_ge(m_ys, g + 1)
                    for r in range(2):
                        for mp in range(2):
                            for j, _, pr in halves:
                                mt = 2 * r + mp
                                b_ = bank[(6 if r == 0 else 2) + j]
                                last = mm(b_[:, mp * 256:mp * 256 + 256], ye[pr, mt * P:mt * P + P],
                                          ST[pr, :, :].rearrange("p a b -> p (a b)"),
                                          start=True, stop=True, tile_position=(64 * j, 0))
                        last.then_inc(m_comb, 1)
                pe.reg_add(cum, cum, n)
            norm_sum("final", KD, SEQ)

        @block.scalar
        def _(act):
            A = nc.scalar.activation
            act.dma_start(c_all, c_in.partition_broadcast(P)).then_inc(inputs_in, 16)
            for i in range(2):
                act.dma_start(ada_w[:, i, :], ada[i, :, :]).then_inc(ada_in[i], 16)
            act.wait_ge(inputs_in, 64)
            seen = [0]

            def link(ins):
                seen[0] += 1
                ins.then_inc(act_chain, 1)
                act.wait_ge(act_chain, seen[0])

            tables = [None]

            def use(which):
                if tables[0] != which:
                    tables[0] = which
                    if isinstance(which, str):
                        act.preload_act_table_set(which)
                    else:
                        act.preload_act_table(which)

            def squares(n, tiles, src, after=None, first=0):
                for m in range(tiles):
                    if after is not None:
                        act.wait_ge(after, m + 1)
                    s = src(m)
                    A(sq[:, first + m, 0:s.shape[1]], s, ACT.Square).then_inc(n_sq, 1)

            def root(n, width, mean, eps, ps=None):
                use("natural_log_exp_and_others")
                act.wait_ge(n_sum, AT[n_sum][n] + 1)
                ps = bank[7] if ps is None else ps
                link(A(rtmp[:, 0:width], ps[:, 0:width], ACT.Ln, scale=1.0 / mean, bias=const(eps)))
                A(rstd[:, 0:width], rtmp[:, 0:width], ACT.Exp, scale=-0.5).then_inc(n_rs, 1)

            squares("f1_pre", KD, lambda m: res[:, m, :])
            root("f1_pre", TOK, D, "eps1")
            use(ACT.Silu)
            A(c_all, c_all, ACT.Silu).then_inc(c_silu, 1)
            with act.Fori(0, 2) as it:
                for j in range(RING):
                    act.wait_ge(up_ready, it * RING + (j + 1))
                    A(sig[:, j % 2, 0:TOK], bank[(j % 2) * 2][:, 0:TOK], ACT.Silu)\
                        .then_inc(exp_ready, 1)
                    for i in range(2):
                        act.wait_ge(ada_used, it * (2 * RING) + (2 * j + i + 2))
                        act.dma_start(ada_w[:, i, :],
                                      ada[bass.ds(it * (2 * RING) + (2 * j + i + 2), 1), :, :]
                                      .rearrange("o p n -> p (o n)")).then_inc(ada_in[i], 16)
            for i in range(2):
                act.wait_ge(ada_used, 4 * RING + i + 2)
                act.dma_start(ada_w[:, i, :], ada[4 * RING + 2 + i, :, :]).then_inc(ada_in[i], 16)
            for m in range(KD):
                act.wait_ge(down_ready, m + 1)
                b = bank[4 + m % 2][:, 0:TOK]
                A(sq[:, m, :], b, ACT.Square).then_inc(n_sq, 1)
                A(nrm[:, m, :], b, ACT.Copy).then_inc(down_out, 1)
            root("f1_post", TOK, D, "eps1")
            squares("mix_pre", KD, lambda m: res[:, m, :], updated["f1"])
            root("mix_pre", TOK, D, "eps1")
            for i in range(7):
                act.wait_ge(proj, AT[proj]["lat"] + i + 1)
                A(lat[:, i, :], bank[i % 2][:, 0:TOK], ACT.Copy).then_inc(evac["lat"], 1)
            act.wait_ge(evac["lat"], 5)
            for i in range(8):
                act.wait_ge(proj, AT[proj]["qk"] + i + 1)
                if i < 4:
                    A(sb_q[:, i, :], bank[2 + i % 2][:, 0:SEQ], ACT.Copy, scale=0.125).then_inc(evac["qk"], 1)
                else:
                    A(sb_k[:, i - 4, :], bank[2 + i % 2][:, 0:TOK], ACT.Copy).then_inc(evac["qk"], 1)
                if i == 2:
                    squares("cq", 3, lambda m: lat[:, m, META:TOK])
                    squares("ckv", 2, lambda m: lat[:, 3 + m, :], first=4)
            root("cq", SEQ, 384, "eps1")
            act.wait_ge(n_out, AT[n_out]["cq"] + 3)
            root("ckv", TOK, 256, "eps1", bank[0])
            act.wait_ge(proj, AT[proj]["v"] + 1)
            for t, n in enumerate((P, P, META)):
                A(sb_v[0:n, t, :], bank[4 + t][0:n, :], ACT.Copy).then_inc(evac["v"], 1)
            for i in range(8):
                act.wait_ge(proj, AT[proj]["uq"] + i + 1)
                A(uq[:, i, :], bank[2 + i % 2][:, 0:SEQ], ACT.Copy).then_inc(evac["uq"], 1)
            for i in range(4):
                act.wait_ge(proj, AT[proj]["ukv"] + i + 1)
                A(kn[:, i, :], bank[i % 2][:, 0:TOK], ACT.Copy).then_inc(evac["ukv"], 1)
            act.wait_ge(proj, AT[proj]["ukv"] + 5)
            for t, n in enumerate((P, P, META)):
                A(v2[0:n, t, :], bank[4 + t][0:n, :], ACT.Copy).then_inc(evac["ukv"], 1)

            def gate_evac(i, which):
                act.wait_ge(proj, AT[proj][which] + i + 1)
                if which == "gates":
                    A(graw[:, i, :], bank[6 + i % 2][:, 0:SEQ], ACT.Identity,
                      bias=vec("b_gate", i)).then_inc(evac[which], 1)
                else:
                    A(graw2[:, i, :], bank[6 + i % 2][:, 0:SEQ], ACT.Copy).then_inc(evac[which], 1)

            def open_gates(which, gr):
                use(ACT.Sigmoid)
                act.wait_ge(evac[which], 16)
                for m in range(KD):
                    A(gr[:, m, :], gr[:, m, :], ACT.Sigmoid)
                    A(gr[:, 8 + m, :], gr[:, 8 + m, :], ACT.Sigmoid).then_inc(gates_ready, 1)

            def softplus_part(h):
                act.wait_ge(z_ready, h + 1)
                X, Y, e_ = bank[h % 2], bank[2 + h % 2], t_e[:, h % 2, :]
                A(e_[:, 0:384], X[:, 0:384], ACT.Abs)
                link(A(e_[0:META, 384:640], Y[0:META, 0:256], ACT.Abs))
                for func, kw in ((ACT.Exp, dict(scale=-1.0)), (ACT.Ln, dict(bias=const("one")))):
                    A(e_[:, 0:384], e_[:, 0:384], func, **kw)
                    kw = dict(kw, bias=const("one", rows=META)) if "bias" in kw else kw
                    last = A(e_[0:META, 384:640], e_[0:META, 384:640], func, **kw)
                    if func == ACT.Exp:
                        link(last)
                last.then_inc(e_done, 1)

            def attend_exp(h):
                act.wait_ge(la_ready, h + 1)
                act.wait_ge(cap_done, h + 1)
                if h >= 2:
                    act.wait_ge(av_done, h - 1)
                X, Y, e_, t = bank[h % 2], bank[2 + h % 2], t_e[:, h % 2, :], t_a[:, h % 2, :]
                A(t[:, 128:256], X[:, 128:256], ACT.Exp)
                A(t[0:META, 384:640], Y[0:META, 0:256], ACT.Exp)
                A(t[:, 0:128], e_[:, 0:128], ACT.Exp)
                A(t[:, 256:384], e_[:, 256:384], ACT.Exp).then_inc(at_done, 1)

            def y_evac(h, dst, ready, done):
                if h >= 0 and h % 2:
                    act.wait_ge(ready, h + 1)
                    m = h // 2
                    A(dst[:, m, :], bank[4 + m % 2][:, 0:SEQ], ACT.Copy).then_inc(done, 1)

            softplus_part(0)
            for h in range(HEADS):
                if h + 1 < HEADS:
                    softplus_part(h + 1)
                gate_evac(h, "gates")
                attend_exp(h)
                y_evac(h - 1, y_sb, av_done, y_out)
            y_evac(HEADS - 1, y_sb, av_done, y_out)

            def soft_exp(kind, h, p, split):
                s = soft[kind]
                act.wait_ge(s["maxed"], h + 1)
                pp, i = p[:, h % 2, :], h % 2
                A(pp[:, 0:split], pp[:, 0:split], ACT.Exp, bias=smx[:, i, 0:1], accum_out=ssum[:, i, 0:1])
                A(pp[:, split:], pp[:, split:], ACT.Exp, bias=smx[:, i, 1:2],
                  accum_out=ssum[:, i, 1:2]).then_inc(s["exped"], 1)

            soft_exp("mla", 0, p_sb, 144)
            for h in range(HEADS):
                if h + 1 < HEADS:
                    soft_exp("mla", h + 1, p_sb, 144)
                gate_evac(8 + h, "gates")
                act.wait_ge(soft["mla"]["pt"], h + 1)
                if h >= 2:
                    act.wait_ge(soft["mla"]["pv"], h - 1)
                A(pt_sb[0:META, h % 2, 384:640], bank[3][0:META, 0:256], ACT.Copy)\
                    .then_inc(soft["mla"]["pt_a"], 1)
                y_evac(h - 1, y_mla, soft["mla"]["pv"], soft["mla"]["y"])
            y_evac(HEADS - 1, y_mla, soft["mla"]["pv"], soft["mla"]["y"])
            open_gates("gates", graw)
            for m in range(KD):
                act.wait_ge(proj, AT[proj]["w1"] + m + 1)
                b = bank[4 + m % 2][:, 0:SEQ]
                A(sq[:, m, 0:SEQ], b, ACT.Square).then_inc(n_sq, 1)
                A(mix_o[:, m, :], b, ACT.Copy).then_inc(evac["w1"], 1)
            root("mix_post", SEQ, D, "eps1")
            squares("f2_pre", KD, lambda m: real(res[:, m, :]), updated["m1"])
            root("f2_pre", SEQ, D, "eps1")
            use(ACT.Silu)
            with act.Fori(0, 2) as it:
                for j in range(RING):
                    act.wait_ge(up_ready, it * RING + (NF + j + 1))
                    A(sig[:, j % 2, 0:SEQ], bank[(j % 2) * 2][:, 0:SEQ], ACT.Silu)\
                        .then_inc(exp_ready, 1)
            for m in range(KD):
                act.wait_ge(down_ready, KD + m + 1)
                b = bank[4 + m % 2][:, 0:SEQ]
                A(sq[:, m, 0:SEQ], b, ACT.Square).then_inc(n_sq, 1)
                A(nrm[:, m, 0:SEQ], b, ACT.Copy).then_inc(down_out, 1)
            root("f2_post", SEQ, D, "eps1")

            squares("n1", KD, lambda m: real(res[:, m, :]), updated["f2"])
            root("n1", SEQ, D, "eps2")
            use(ACT.Sigmoid)
            for m in range(CT):
                act.wait_ge(proj, AT[proj]["conv"] + m + 1)
                if m >= 2:
                    act.wait_ge(evac["conv"], m - 1)
                A(csg[:, m % 2, :], bank[2 * (m % 2) + 1][:, 0:SEQ], ACT.Sigmoid).then_inc(conv_sig, 1)
            use("natural_log_exp_and_others")
            act.wait_ge(proj, AT[proj]["f"] + 1)
            link(A(lf[0:8, :], bank[6][0:8, 0:SEQ], ACT.Identity, bias=vec("b_forget", rows=8)))
            link(A(lft[0:8, :], lf[0:8, :], ACT.Abs))
            link(A(lft[0:8, :], lft[0:8, :], ACT.Exp, scale=-1.0))
            A(lft[0:8, :], lft[0:8, :], ACT.Ln, bias=const("one", rows=8)).then_inc(evac["f"], 1)
            for i in range(8):
                act.wait_ge(proj, AT[proj]["qk2"] + i + 1)
                b = bank[4 + i % 2][:, 0:SEQ]
                if i < 4:
                    A(q2[:, i, :], b, ACT.Copy, scale=0.125).then_inc(evac["qk2"], 1)
                else:
                    A(k2[:, i - 4, :], b, ACT.Copy).then_inc(evac["qk2"], 1)
            act.wait_ge(proj, AT[proj]["v2"] + 1)
            for t in range(2):
                A(w2v[:, t, :], bank[t][:, :], ACT.Copy).then_inc(evac["v2"], 1)
            act.wait_ge(logf_t, 1)
            A(lfn[:, :, :].rearrange("p a b -> p (a b)"), bank[2][:, 0:16], ACT.Copy).then_inc(logf_n, 1)
            act.wait_ge(f_sums, 1)
            A(fcum[:, :, :].rearrange("p a b -> p (a b)"), bank[3][:, 0:16], ACT.Copy).then_inc(f_out, 1)
            A(neg_f[0:8, :], bank[2][0:8, 256:512], ACT.Copy, scale=-1.0).then_inc(f_out, 1)
            soft_exp("fa", 0, p2, P)
            for h in range(HEADS):
                if h + 1 < HEADS:
                    soft_exp("fa", h + 1, p2, P)
                gate_evac(2 * h, "gates2")
                gate_evac(2 * h + 1, "gates2")
                act.wait_ge(soft["fa"]["pt"], h + 1)
                if h >= 2:
                    act.wait_ge(soft["fa"]["pv"], h - 1)
                A(pt2[:, h % 2, :], bank[2][:, 0:384], ACT.Copy).then_inc(soft["fa"]["pt_v"], 1)
                y_evac(h - 1, y2, soft["fa"]["pv"], soft["fa"]["y"])
            y_evac(HEADS - 1, y2, soft["fa"]["pv"], soft["fa"]["y"])
            act.wait_ge(n_sum, AT[n_sum]["ln_mean"] + 1)
            A(lnm, bank[4][:, 0:SEQ], ACT.Copy, scale=1.0 / 512).then_inc(n_rs, 1)
            squares("ln_var", CT, lambda m: cv[:, m, :], ln_in)
            root("ln_var", SEQ, 512, "eps2")
            use(ACT.Silu)
            for m in range(CT):
                act.wait_ge(n_out, AT[n_out]["ln_var"] + m + 1)
                A(cv[:, m, :], cv[:, m, :], ACT.Silu).then_inc(conv_silu, 1)
            open_gates("gates2", graw2)
            use("natural_log_exp_and_others")
            squares("n2", KD, lambda m: real(res[:, m, :]), evac["w2"])
            root("n2", SEQ, D, "eps2")
            act.dma_start(b_all[0:E, :], b_exp).then_inc(bias_in, 16)
            act.wait_ge(top_max, 1)
            for t in range(2):
                A(tope[:, t, 0:TOPK], top[:, t, 0:TOPK], ACT.Exp, bias=tops[:, t, 0:1],
                  accum_out=tops[:, t, 1:2]).then_inc(top_exp, 1)
            act.wait_ge(nat, 1)
            for t in range(2):
                for c in range(2):
                    A(h2n[:, t, c * 512:c * 512 + 512], bank[2 + 2 * t + c][:, :], ACT.Copy)\
                        .then_inc(nat_out, 1)

            act.wait_ge(counts_ready, 1)
            use(ACT.Sigmoid)
            cum = act.alloc_register("act_cum")
            act.reg_mov(cum, 0)
            with act.Fori(0, E) as e:
                n = act.value_load(count_i[0:1, bass.ds(e, 1)], min_val=1, max_val=4)
                before = nc.snap(cum, engines=[ACT_])
                with act.Fori(0, n) as b:
                    g = before + b
                    act.wait_ge(m_xt, g + 1)
                    A(ST[:, :, :].rearrange("p a b -> p (a b)"), bank[4][:, 0:256], ACT.Copy).then_inc(m_sts, 1)
                    act.wait_ge(m_gl, g + 1)
                    A(eg, gl, ACT.Sigmoid, scale=1.702).then_inc(m_eg, 1)
                    act.wait_ge(m_hmt, g + 1)
                    A(hmT[:, :, :, :].rearrange("p a b c -> p (a b c)"), bank[4][:, :], ACT.Copy).then_inc(m_hms, 1)
                    act.wait_ge(m_y, g + 1)
                    A(ye, bank[5][:, :], ACT.Copy).then_inc(m_ys, 1)
                act.reg_add(cum, cum, n)
            for m in range(KD):
                act.wait_ge(fin_x, m + 1)
                A(sq[:, m, 0:SEQ], fin[:, m, :], ACT.Square).then_inc(n_sq, 1)
            root("final", SEQ, D, "eps2")

        @block.vector
        def _(dve):
            V = nc.vector
            seen = [0]

            def link(ins, *waits):
                seen[0] += 1
                ins.then_inc(dve_chain, 1)
                dve.wait_ge(dve_chain, seen[0])

            def mark(ins):
                seen[0] += 1
                ins.then_inc(dve_chain, 1)

            def settle():
                dve.wait_ge(dve_chain, seen[0])

            def stt(out_, in0, scalar, in1, op0, op1):
                return V.scalar_tensor_tensor(out=out_, in0=in0, scalar=scalar, in1=in1, op0=op0, op1=op1)

            def ts(out_, in0, s1, s2, op0, op1=None):
                if op1 is None:
                    return V.tensor_scalar(out_, in0, s1, None, op0)
                return V.tensor_scalar(out_, in0, s1, s2, op0, op1)

            tt = V.tensor_tensor

            dve.sem_inc(freed, RING - 1)
            dve.sem_inc(hid_ready, 2)
            dve.sem_inc(down_out, 2)
            for s in (ada_used, ada_copied, m_acc):
                dve.sem_inc(s, 1)
            dve.wait_ge(inputs_in, 64)
            mark(ts(half_f1, vec("f1_post", 0, 8), 0.5, None, ALU.mult))
            mark(ts(half_f2, vec("f2_post", 0, 8), 0.5, None, ALU.mult))

            def normed(n, tiles, src, gain, dst):
                dve.wait_ge(n_rs, AT[n_rs][n] + 1)
                for m in range(tiles):
                    s = src(m)
                    stt(dst(m), s, gain(m), rstd[:, 0:s.shape[1]], ALU.mult, ALU.mult).then_inc(n_out, 1)

            def residual(n, src, gain, into, upd):
                dve.wait_ge(n_rs, AT[n_rs][n] + 1)
                at = seen[0]
                for m in range(KD):
                    s = src(m)
                    mark(stt(s, s, gain(m), rstd[:, 0:s.shape[1]], ALU.mult, ALU.mult))
                for m in range(KD):
                    dve.wait_ge(dve_chain, at + m + 1)
                    tt(into(m), into(m), src(m), ALU.add).then_inc(upd, 1)

            normed("f1_pre", KD, lambda m: res[:, m, :], lambda m: vec("f1_pre", m), lambda m: nrm[:, m, :])
            dve.wait_ge(c_silu, 1)

            def ada_tile(i, n, w, to):
                dve.wait_ge(ada_in[i], w)
                dve.wait_ge(ada_used, n + 1)
                V.tensor_tensor_reduce(out=ada_t, in0=ada_w[:, i, :], in1=c_all, scale=1.0, scalar=0.0,
                                       op0=ALU.mult, op1=ALU.add,
                                       accum_out=to).then_inc(ada_used, 1)

            def ffn(f, w):
                base = f * NF
                with dve.Fori(0, 2) as it:
                    if f == 0:
                        dve.wait_ge(ada_copied, it + 1)
                    for j in range(RING):
                        i = j % 2
                        dve.wait_ge(exp_ready, it * RING + (base + j + 1))
                        tt(hid[:, bass.ds(it * RING + j, 1), 0:w].rearrange("p o t -> p (o t)"), sig[:, i, 0:w],
                           bank[2 * i + 1][:, 0:w], ALU.mult).then_inc(hid_ready, 1)
                        if f == 0:
                            for i in range(2):
                                ada_tile(i, it * (2 * RING) + (2 * j + i), it * (16 * RING) + 16 * (j + 1),
                                         ada_acc[:, 2 * j + i:2 * j + i + 1])
                    if f == 0:
                        dve.wait_ge(ada_used, it * (2 * RING) + (2 * RING + 1))
                        V.tensor_copy(mod[:, bass.ds(it * (2 * RING), 2 * RING)], ada_acc)\
                            .then_inc(ada_copied, 1)

            ffn(0, TOK)
            for n in range(4 * RING, 48):
                ada_tile(n % 2, n, 16 * (n // 2 + 1), mod[:, n:n + 1])
            dve.wait_ge(ada_copied, 3)
            dve.wait_ge(ada_used, 49)
            link(tt(mod, mod, vec("b_ada", 0, 48), ALU.add))
            link(ts(g1s, mod[:, 8:16], 1.0, None, ALU.add))
            link(ts(g2s, mod[:, 32:40], 1.0, None, ALU.add))
            mark(tt(g1s, g1s, vec("n1_g", 0, 8), ALU.mult))
            mark(tt(g2s, g2s, vec("n2_g", 0, 8), ALU.mult))
            residual("f1_post", lambda m: nrm[:, m, :], lambda m: half_f1[:, m:m + 1], lambda m: res[:, m, :],
                     updated["f1"])
            dve.wait_ge(updated["f1"], KD)
            normed("mix_pre", KD, lambda m: res[:, m, :], lambda m: vec("mix_pre", m), lambda m: nrm[:, m, :])
            normed("cq", 3, lambda m: lat[:, m, META:TOK], lambda m: vec("q_g", m), lambda m: lat[:, m, META:TOK])
            normed("ckv", 2, lambda m: lat[:, 3 + m, :], lambda m: vec("kv_g", m), lambda m: lat[:, 3 + m, :])
            mark(tt(lat[:, 5, :], lat[:, 5, :], const("cos"), ALU.mult))
            mark(tt(lat[:, 6, :], lat[:, 6, :], const("sin"), ALU.mult))
            settle()
            tt(lat[:, 5, :], lat[:, 5, :], lat[:, 6, :], ALU.add).then_inc(roped, 1)
            dve.wait_ge(evac["uq"], 8)
            for m in range(2):
                mark(tt(uq[:, 4 + m, :], uq[:, 4 + m, :], const("cos", META), ALU.mult))
                mark(tt(uq[:, 6 + m, :], uq[:, 6 + m, :], const("sin", META), ALU.mult))
            settle()
            tt(uq[:, 4:6, :], uq[:, 4:6, :], uq[:, 6:8, :], ALU.add).then_inc(roped, 1)

            def softplus(h):
                dve.wait_ge(e_done, h + 1)
                X, Y = bank[h % 2], bank[2 + h % 2]
                e_, s = t_e[:, h % 2, :], t_sp[:, h % 2, :]
                mark(stt(s[:, 0:384], X[:, 0:384], 0.0, e_[:, 0:384], ALU.max, ALU.add))
                mark(stt(s[0:META, 384:640], Y[0:META, 0:256], 0.0, e_[0:META, 384:640], ALU.max, ALU.add))
                settle()
                tt(s[:, 0:128], s[:, 0:128], const("strict"), ALU.mult)
                tt(s[:, 256:384], s[:, 256:384], const("strict"), ALU.mult).then_inc(sp_done, 1)

            def cap_diagonal(h):
                dve.wait_ge(la_ready, h + 1)
                X, e_ = bank[h % 2], t_e[:, h % 2, :]
                tt(e_[:, 0:128], X[:, 0:128], const("cap"), ALU.min)
                tt(e_[:, 256:384], X[:, 256:384], const("cap"), ALU.min).then_inc(cap_done, 1)

            softplus(0)
            for h in range(HEADS):
                if h + 1 < HEADS:
                    softplus(h + 1)
                cap_diagonal(h)

            def soft_norm(kind, h, p, split):
                s = soft[kind]
                dve.wait_ge(s["exped"], h + 1)
                pp, i = p[:, h % 2, :], h % 2
                link(V.reciprocal(srec[:, i, :], ssum[:, i, :]))
                ts(pp[:, 0:split], pp[:, 0:split], srec[:, i, 0:1], None, ALU.mult)
                ts(pp[:, split:], pp[:, split:], srec[:, i, 1:2], None, ALU.mult).then_inc(s["normed"], 1)

            def soft_max(kind, h, p, split):
                pp, i = p[:, h % 2, :], h % 2
                mark(V.reduce_max(smx[:, i, 0:1], pp[:, 0:split], AX.X))
                mark(V.reduce_max(smx[:, i, 1:2], pp[:, split:], AX.X))
                settle()
                ts(smx[:, i, :], smx[:, i, :], -1.0, None, ALU.mult).then_inc(soft[kind]["maxed"], 1)

            def mla_scores(h):
                dve.wait_ge(soft["mla"]["scores"], h + 1)
                if h >= 2:
                    dve.wait_ge(soft["mla"]["pt"], h - 1)
                link(stt(p_sb[:, h % 2, :], bank[h % 2][:, 0:416], MLA_SCALE, const("mla_mask"),
                         ALU.mult, ALU.add))
                soft_max("mla", h, p_sb, 144)

            dve.wait_ge(av_done, HEADS)
            mla_scores(0)
            for h in range(HEADS):
                soft_norm("mla", h, p_sb, 144)
                if h + 1 < HEADS:
                    mla_scores(h + 1)
                dve.wait_ge(soft["mla"]["pt"], h + 1)
                if h >= 2:
                    dve.wait_ge(soft["mla"]["pv"], h - 1)
                V.tensor_copy(pt_sb[:, h % 2, 0:384], bank[2][:, 0:384]).then_inc(soft["mla"]["pt_v"], 1)

            def gated(n, gr, tmp):
                for m in range(KD):
                    dve.wait_ge(proj, AT[proj][n] + m + 1)
                    dve.wait_ge(gates_ready, (KD if n == "o2" else 0) + m + 1)
                    if m:
                        dve.wait_ge(evac[n], m)
                    b0 = 2 * (m % 2)
                    mark(tt(tmp[:, 0, :], bank[b0][:, 0:SEQ], gr[:, m, :], ALU.mult))
                    mark(tt(tmp[:, 1, :], bank[b0 + 1][:, 0:SEQ], gr[:, 8 + m, :], ALU.mult))
                    settle()
                    tt(nrm[:, m, 0:SEQ], tmp[:, 0, :], tmp[:, 1, :], ALU.add).then_inc(evac[n], 1)

            gated("o1", graw, mtmp)
            residual("mix_post", lambda m: mix_o[:, m, :], lambda m: vec("mix_post", m),
                     lambda m: real(res[:, m, :]), updated["m1"])
            dve.wait_ge(updated["m1"], KD)
            normed("f2_pre", KD, lambda m: real(res[:, m, :]), lambda m: vec("f2_pre", m),
                   lambda m: real(nrm[:, m, :]))
            ffn(1, SEQ)
            residual("f2_post", lambda m: nrm[:, m, 0:SEQ], lambda m: half_f2[:, m:m + 1],
                     lambda m: real(res[:, m, :]), updated["f2"])
            dve.wait_ge(updated["f2"], KD)

            def modulated(n, gains, shift):
                dve.wait_ge(n_rs, AT[n_rs][n] + 1)
                at = seen[0]
                for m in range(KD):
                    mark(stt(nrm[:, m, 0:SEQ], real(res[:, m, :]), gains[:, m:m + 1], rstd[:, 0:SEQ],
                             ALU.mult, ALU.mult))
                for m in range(KD):
                    dve.wait_ge(dve_chain, at + m + 1)
                    ts(nrm[:, m, 0:SEQ], nrm[:, m, 0:SEQ], mod[:, shift + m:shift + m + 1], None, ALU.add)\
                        .then_inc(n_out, 1)

            mark(V.memset(ca[:, :, 0:CONV_K - 1], 0.0))
            modulated("n1", g1s, 0)
            for m in range(CT):
                dve.wait_ge(conv_sig, m + 1)
                tt(ca[:, m, CONV_K - 1:], bank[2 * (m % 2)][:, 0:SEQ], csg[:, m % 2, :], ALU.mult)\
                    .then_inc(evac["conv"], 1)
            dve.wait_ge(evac["f"], 1)
            stt(lf[0:8, :], lf[0:8, :], 0.0, lft[0:8, :], ALU.min, ALU.subtract).then_inc(logf_ready, 1)
            dve.wait_ge(evac["conv"], CT)

            taps = [(m, k) for m in range(CT) for k in range(CONV_K)]

            def conv_taps(n):
                for _ in range(n):
                    if not taps:
                        return
                    m, k = taps.pop(0)
                    w = vec("conv_w", m * CONV_K + k)
                    x = ca[:, m, k:k + SEQ]
                    if k == 0:
                        link(ts(cv[:, m, :], x, w, vec("conv_b", m), ALU.mult, ALU.add))
                    elif k < CONV_K - 1:
                        link(stt(cv[:, m, :], x, w, cv[:, m, :], ALU.mult, ALU.add))
                    else:
                        stt(cv[:, m, :], x, w, cv[:, m, :], ALU.mult, ALU.add).then_inc(conv_done, 1)

            conv_taps(40)

            def fa_scores(h):
                dve.wait_ge(soft["fa"]["scores"], h + 1)
                if h >= 2:
                    dve.wait_ge(soft["fa"]["pt"], h - 1)
                p, b_ = p2[:, h % 2, :], bank[h % 2]
                mark(stt(p[:, 0:P], b_[:, 0:P], fcum[:, 0, h:h + 1], const("causal"), ALU.add, ALU.add))
                mark(ts(p[:, P:256], b_[:, P:256], fcum[:, 1, h:h + 1], None, ALU.add))
                mark(stt(p[:, 256:384], b_[:, 256:384], fcum[:, 1, h:h + 1], const("causal"), ALU.add, ALU.add))
                settle()
                soft_max("fa", h, p2, P)

            fa_scores(0)
            for h in range(HEADS):
                soft_norm("fa", h, p2, P)
                if h + 1 < HEADS:
                    fa_scores(h + 1)
                conv_taps(11)
            conv_taps(len(taps))
            dve.wait_ge(conv_done, CT)
            dve.wait_ge(n_rs, AT[n_rs]["ln_mean"] + 1)
            for m in range(CT):
                tt(cv[:, m, :], cv[:, m, :], lnm, ALU.subtract).then_inc(ln_in, 1)
            dve.wait_ge(n_rs, AT[n_rs]["ln_var"] + 1)
            dve.wait_ge(ln_in, CT)
            at = seen[0]
            for m in range(CT):
                mark(tt(cv[:, m, :], cv[:, m, :], rstd[:, 0:SEQ], ALU.mult))
            for m in range(CT):
                dve.wait_ge(dve_chain, at + m + 1)
                ts(cv[:, m, :], cv[:, m, :], vec("ln_g", m), vec("ln_b", m), ALU.mult, ALU.add)\
                    .then_inc(n_out, 1)
            gated("o2", graw2, mt2)
            for m in range(KD):
                dve.wait_ge(proj, AT[proj]["w2"] + m + 1)
                r = real(res[:, m, :])
                stt(r, bank[4 + m % 2][:, 0:SEQ], mod[:, 16 + m:17 + m], r, ALU.mult, ALU.add)\
                    .then_inc(evac["w2"], 1)
            dve.wait_ge(evac["w2"], KD)
            modulated("n2", g2s, 24)

            mark(V.memset(acc, 0.0))
            dve.wait_ge(logits, 1)
            for t in range(2):
                mark(tt(lgt[:, t, :], bank[t][:, 0:E], vec("b_router", 0, E), ALU.add))
            settle()
            for t in range(2):
                mark(V.max(top[:, t, :], lgt[:, t, :]))
            settle()
            for t in range(2):
                mark(V.max_index(idx_u[:, t, :], top[:, t, :], lgt[:, t, :]))
            settle()
            mark(V.tensor_copy(topi[:, :, :], idx_u[:, :, :]))
            for t in range(2):
                last = ts(tops[:, t, 0:1], top[:, t, 0:1], -1.0, None, ALU.mult)
            last.then_inc(top_max, 1)
            settle()
            for t in range(2):
                mark(ts(msk[:, t, :], const("iota", 0, E), topi[:, t, 0:1], None, ALU.is_equal))
            for j in range(1, TOPK):
                settle()
                for t in range(2):
                    last = stt(msk[:, t, :], const("iota", 0, E), topi[:, t, j:j + 1], msk[:, t, :],
                               ALU.is_equal, ALU.add)
                    if j < TOPK - 1:
                        mark(last)
            last.then_inc(masked, 1)
            dve.wait_ge(top_exp, 2)
            mark(V.reciprocal(tops[:, :, 1:2], tops[:, :, 1:2]))
            settle()
            for t in range(2):
                mark(ts(tope[:, t, 0:TOPK], tope[:, t, 0:TOPK], tops[:, t, 1:2], None, ALU.mult))
            settle()
            for t in range(2):
                mark(ts(gate[:, t, :], const("iota", 0, E), topi[:, t, 0:1], tope[:, t, 0:1],
                        ALU.is_equal, ALU.mult))
            for j in range(1, TOPK):
                settle()
                dve.wait_ge(masked, 1)
                for t, tmp in enumerate((ctmp, csum)):
                    mark(ts(tmp, const("iota", 0, E), topi[:, t, j:j + 1], tope[:, t, j:j + 1],
                            ALU.is_equal, ALU.mult))
                settle()
                for t, tmp in enumerate((ctmp, csum)):
                    mark(tt(gate[:, t, :], gate[:, t, :], tmp, ALU.add))
            settle()
            dve.wait_ge(counted, 1)
            for t in range(2):
                mark(stt(slot[:, t, :], bank[6][:, t * E:t * E + E], 1.0, msk[:, t, :], ALU.add, ALU.mult))
            counts = bank[6][0:1, 2 * E:3 * E]
            mark(ts(ctmp[0:1, :], counts, 64.0, 1.0, ALU.is_gt, ALU.add))
            for lim in (128.0, 192.0):
                settle()
                mark(stt(ctmp[0:1, :], counts, lim, ctmp[0:1, :], ALU.is_gt, ALU.add))
            settle()
            for t in range(2):
                mark(ts(slot[:, t, :], slot[:, t, :], 1.0, None, ALU.subtract))
            settle()
            V.tensor_copy(count_i[:, :], ctmp[0:1, :]).then_inc(counts_ready, 1)
            dve.wait_ge(counts_ready, 1)

            cum = dve.alloc_register("dve_cum")
            dve.reg_mov(cum, 0)
            with dve.Fori(0, E) as e:
                n = dve.value_load(count_i[0:1, bass.ds(e, 1)], min_val=1, max_val=4)
                before = nc.snap(cum, engines=[DVE_])
                with dve.Fori(0, n) as b:
                    g = before + b
                    iota_b = cst[:, bass.ds(b * SLOT_TOK + CONST["iota"][0], SLOT_TOK)]
                    dve.wait_ge(m_acc, g + 1)
                    for t in range(2):
                        place, weight = slot[:, t, bass.ds(e, 1)], gate[:, t, bass.ds(e, 1)]
                        V.tensor_scalar(S[:, t, :], iota_b, place, None, ALU.is_equal)
                        for i in range(2):
                            V.tensor_scalar(SG[:, t, i, :], iota_b, place, weight, ALU.is_equal, ALU.mult)
                    V.tensor_scalar(onehot[0:E, :], const("ones", 0, SLOT_TOK, E),
                                    cst[0:E, bass.ds(e + CONST["ident"][0], 1)], None, ALU.mult).then_inc(m_sel, 1)
                    dve.wait_ge(m_gath, g + 1)
                    V.tensor_copy(xg, bank[0][:, :]).then_inc(m_xg, 1)
                    dve.wait_ge(m_xt, g + 1)
                    V.tensor_copy(xT[:, :, :, :].rearrange("p a b c -> p (a b c)"), bank[1][:, :]).then_inc(m_xts, 1)
                    dve.wait_ge(m_hc, g + 1)
                    ts(gl, bank[2][:, :], 7.0, None, ALU.min).then_inc(m_gl, 1)
                    dve.wait_ge(m_gl, g + 1)
                    ts(ul, bank[3][:, :], 7.0, -7.0, ALU.min, ALU.max).then_inc(moe_dve, 1)
                    dve.wait_ge(moe_dve, g * 2 + 1)
                    stt(ul, ul, 1.0, gl, ALU.add, ALU.mult).then_inc(moe_dve, 1)
                    dve.wait_ge(m_eg, g + 1)
                    dve.wait_ge(moe_dve, g * 2 + 2)
                    tt(gl, ul, eg, ALU.mult).then_inc(m_hm, 1)
                    for r in range(2):
                        dve.wait_ge(m_comb, g * 2 + (r + 1))
                        for j in range(2):
                            av_ = acc[:, 4 * j + 2 * r:4 * j + 2 * r + 2, :]
                            last = tt(av_, av_, bank[(6 if r == 0 else 2) + j][:, :]
                                      .rearrange("p (a b) -> p a b", a=2), ALU.add)
                    last.then_inc(m_acc, 1)
                dve.reg_add(cum, cum, n)
            dve.wait_ge(m_acc, nc.snap(cum, engines=[DVE_]) + 1)
            for m in range(KD):
                stt(fin[:, m, :], acc[:, m, :], mod[:, 40 + m:41 + m], real(res[:, m, :]),
                    ALU.mult, ALU.add).then_inc(fin_x, 1)
            dve.wait_ge(n_rs, AT[n_rs]["final"] + 1)
            dve.wait_ge(fin_x, KD)
            for m in range(KD):
                stt(fin[:, m, :], fin[:, m, :], vec("final_g", m), rstd[:, 0:SEQ], ALU.mult, ALU.mult)\
                    .then_inc(fin_ready, 1)


def block_stream(mats):
    parts = []
    for w, kind in mats:
        k, n = w.shape
        if kind == "tiles":
            parts.append(w.reshape(k // P, P, n // P, P).transpose(1, 2, 0, 3).reshape(P, -1))
        else:
            parts.append(w.reshape(k // P, P, n).transpose(1, 0, 2).reshape(P, -1))
    s = np.concatenate(parts, axis=1)
    return s.reshape(P, -1, PIECE).transpose(1, 0, 2)


def interleave(a, b):
    k = a.shape[0]
    return np.stack([a.reshape(k, -1, P), b.reshape(k, -1, P)], axis=2).reshape(k, -1)


def column(v):
    return np.asarray(v).reshape(-1, P).T


def kernel(**inputs):
    from concourse import bacc
    from concourse.bass_utils import run_bass_kernel_spmd

    x = {k: np.asarray(v) for k, v in inputs.items()}
    w_in = x["w_in"][0]
    at = np.cumsum([0, 512, 512, 512, 384, 256, 32, 2048])
    sq_, sk_, sv_, cq_, ckv_, kr_, gt_ = [w_in[:, at[i]:at[i + 1]] for i in range(7)]

    def swap(w):
        return np.concatenate([w[..., 16:], w[..., :16]], axis=-1)

    uq = x["w_uq"][0]
    ukv = x["w_ukv"][0]
    krs = np.tile(kr_, (1, 4)), np.tile(swap(kr_), (1, 4))
    mix1 = block_stream([
        (np.concatenate([cq_, ckv_, krs[0], krs[1], sq_, sk_], axis=1), "tiles"), (sv_, "rows"),
        (np.concatenate([uq[..., :64].reshape(384, 512), uq[..., 64:].reshape(384, 256),
                         swap(uq[..., 64:]).reshape(384, 256)], axis=1), "tiles"),
        (ukv[..., :64].reshape(256, 512), "tiles"), (ukv[..., 64:].reshape(256, 512), "rows"),
        (gt_, "tiles"), (interleave(x["w_sb_o"][0], x["w_mla_o"][0]), "tiles"), (x["w_out"][0], "tiles")])
    w2 = x["w_in_2"][0]
    at = np.cumsum([0, 512, 512, 512, 512, 512, 8, 1024, 1024])
    val, gat, q2, k2, v2, wf, gc, ga = [w2[:, at[i]:at[i + 1]] for i in range(8)]
    mix2 = block_stream([
        (np.concatenate([interleave(val, gat), q2, k2], axis=1), "tiles"), (v2, "rows"),
        (np.concatenate([gc, ga], axis=1), "tiles"),
        (interleave(x["w_conv_out_2"][0], x["w_attn_out_2"][0]), "tiles"), (x["w_out_2"][0], "tiles")])

    def ffn(n):
        return block_stream([(interleave(x[f"{n}_w_gate"][0], x[f"{n}_w_up"][0]), "tiles"),
                             (x[f"{n}_w_down"][0], "tiles")])

    stream = np.ascontiguousarray(np.concatenate([ffn("ffn1"), mix1, ffn("ffn2"), mix2]))
    cols = {
        "f1_pre": column(x["ffn1_pre_g"]), "f1_post": column(x["ffn1_post_g"]), "mix_pre": column(x["mix_pre_g"]),
        "b_gate": column(x["b_gate"]), "q_g": column(x["q_norm_g"]), "kv_g": column(x["kv_norm_g"]),
        "mix_post": column(x["mix_post_g"]), "f2_pre": column(x["ffn2_pre_g"]),
        "f2_post": column(x["ffn2_post_g"]), "b_ada": column(x["b_ada_2"]), "n1_g": column(x["norm1_g_2"]),
        "conv_b": column(x["conv_b_2"]), "ln_g": column(x["conv_ln_g_2"]), "ln_b": column(x["conv_ln_b_2"]),
        "n2_g": column(x["norm2_g_2"]), "final_g": column(x["final_g_2"]),
        "conv_w": x["conv_w_2"][0].reshape(CONV_K, CT, P).transpose(2, 1, 0).reshape(P, -1),
        "w_f": wf.reshape(KD, P, HEADS).transpose(1, 0, 2).reshape(P, -1),
        "w_router": x["w_router_2"][0].reshape(KD, P, E).transpose(1, 0, 2).reshape(P, -1),
        "b_router": np.tile(x["b_router_2"], (P, 1)),
        "b_forget": np.concatenate([x["b_forget_2"][0], np.zeros(P - HEADS, np.float32)])[:, None],
    }
    arrays = {
        "xT_in": np.ascontiguousarray(np.concatenate([x["meta_tokens"], x["x"][0]]).T),
        "stream": stream,
        "ada": np.ascontiguousarray(x["w_ada_2"][0].T.reshape(48, P, D)),
        "c_in": np.ascontiguousarray(x["c_2"][0]),
        "cols_in": np.ascontiguousarray(np.concatenate([cols[k] for k in COLS], axis=1)),
        "const_in": shape_constants(),
        "w_exp_in": np.ascontiguousarray(x["w_exp_in_2"][0]).reshape(E * 8, P, 2 * D),
        "w_exp_out": np.ascontiguousarray(x["w_exp_out_2"][0]).reshape(E * 8, P, D),
        "b_exp": np.ascontiguousarray(np.concatenate([x["b_exp_in_2"][0], x["b_exp_out_2"][0]], axis=1)),
    }
    nc = bacc.Bacc("TRN2", target_bir_lowering=False, num_devices=1)
    args = {n: nc.dram_tensor(n, a.shape, mybir.dt.from_np(a.dtype), kind="ExternalInput").ap()
            for n, a in arrays.items()}
    out = nc.dram_tensor("outT", (D, SEQ), mybir.dt.float32, kind="ExternalOutput").ap()
    build(nc, out=out, **args)
    r = run_bass_kernel_spmd(nc, [arrays], core_ids=[0])
    return np.ascontiguousarray(r.results[0]["outT"].T)[None]
```

```python
import concourse.bass as bass
from concourse import mybir
from concourse.alu_op_type import AluOpType as ALU
from contextlib import ExitStack
import numpy as np

P = 128
D = 1024
KD = D // P
SEQ = 256
META = 16
TOK = SEQ + META
FF = 2816
NF = FF // P
HEADS = 8
E = 32
TOPK = 4
EPS1 = 1e-6
EPS2 = 1e-5
MLA_SCALE = 96 ** -0.5
CONV_K = 31
CT = 4
PIECE = 2048
BLK = 16
RING = 6
SLOTS = 12
SPLIT_BUFS = 3
SLOT_TOK = 64
MAX_BLOCKS = E + SEQ * TOPK // SLOT_TOK
NEG = -1e30

FFN_PIECES = NF + NF // 2
MIX1_BLOCKS = 448
MIX2_BLOCKS = 416
MIX1_PIECES = MIX1_BLOCKS // BLK
MIX2_PIECES = MIX2_BLOCKS // BLK


FFN1_AT = 0
MIX1_AT = FFN_PIECES
FFN2_AT = MIX1_AT + MIX1_PIECES
MIX2_AT = FFN2_AT + FFN_PIECES
DENSE = MIX2_AT + MIX2_PIECES
ROUNDS = DENSE // RING
assert DENSE % RING == 0 and FFN_PIECES % SPLIT_BUFS == 0 and RING % SPLIT_BUFS == 0 and RING % 2 == 0


def loads_of(p):
    return p // RING + 1


COLS = {}


def _columns():
    at = 0
    for name, n in (("f1_pre", 8), ("f1_post", 8), ("mix_pre", 8), ("b_gate", 16), ("q_g", 3), ("kv_g", 2),
                    ("mix_post", 8), ("f2_pre", 8), ("f2_post", 8), ("b_ada", 48), ("n1_g", 8),
                    ("conv_b", 4), ("ln_g", 4), ("ln_b", 4), ("n2_g", 8), ("final_g", 8),
                    ("conv_w", CT * CONV_K), ("w_f", KD * HEADS), ("w_router", KD * E),
                    ("b_router", E), ("b_forget", 1)):
        COLS[name] = (at, n)
        at += n
    return at


NCOLS = _columns()

CONST = {}


def _const_columns():
    at = 0
    for name, n in (("ident", 128), ("ones", 128), ("neg_ones", 128), ("neg_tri_ge", 128), ("tri_le", 128),
                    ("strict", 128), ("cap", 128), ("mla_mask", 416), ("causal", 128), ("iota", 256),
                    ("cos", TOK), ("sin", TOK), ("sel", HEADS * 128), ("eps1", 1), ("eps2", 1), ("one", 1)):
        CONST[name] = (at, n)
        at += n
    return at


NCONST = _const_columns()


def shape_constants():
    c = np.zeros((P, NCONST), np.float32)

    def put(name, a):
        at, n = CONST[name]
        c[: a.shape[0], at:at + n] = a

    i, j = np.arange(128)[:, None], np.arange(128)[None, :]
    put("ident", np.eye(128))
    put("ones", np.ones((128, 128)))
    put("neg_ones", -np.ones((128, 128)))
    put("neg_tri_ge", -(i >= j).astype(np.float32))
    put("tri_le", (i <= j).astype(np.float32))
    put("strict", (i < j).astype(np.float32))
    put("cap", np.where(i < j, 3e38, NEG))
    later = np.where((i < 64) & (np.arange(64)[None, :] >= 0), NEG, 0.0)
    mask = np.zeros((128, 416))
    mask[:, META + 64:144] = later
    mask[:, 144 + META + 192:] = later
    put("mla_mask", mask)
    put("causal", np.where(j <= i, 0.0, NEG))
    put("iota", np.tile(np.arange(256), (128, 1)))
    inv = 10000.0 ** (-np.arange(16, dtype=np.float32) / 16)
    ang = (np.arange(TOK, dtype=np.float32)[None, :] * inv.astype(np.float32)[:, None]).astype(np.float32)
    put("cos", np.tile(np.concatenate([np.cos(ang), np.cos(ang)]), (4, 1)))
    put("sin", np.tile(np.concatenate([-np.sin(ang), np.sin(ang)]), (4, 1)))
    sel = np.zeros((HEADS, HEADS * 128))
    for h in range(HEADS):
        sel[h, h * 128:(h + 1) * 128] = 1.0
    put("sel", sel)
    put("eps1", np.full((128, 1), EPS1))
    put("eps2", np.full((128, 1), EPS2))
    put("one", np.ones((128, 1)))
    return c


def build(nc, xT_in, stream, ada, c_in, cols_in, const_in, w_exp_in, w_exp_out, b_exp, out):
    ENG = mybir.EngineType
    f32, f32r, i32, u32 = mybir.dt.float32, mybir.dt.float32r, mybir.dt.int32, mybir.dt.uint32
    ACT = mybir.ActivationFunctionType
    AX = mybir.AxisListType
    PE_, ACT_, DVE_, SP_ = (ENG.PE, ENG.Activation, ENG.DVE, ENG.SP)
    ctx = ExitStack()
    with ctx:
        def sb(name, shape, dt=f32):
            return ctx.enter_context(nc.sbuf_tensor(name, shape, dt))

        def sem(name):
            return ctx.enter_context(nc.semaphore(name))

        place = [-(-nc.sbuf_base // 64) * 64]

        def at_place(name, shape, dt=f32, over=None):
            size = int(np.prod(shape[1:])) * 4
            offset = place[0] if over is None else over
            if over is None:
                place[0] += size
            return nc.alloc_sbuf_tensor_at(name, shape, dt, offset=offset), offset

        ring, ring_at = at_place("ring", [P, SLOTS, PIECE])
        res, _ = at_place("res", [P, KD, TOK])
        nrm, nrm_at = at_place("nrm", [P, KD, TOK])
        sq, sq_at = at_place("sq", [P, KD, TOK])
        ARENA = 16896
        arena, arena_at = at_place("arena", [P, ARENA])
        slot_bytes = PIECE * 4
        w_hi, _ = at_place("w_hi", [P, SPLIT_BUFS, PIECE], f32r, over=ring_at + RING * slot_bytes)
        w_lo, _ = at_place("w_lo", [P, SPLIT_BUFS, PIECE], f32r, over=ring_at + (RING + SPLIT_BUFS) * slot_bytes)
        x_hi, _ = at_place("x_hi", [P, KD, TOK], f32r, over=nrm_at)
        x_lo, _ = at_place("x_lo", [P, KD, TOK], f32r, over=sq_at)
        hid_hi, _ = at_place("hid_hi", [P, NF, TOK], f32r, over=arena_at)
        hid_lo, _ = at_place("hid_lo", [P, NF, TOK], f32r, over=arena_at + NF * TOK * 4)
        nc.bump_sbuf(place[0] - nc.sbuf_base)
        cst = sb("cst", [P, NCONST])
        col = sb("col", [P, NCOLS])
        small = sb("small", [P, 512])
        rstd = sb("rstd", [P, TOK])
        rtmp = sb("rtmp", [P, TOK])
        count_i = sb("count_i", [1, E + 1], i32)
        block_i = sb("block_i", [1, 2 * (MAX_BLOCKS + 1)], i32)
        idx_u = sb("idx_u", [P, 2, 8], u32)
        bank = [ctx.enter_context(nc.psum_tensor(f"bank{i}", [P, 512], f32)) for i in range(8)]

        def const(name, lo=0, hi=None, rows=P):
            at, n = CONST[name]
            return cst[0:rows, at + lo:at + (n if hi is None else hi)]

        def vec(name, i=0, n=1, rows=P):
            at, _ = COLS[name]
            return col[0:rows, at + i:at + i + n]

        class Area:

            def __init__(self, whole, at=0):
                self.whole, self.at = whole, at

            def take(self, *shape):
                n = int(np.prod(shape))
                v = self.whole[:, self.at:self.at + n]
                self.at += n
                assert self.at <= self.whole.shape[1], (self.at, self.whole.shape)
                if len(shape) == 2:
                    v = v.rearrange("p (a b) -> p a b", a=shape[0])
                if len(shape) == 3:
                    v = v.rearrange("p (a b c) -> p a b c", a=shape[0], b=shape[1])
                return v

        sm_area = Area(small)
        half_f1 = sm_area.take(8)
        half_f2 = sm_area.take(8)
        mod = sm_area.take(48)
        ada_acc = sm_area.take(4)
        g1s = sm_area.take(8)
        g2s = sm_area.take(8)
        c_col = sm_area.take(8)
        top = sm_area.take(2, 8)
        topi = sm_area.take(2, 8)
        tope = sm_area.take(2, 8)
        tops = sm_area.take(2, 2)
        smx = sm_area.take(2, 2)
        ssum = sm_area.take(2, 2)
        srec = sm_area.take(2, 2)
        gate = sm_area.take(2, E)
        slot = sm_area.take(2, E)
        csum = sm_area.take(E)
        ctmp = sm_area.take(E)
        nb_col = sm_area.take(1)
        cum_col = sm_area.take(1)

        a = Area(arena)
        x_all = arena[:, 0:KD * TOK].rearrange("p (a b) -> p a b", a=KD)
        a.take(2, NF, TOK)
        sig = a.take(2, TOK)
        hid = a.take(TOK)
        ada_w = a.take(2, D)
        c_all = a.take(D)
        ada_t = a.take(D)

        a = Area(arena)
        lat = a.take(7, TOK)
        sb_q = a.take(4, SEQ)
        sb_k = a.take(4, TOK)
        sb_v = a.take(3, 512)
        graw = a.take(16, SEQ)
        uq = a.take(8, SEQ)
        kn = a.take(4, TOK)
        v2 = a.take(3, 512)
        t_e = a.take(2, 640)
        t_sp = a.take(2, 640)
        flat_sq = sq[:, :, :].rearrange("p a b -> p (a b)")
        t_a = flat_sq[:, 0:1280].rearrange("p (a b) -> p a b", a=2)
        qr = uq[:, 4:6, :]
        kr = lat[:, 5, :]
        a2 = Area(arena, a.at - 2560)
        p_sb = a2.take(2, 416)
        pt_sb = a2.take(2, 640)
        y_area = ring[:, SLOTS - 1, :]
        y_sb = y_area[:, 0:1024].rearrange("p (a b) -> p a b", a=4)
        y_mla = y_area[:, 1024:2048].rearrange("p (a b) -> p a b", a=4)
        mix_o = graw[:, 0:8, :]
        mtmp = flat_sq[:, 1280:1792].rearrange("p (a b) -> p a b", a=2)

        a = Area(arena)
        ca = a.take(CT, SEQ + CONV_K - 1)
        cv = a.take(CT, SEQ)
        csg = a.take(2, SEQ)
        q2 = a.take(4, SEQ)
        k2 = a.take(4, SEQ)
        w2v = a.take(2, 512)
        lf = a.take(SEQ)
        lft = a.take(SEQ)
        lfn = a.take(2, HEADS)
        fcum = a.take(2, HEADS)
        neg_f = a.take(SEQ)
        graw2 = a.take(16, SEQ)
        p2 = a.take(2, 384)
        pt2 = a.take(2, 384)
        y2 = a.take(4, SEQ)
        lnm = a.take(SEQ)
        mt2 = a.take(2, SEQ)

        a = Area(arena)
        h2n = a.take(2, D)
        acc = a.take(KD, SEQ)
        lgt = a.take(2, E)
        msk = a.take(2, E)
        b_all = a.take(3 * D)
        S = a.take(2, SLOT_TOK)
        SG = a.take(2, 2, SLOT_TOK)
        onehot1 = a.take(SLOT_TOK)
        onehot2 = a.take(SLOT_TOK)
        past = a.take(MAX_BLOCKS + 1)
        table = a.take(2, MAX_BLOCKS + 1)
        xg = a.take(512)
        xT = a.take(4, 2, SLOT_TOK)
        ST = a.take(2, P)
        gl = a.take(512)
        ul = a.take(512)
        eg = a.take(512)
        hmT = a.take(4, 2, SLOT_TOK)
        ye = a.take(512)
        fin = a.take(KD, SEQ)

        inputs_in = sem("inputs_in")
        slot_in = [sem(f"slot_in{s}") for s in range(SLOTS)]
        freed = sem("freed")
        ada_in = [sem(f"ada_in{i}") for i in range(2)]
        ada_used = sem("ada_used")
        ada_copied = sem("ada_copied")
        bias_in = sem("bias_in")
        stored_out = sem("stored_out")
        act_chain = sem("act_chain")
        dve_chain = sem("dve_chain")
        n_sq = sem("norm_squares")
        n_sum = sem("norm_sum")
        n_rs = sem("norm_rstd")
        n_out = sem("normed")
        proj = sem("projected")

        def bases(*parts):
            at, found = 0, {}
            for name, n in parts:
                found[name] = at
                at += n
            return found

        AT = {
            n_sq: bases(("f1_pre", 8), ("f1_post", 8), ("mix_pre", 8), ("cq", 3), ("ckv", 2), ("mix_post", 8),
                        ("f2_pre", 8), ("f2_post", 8), ("n1", 8), ("ln_var", 4), ("n2", 8), ("final", 8)),
            n_sum: bases(*((n, 1) for n in ("f1_pre", "f1_post", "mix_pre", "cq", "ckv", "mix_post", "f2_pre",
                                            "f2_post", "n1", "ln_mean", "ln_var", "n2", "final"))),
            n_out: bases(("f1_pre", 8), ("mix_pre", 8), ("cq", 3), ("ckv", 2), ("f2_pre", 8), ("n1", 8),
                         ("ln_var", 4), ("n2", 8)),
            proj: bases(("lat", 7), ("qk", 8), ("v", 1), ("uq", 8), ("ukv", 5), ("gates", 16), ("o1", 8),
                        ("w1", 8), ("conv", 4), ("f", 1), ("qk2", 8), ("v2", 1), ("gates2", 16), ("o2", 8),
                        ("w2", 8)),
        }
        AT[n_rs] = AT[n_sum]
        updated = {n: sem(f"residual_{n}") for n in ("f1", "m1", "f2", "m2")}
        up_ready = sem("up_ready")
        exp_ready = sem("exp_ready")
        c_silu = sem("c_silu")
        fin_x = sem("fin_x")
        hid_ready = sem("hid_ready")
        hid_high = sem("hid_high")
        hid_split = sem("hid_split")
        x_high = sem("x_high")
        x_split = sem("x_split")
        w_high = sem("w_high")
        w_split = sem("w_split")
        down_ready = sem("down_ready")
        down_out = sem("down_out")
        evac = {n: sem(f"evac_{n}") for n in ("lat", "qk", "v", "uq", "ukv", "gates", "o1", "w1",
                                              "conv", "qk2", "v2", "f", "gates2", "o2", "w2")}
        roped = sem("roped")
        z_ready = sem("z_ready")
        e_done = sem("e_done")
        sp_done = sem("sp_done")
        la_ready = sem("la_ready")
        cap_done = sem("cap_done")
        at_done = sem("at_done")
        av_done = sem("av_done")
        y_out = sem("y_out")
        soft = {k: {n: sem(f"{n}_{k}") for n in ("scores", "maxed", "exped", "normed", "pt", "pt_v", "pt_a",
                                                 "pv", "y")} for k in ("mla", "fa")}
        gates_ready = sem("gates_ready")
        conv_sig = sem("conv_sig")
        conv_in = sem("conv_in")
        conv_done = sem("conv_done")
        ln_in = sem("ln_in")
        conv_silu = sem("conv_silu")
        logf_ready = sem("logf_ready")
        logf_t = sem("logf_t")
        logf_n = sem("logf_n")
        f_sums = sem("f_sums")
        f_out = sem("f_out")
        logits = sem("logits")
        top_max = sem("top_max")
        top_exp = sem("top_exp")
        masked = sem("masked")
        counted = sem("counted")
        counts_ready = sem("counts_ready")
        nat = sem("nat")
        nat_out = sem("nat_out")
        nb_ready = sem("nb_ready")
        cum_ready = sem("cum_ready")
        past_ready = sem("past_ready")
        table_sums = sem("table_sums")
        m_S = sem("m_S")
        m_SG = sem("m_SG")
        m_oh1 = sem("m_oh1")
        m_gath = sem("m_gath")
        m_xg = sem("m_xg")
        m_xt = sem("m_xt")
        m_xts = sem("m_xts")
        m_sts = sem("m_sts")
        m_hc = sem("m_hc")
        m_gl = sem("m_gl")
        m_eg = sem("m_eg")
        m_hm = sem("m_hm")
        m_hmt = sem("m_hmt")
        m_hms = sem("m_hms")
        m_y = sem("m_y")
        m_ys = sem("m_ys")
        m_comb = sem("m_comb")
        m_acc = sem("m_acc")
        moe_dve = sem("moe_dve")
        fin_ready = sem("fin_ready")

        def real(x):
            return x[:, META:TOK]

        block = ctx.enter_context(nc.Block())

        @block.sync
        def _(sp):
            sp.dma_start(cst[:, :], const_in).then_inc(inputs_in, 16)
            sp.dma_start(col[:, :], cols_in).then_inc(inputs_in, 16)
            sp.dma_start(res[:, :, :], xT_in.rearrange("(k p) t -> p k t", p=P)).then_inc(inputs_in, 16)

            def load_rounds(first, last):
                with sp.Fori(first, last) as it:
                    for j in range(RING):
                        sp.wait_ge(freed, it * RING + (j + 1))
                        sp.dma_start(ring[:, j, :], stream[bass.ds(it * RING + j, 1), :, :]
                                     .rearrange("o p n -> p (o n)")).then_inc(slot_in[j], 16)

            def expert_piece(e, j):
                if j < 8:
                    return ring[:, j, :], w_exp_in[bass.ds(e * 8 + j, 1), :, :].rearrange("o p n -> p (o n)")
                return (ring[:, j, :].rearrange("p (t n) -> p t n", t=2),
                        w_exp_out[bass.ds(e * 8 + (j - 8) * 2, 2), :, :].rearrange("t p n -> p t n"))

            early = ROUNDS - 2
            load_rounds(0, early)
            sp.wait_ge(n_sum, AT[n_sum]["n1"] + 1)
            for j in range(RING, SLOTS):
                dst, src = expert_piece(0, j)
                sp.dma_start(dst, src).then_inc(slot_in[j], 16)
            load_rounds(early, ROUNDS)
            for j in range(RING):
                sp.wait_ge(freed, DENSE + j + 1)
                dst, src = expert_piece(0, j)
                sp.dma_start(dst, src).then_inc(slot_in[j], 16)
            sp.wait_ge(counts_ready, 1)
            cum = sp.alloc_register("sp_cum")
            n0 = sp.value_load(count_i[0:1, 0:1], min_val=1, max_val=4)
            sp.reg_mov(cum, 0)
            sp.reg_add(cum, cum, n0)
            with sp.Fori(1, E) as e:
                before = nc.snap(cum, engines=[SP_])
                for j in range(SLOTS):
                    sp.wait_ge(freed, before * SLOTS + (DENSE + RING + 1 - SLOTS + j))
                    dst, src = expert_piece(e, j)
                    sp.dma_start(dst, src).then_inc(slot_in[j], 16)
                n = sp.value_load(count_i[0:1, bass.ds(e, 1)], min_val=1, max_val=4)
                sp.reg_add(cum, cum, n)
            sp.wait_ge(fin_ready, KD)
            sp.dma_start(out.rearrange("(k p) t -> p k t", p=P), fin[:, :, :]).then_inc(stored_out, 16)
            sp.wait_ge(stored_out, 16)

        @block.tensor
        def _(pe):
            mm = nc.tensor.matmul
            pe.wait_ge(inputs_in, 48)

            def norm_sum(n, tiles, width):
                for m in range(tiles):
                    pe.wait_ge(n_sq, AT[n_sq][n] + m + 1)
                    last = mm(bank[7][:, 0:width], const("ones"), sq[:, m, 0:width],
                              start=(m == 0), stop=(m == tiles - 1))
                last.then_inc(n_sum, 1)

            def three(out_, wh, wl, xh, xl, start, stop):
                begin = mm(out_, wh, xh, start=start, stop=False)
                mm(out_, wh, xl, start=False, stop=False)
                return begin, mm(out_, wl, xh, start=False, stop=stop)

            def ffn(f, at, lo):
                w = TOK - lo
                base = f * NF

                def up_tile(j, piece, hid_at):
                    pe.wait_ge(w_split, piece)
                    pe.wait_ge(hid_ready, hid_at)
                    for g in range(2):
                        for k in range(KD):
                            c0 = (g * KD + k) * P
                            b = j % SPLIT_BUFS
                            begin, last = three(bank[2 * (j % 2) + g][:, 0:w], w_hi[:, b, c0:c0 + P],
                                                w_lo[:, b, c0:c0 + P], x_hi[:, k, lo:TOK], x_lo[:, k, lo:TOK],
                                                k == 0, k == KD - 1)
                            if g == 0 and k == 0:
                                begin.then_inc(freed, 1)
                    last.then_inc(up_ready, 1)

                pe.wait_ge(x_split, (f + 1) * KD)
                with pe.Fori(0, NF // RING) as it:
                    for j in range(RING):
                        up_tile(j, it * RING + (f * FFN_PIECES + j + 1), it * RING + (base + j + 1))
                for j in range(NF // RING * RING, NF):
                    up_tile(j, f * FFN_PIECES + j + 1, base + j + 1)
                at_block = NF * BLK
                for m in range(KD):
                    pe.wait_ge(down_out, f * KD + m + 1)
                    for k in range(NF):
                        p, c0 = at_block // BLK, at_block % BLK * P
                        if c0 == 0:
                            pe.wait_ge(w_split, f * FFN_PIECES + p + 1)
                        if m == 0:
                            pe.wait_ge(hid_split, base + k + 2)
                        b = p % SPLIT_BUFS
                        begin, last = three(bank[4 + m % 2][:, 0:w], w_hi[:, b, c0:c0 + P], w_lo[:, b, c0:c0 + P],
                                            hid_hi[:, k, 0:w], hid_lo[:, k, 0:w], k == 0, k == NF - 1)
                        if c0 == 0:
                            begin.then_inc(freed, 1)
                        at_block += 1
                    last.then_inc(down_ready, 1)

            class Cursor:

                def __init__(self, piece):
                    self.b = piece * BLK
                    self.owed = 0

                def take(self, n=1):
                    p, c = self.b // BLK, (self.b % BLK) * P
                    begins = self.b % BLK == 0
                    if begins:
                        pe.wait_ge(slot_in[p % RING], 16 * loads_of(p))
                    self.b += n
                    return ring[:, p % RING, c:c + n * P], int(begins)

            def tile(cur, out_, rhs, n_k, ready=None):
                for k in range(n_k):
                    w, back = cur.take()
                    last = mm(out_, w, rhs(k), start=(k == 0), stop=(k == n_k - 1))
                    cur.owed += back
                    if cur.owed and k < n_k - 1:
                        last.then_inc(freed, cur.owed)
                        cur.owed = 0
                if ready is not None:
                    last.then_inc(ready, 1)

            def natural(cur, n_k, parts, ready):
                for k in range(n_k):
                    w, back = cur.take(4)
                    for n, (o, lhs) in enumerate(parts):
                        last = mm(o, lhs(k), w, start=(k == 0), stop=(k == n_k - 1))
                        if n == 0 and back + cur.owed:
                            last.then_inc(freed, back + cur.owed)
                            cur.owed = 0
                last.then_inc(ready, 1)

            norm_sum("f1_pre", KD, TOK)
            ffn(0, FFN1_AT, 0)
            norm_sum("f1_post", KD, TOK)
            norm_sum("mix_pre", KD, TOK)
            cur = Cursor(MIX1_AT)
            pe.wait_ge(n_out, AT[n_out]["mix_pre"] + KD)
            for i in range(7):
                if i >= 2:
                    pe.wait_ge(evac["lat"], i - 1)
                tile(cur, bank[i % 2][:, 0:TOK], lambda k: nrm[:, k, :], KD, proj)
            for i in range(8):
                if i >= 2:
                    pe.wait_ge(evac["qk"], i - 1)
                lo = META if i < 4 else 0
                tile(cur, bank[2 + i % 2][:, 0:TOK - lo], lambda k: nrm[:, k, lo:TOK], KD, proj)
            pe.wait_ge(evac["lat"], 7)
            v_parts = ((META, P), (META + P, P), (0, META))
            natural(cur, KD, [(bank[4 + t][0:n, :], lambda k, c0=c0, n=n: nrm[:, k, c0:c0 + n])
                              for t, (c0, n) in enumerate(v_parts)], proj)
            norm_sum("cq", 3, SEQ)
            for m in range(2):
                pe.wait_ge(n_sq, AT[n_sq]["ckv"] + m + 1)
                last = mm(bank[0][:, 0:TOK], const("ones"), sq[:, 4 + m, :], start=(m == 0), stop=(m == 1))
            last.then_inc(n_sum, 1)
            pe.wait_ge(n_out, AT[n_out]["cq"] + 3)
            pe.wait_ge(evac["qk"], 8)
            for i in range(8):
                if i >= 2:
                    pe.wait_ge(evac["uq"], i - 1)
                tile(cur, bank[2 + i % 2][:, 0:SEQ], lambda k: lat[:, k, META:TOK], 3, proj)
            pe.wait_ge(n_out, AT[n_out]["ckv"] + 2)
            for i in range(4):
                if i >= 2:
                    pe.wait_ge(evac["ukv"], i - 1)
                tile(cur, bank[i % 2][:, 0:TOK], lambda k: lat[:, 3 + k, :], 2, proj)
            pe.wait_ge(evac["v"], 3)
            natural(cur, 2, [(bank[4 + t][0:n, :], lambda k, c0=c0, n=n: lat[:, 3 + k, c0:c0 + n])
                             for t, (c0, n) in enumerate(v_parts)], proj)
            pe.wait_ge(evac["uq"], 8)
            pe.wait_ge(evac["ukv"], 7)

            def gate_tile(i, which):
                if i >= 2:
                    pe.wait_ge(evac[which], i - 1)
                tile(cur, bank[6 + i % 2][:, 0:SEQ], lambda k: nrm[:, k, META:TOK] if which == "gates"
                     else nrm[:, k, 0:SEQ], KD, proj)

            def rows(x, j, n=64):
                return x[64 * j:64 * j + n]

            def z(h):
                m, j = h // 2, h % 2
                if h >= 2:
                    pe.wait_ge(at_done, h - 1)
                X, Y = bank[h % 2], bank[2 + h % 2]
                pos = (64 * j, 0)
                kk, qq = rows(sb_k[:, m, :], j), rows(sb_q[:, m, :], j)
                mm(X[:, 0:256], kk[:, META:META + P], qq, start=True, stop=False, tile_position=pos,
                   skip_group_check=True)
                mm(X[:, 256:384], kk[:, META + P:TOK], qq[:, P:SEQ], start=False, stop=False, tile_position=pos,
                   skip_group_check=True)
                mm(Y[0:META, 0:256], kk[:, 0:META], qq, start=True, stop=False, tile_position=pos,
                   skip_group_check=True).then_inc(z_ready, 1)

            def suffix(h):
                pe.wait_ge(sp_done, h + 1)
                X, Y, sp_ = bank[h % 2], bank[2 + h % 2], t_sp[:, h % 2, :]
                tri, no = const("neg_tri_ge"), const("neg_ones")
                kw = dict(start=False, skip_group_check=True)
                mm(X[:, 0:256], tri, sp_[:, 0:256], stop=False, **kw)
                mm(X[:, 128:256], no, sp_[:, 256:384], stop=False, **kw)
                mm(X[:, 256:384], tri, sp_[:, 256:384], stop=True, **kw)
                mm(Y[0:META, 0:256], no[:, 0:META], sp_[:, 0:256], stop=False, **kw)
                mm(Y[0:META, 128:256], no[:, 0:META], sp_[:, 256:384], stop=False, **kw)
                mm(Y[0:META, 0:256], const("neg_tri_ge", 0, META, META), sp_[0:META, 384:640], stop=True,
                   **kw).then_inc(la_ready, 1)

            def pv(h, v, ready, parts):
                j = h % 2
                pos = (0, 64 * j)
                o = bank[4 + h // 2 % 2][64 * j:64 * j + 64, 0:SEQ]
                for n, (vt, n_rows, ap, lo) in enumerate(parts):
                    last = mm(o[:, lo:SEQ], v[0:n_rows, vt, 64 * h:64 * h + 64], ap,
                              start=(n == 0), stop=(n == len(parts) - 1), tile_position=pos,
                              skip_group_check=True)
                last.then_inc(ready, 1)

            def av(h):
                pe.wait_ge(at_done, h + 1)
                if h % 2 == 0 and h >= 4:
                    pe.wait_ge(y_out, h // 2 - 1)
                t = t_a[:, h % 2, :]
                pv(h, sb_v, av_done,
                   ((0, P, t[:, 0:256], 0), (1, P, t[:, 256:384], P), (2, META, t[0:META, 384:640], 0)))

            gi = 0
            z(0)
            for h in range(HEADS):
                if h + 1 < HEADS:
                    z(h + 1)
                gate_tile(gi, "gates")
                gi += 1
                suffix(h)
                if h:
                    av(h - 1)
            av(HEADS - 1)

            def scores_mla(h):
                m, j = h // 2, h % 2
                if h >= 2:
                    pe.wait_ge(soft["mla"]["maxed"], h - 1)
                if h == 0:
                    pe.wait_ge(at_done, HEADS)
                    pe.wait_ge(roped, 2)
                Bk = bank[h % 2]
                r, g = h // 4, 32 * (h % 4)
                qn_, kn_ = rows(uq[:, m, :], j), rows(kn[:, m, :], j)
                qr_, kr_ = qr[g:g + 32, r, :], kr[g:g + 32, :]
                for t, (c0, n) in enumerate(((0, 144), (144, TOK))):
                    mm(Bk[:, c0:c0 + n], qn_[:, t * P:t * P + P], kn_[:, 0:n], start=True, stop=False,
                       tile_position=(64 * j, 0), skip_group_check=True)
                    last = mm(Bk[:, c0:c0 + n], qr_[:, t * P:t * P + P], kr_[:, 0:n], start=False, stop=True,
                              tile_position=(g, 0), skip_group_check=True)
                last.then_inc(soft["mla"]["scores"], 1)

            def transposes(kind, h, p, parts):
                s = soft[kind]
                pe.wait_ge(s["normed"], h + 1)
                if h:
                    pe.wait_ge(s["pt_v"], h)
                    if kind == "mla":
                        pe.wait_ge(s["pt_a"], h)
                for o, i in parts:
                    last = nc.tensor.transpose(o, i, const("ident"))
                last.then_inc(s["pt"], 1)

            def pt_mla(h):
                p = p_sb[:, h % 2, :]
                b2, b3 = bank[2], bank[3]
                transposes("mla", h, p, ((b3[0:META, 0:P], p[:, 0:META]), (b2[:, 0:P], p[:, META:144]),
                                         (b3[0:META, P:256], p[:, 144:160]), (b2[:, P:256], p[:, 160:288]),
                                         (b2[:, 256:384], p[:, 288:416])))

            def pv_mla(h):
                s = soft["mla"]
                pe.wait_ge(s["pt_v"], h + 1)
                pe.wait_ge(s["pt_a"], h + 1)
                if h in (0, 2):
                    pe.wait_ge(y_out, 3 + h // 2)
                if h % 2 == 0 and h >= 4:
                    pe.wait_ge(s["y"], h // 2 - 1)
                t = pt_sb[:, h % 2, :]
                pv(h, v2, s["pv"],
                   ((0, P, t[:, 0:256], 0), (1, P, t[:, 256:384], P), (2, META, t[0:META, 384:640], 0)))

            scores_mla(0)
            for h in range(HEADS):
                if h + 1 < HEADS:
                    scores_mla(h + 1)
                gate_tile(gi, "gates")
                gi += 1
                pt_mla(h)
                if h:
                    pv_mla(h - 1)
            pv_mla(HEADS - 1)

            def out_proj(n, ya, yb_, ready_a, ready_b):
                ready_a()
                for m in range(KD):
                    if m >= 2:
                        pe.wait_ge(evac[n], m - 1)
                    b0 = 2 * (m % 2)
                    tile(cur, bank[b0][:, 0:SEQ], lambda k: ya[:, k, :], 4)
                    if m == 0:
                        ready_b()
                    tile(cur, bank[b0 + 1][:, 0:SEQ], lambda k: yb_[:, k, :], 4, proj)

            out_proj("o1", y_sb, y_mla, lambda: pe.wait_ge(y_out, 4),
                     lambda: (pe.wait_ge(soft["mla"]["y"], 4)))
            pe.wait_ge(evac["o1"], KD)
            for m in range(KD):
                if m >= 2:
                    pe.wait_ge(evac["w1"], m - 1)
                tile(cur, bank[4 + m % 2][:, 0:SEQ], lambda k: nrm[:, k, 0:SEQ], KD, proj)
            norm_sum("mix_post", KD, SEQ)
            norm_sum("f2_pre", KD, SEQ)
            ffn(1, FFN2_AT, META)
            norm_sum("f2_post", KD, SEQ)

            norm_sum("n1", KD, SEQ)
            cur = Cursor(MIX2_AT)
            pe.wait_ge(n_out, AT[n_out]["n1"] + KD)
            x2 = lambda k: nrm[:, k, 0:SEQ]
            for m in range(CT):
                if m >= 2:
                    pe.wait_ge(evac["conv"], m - 1)
                tile(cur, bank[2 * (m % 2)][:, 0:SEQ], x2, KD)
                tile(cur, bank[2 * (m % 2) + 1][:, 0:SEQ], x2, KD, proj)
            for k in range(KD):
                last = mm(bank[6][0:HEADS, 0:SEQ], vec("w_f", k * HEADS, HEADS), x2(k),
                          start=(k == 0), stop=(k == KD - 1))
            last.then_inc(proj, 1)
            for i in range(8):
                if i >= 2:
                    pe.wait_ge(evac["qk2"], i - 1)
                tile(cur, bank[4 + i % 2][:, 0:SEQ], x2, KD, proj)
            pe.wait_ge(evac["conv"], CT)
            natural(cur, KD, [(bank[t][:, :], lambda k, t=t: nrm[:, k, t * P:t * P + P]) for t in range(2)],
                    proj)
            pe.wait_ge(logf_ready, 1)
            for t in range(2):
                last = nc.tensor.transpose(bank[2][:, t * 8:t * 8 + 8], lf[0:8, t * P:t * P + P],
                                           const("ident", 0, 8, 8))
            last.then_inc(logf_t, 1)
            pe.wait_ge(logf_n, 1)
            kw = dict(skip_group_check=True)
            mm(bank[3][:, 0:8], const("tri_le"), lfn[:, 0, :], start=True, stop=False, **kw)
            mm(bank[3][:, 8:16], const("ones"), lfn[:, 0, :], start=False, stop=False, **kw)
            mm(bank[3][:, 8:16], const("tri_le"), lfn[:, 1, :], start=False, stop=True, **kw)
            mm(bank[2][0:8, 256:384], lfn[:, 0, :], const("tri_le"), start=True, stop=False, **kw)
            mm(bank[2][0:8, 384:512], lfn[:, 0, :], const("ones"), start=False, stop=False, **kw)
            mm(bank[2][0:8, 384:512], lfn[:, 1, :], const("tri_le"), start=False, stop=True,
               **kw).then_inc(f_sums, 1)
            pe.wait_ge(evac["qk2"], 8)
            pe.wait_ge(evac["v2"], 2)
            pe.wait_ge(f_out, 2)

            def scores_fa(h):
                m, j = h // 2, h % 2
                if h >= 2:
                    pe.wait_ge(soft["fa"]["maxed"], h - 1)
                Bk = bank[h % 2]
                q_, k_ = rows(q2[:, m, :], j), rows(k2[:, m, :], j)
                for t, (c0, n) in enumerate(((0, P), (P, SEQ))):
                    mm(Bk[:, c0:c0 + n], q_[:, t * P:t * P + P], k_[:, 0:n], start=True, stop=False,
                       tile_position=(64 * j, 0), skip_group_check=True)
                    last = mm(Bk[:, c0:c0 + n], const("sel", h * P, h * P + P, HEADS), neg_f[0:8, 0:n],
                              start=False, stop=True, skip_group_check=True)
                last.then_inc(soft["fa"]["scores"], 1)

            def pt_fa(h):
                p = p2[:, h % 2, :]
                b2 = bank[2]
                transposes("fa", h, p, ((b2[:, 0:P], p[:, 0:P]), (b2[:, P:256], p[:, P:256]),
                                        (b2[:, 256:384], p[:, 256:384])))

            def pv_fa(h):
                s = soft["fa"]
                pe.wait_ge(s["pt_v"], h + 1)
                if h % 2 == 0 and h >= 4:
                    pe.wait_ge(s["y"], h // 2 - 1)
                t = pt2[:, h % 2, :]
                pv(h, w2v, s["pv"], ((0, P, t[:, 0:256], 0), (1, P, t[:, 256:384], P)))

            pe.wait_ge(evac["f"], 1)
            scores_fa(0)
            for h in range(HEADS):
                if h + 1 < HEADS:
                    scores_fa(h + 1)
                gate_tile(2 * h, "gates2")
                gate_tile(2 * h + 1, "gates2")
                pt_fa(h)
                if h:
                    pv_fa(h - 1)
            pv_fa(HEADS - 1)
            pe.wait_ge(soft["fa"]["y"], 3)
            for m in range(CT):
                pe.wait_ge(conv_done, m + 1)
                last = mm(bank[4][:, 0:SEQ], const("ones"), cv[:, m, :], start=(m == 0), stop=(m == CT - 1))
            last.then_inc(n_sum, 1)
            pe.wait_ge(evac["gates2"], 16)
            norm_sum("ln_var", CT, SEQ)
            out_proj("o2", cv, y2, lambda: pe.wait_ge(conv_silu, CT), lambda: pe.wait_ge(soft["fa"]["y"], 4))
            pe.wait_ge(evac["o2"], KD)
            for m in range(KD):
                if m >= 2:
                    pe.wait_ge(evac["w2"], m - 1)
                tile(cur, bank[4 + m % 2][:, 0:SEQ], x2, KD, proj)
            norm_sum("n2", KD, SEQ)

            pe.wait_ge(n_out, AT[n_out]["n2"] + KD)
            for t in range(2):
                for k in range(KD):
                    last = mm(bank[t][:, 0:E], nrm[:, k, t * P:t * P + P], vec("w_router", k * E, E),
                              start=(k == 0), stop=(k == KD - 1))
            last.then_inc(logits, 1)
            for t in range(2):
                for k in range(KD):
                    b = bank[2 + 2 * t + k // 4]
                    last = nc.tensor.transpose(b[:, (k % 4) * P:(k % 4 + 1) * P], nrm[:, k, t * P:t * P + P],
                                               const("ident"))
            last.then_inc(nat, 1)
            pe.wait_ge(masked, 1)
            mm(bank[6][:, 0:E], const("strict"), msk[:, 0, :], start=True, stop=False, **kw)
            mm(bank[6][:, E:2 * E], const("ones"), msk[:, 0, :], start=False, stop=False, **kw)
            mm(bank[6][:, E:2 * E], const("strict"), msk[:, 1, :], start=False, stop=False, **kw)
            mm(bank[6][:, 2 * E:3 * E], const("ones"), msk[:, 0, :], start=False, stop=False, **kw)
            mm(bank[6][:, 2 * E:3 * E], const("ones"), msk[:, 1, :], start=False, stop=True,
               **kw).then_inc(counted, 1)

            for t in range(2):
                last = mm(bank[0][0:E, 0:1], msk[:, t, :], const("ones", 0, 1), start=(t == 0), stop=(t == 1))
            last.then_inc(nb_ready, 1)
            pe.wait_ge(nb_ready, 2)
            mm(bank[1][0:E, 0:1], const("tri_le", 0, E, E), nb_col[0:E, :], start=True, stop=True)\
                .then_inc(cum_ready, 1)
            pe.wait_ge(past_ready, 1)
            width = MAX_BLOCKS + 1
            mm(bank[0][0:1, 0:width], const("ones", 0, 1, E), past[0:E, :], start=True, stop=False, **kw)
            mm(bank[0][0:1, width:2 * width], nb_col[0:E, :], past[0:E, :], start=False, stop=False, **kw)
            mm(bank[0][0:1, 2 * width:2 * width + 1], nb_col[0:E, :], const("ones", 0, 1, E),
               start=False, stop=True, **kw).then_inc(table_sums, 1)

            pe.wait_ge(nat_out, 4)
            pe.wait_ge(bias_in, 16)
            pe.wait_ge(counts_ready, 1)
            halves = [(j, (0, 64 * j), slice(64 * j, 64 * j + 64)) for j in range(2)]
            loaded = [16 * ROUNDS if s < RING else 0 for s in range(SLOTS)]

            def gather(n):
                pe.wait_ge(m_S, n)
                for t in range(2):
                    for j, pos, pr in halves:
                        last = mm(bank[0][pr, :], S[:, t, :], h2n[:, t, 512 * j:512 * j + 512],
                                  start=(t == 0), stop=(t == 1), tile_position=pos)
                last.then_inc(m_gath, 1)

            def turn_rows():
                for c in range(4):
                    last = nc.tensor.transpose(bank[1][:, c * P:c * P + P], xg[:, c * P:c * P + P], const("ident"))
                return last

            def first(e, ks):
                for k in ks:
                    pe.wait_ge(slot_in[k], e * 16 + (loaded[k] + 16))
                    for gu in range(2):
                        for j, pos, pr in halves:
                            c0 = gu * D + j * 512
                            last = mm(bank[2 + gu][pr, :], xT[:, k % 4, k // 4, :], ring[:, k, c0:c0 + 512],
                                      start=(k == 0), stop=False, tile_position=pos)
                            if gu == 0 and j == 0:
                                last.then_inc(freed, 1)

            def back_to_tokens(r):
                for mp in range(2):
                    for j, _, pr in halves:
                        mt = 2 * r + mp
                        last = mm(bank[6 + j][:, mp * 256:mp * 256 + 256], ye[pr, mt * P:mt * P + P],
                                  ST[pr, :, :].rearrange("p a b -> p (a b)"),
                                  start=True, stop=True, tile_position=(64 * j, 0))
                last.then_inc(m_comb, 1)

            n_blocks = pe.value_load(count_i[0:1, E:E + 1], min_val=E, max_val=MAX_BLOCKS)
            gather(1)
            pe.wait_ge(m_xg, 1)
            turn_rows().then_inc(m_xt, 1)
            with pe.Fori(0, n_blocks) as g:
                e = pe.value_load(block_i[0:1, bass.ds(g, 1)], min_val=0, max_val=E - 1)
                pe.wait_ge(m_xts, g + 1)
                first(e, range(0, 4))
                pe.wait_ge(m_ys, g + 1)
                pe.wait_ge(m_sts, g + 1)
                pe.wait_ge(m_acc, g * 2 + 1)
                back_to_tokens(0)
                first(e, range(4, KD))
                pe.wait_ge(m_oh1, g + 1)
                for gu in range(2):
                    for j, pos, pr in halves:
                        c0 = gu * D + j * 512
                        last = mm(bank[2 + gu][pr, :], onehot1[0:E, :], b_all[0:E, c0:c0 + 512],
                                  start=False, stop=True, tile_position=pos)
                last.then_inc(m_hc, 1)
                pe.wait_ge(m_acc, g * 2 + 2)
                back_to_tokens(1)
                gather(g + 2)
                pe.wait_ge(m_hm, g + 1)
                for c in range(4):
                    last = nc.tensor.transpose(bank[4][:, c * P:c * P + P], gl[:, c * P:c * P + P],
                                               const("ident"))
                last.then_inc(m_hmt, 1)
                pe.wait_ge(m_xg, g + 2)
                turn_rows()
                pe.wait_ge(m_SG, g + 1)
                for t in range(2):
                    last = nc.tensor.transpose(bank[0][:, t * P:t * P + P],
                                               SG[:, t, :, :].rearrange("p a b -> p (a b)"), const("ident"))
                last.then_inc(m_xt, 1)
                pe.wait_ge(m_hms, g + 1)
                for k in range(KD):
                    s = 8 + k // 2
                    if k % 2 == 0:
                        pe.wait_ge(slot_in[s], e * 16 + (loaded[s] + 16))
                    for j, pos, pr in halves:
                        c0 = (k % 2) * D + j * 512
                        last = mm(bank[5][pr, :], hmT[:, k % 4, k // 4, :], ring[:, s, c0:c0 + 512],
                                  start=(k == 0), stop=False, tile_position=pos)
                        if k % 2 == 0 and j == 0:
                            last.then_inc(freed, 1)
                for j, pos, pr in halves:
                    last = mm(bank[5][pr, :], onehot2[0:E, :], b_all[0:E, 2 * D + 512 * j:2 * D + 512 * j + 512],
                              start=False, stop=True, tile_position=pos)
                last.then_inc(m_y, 1)
            pe.wait_ge(m_ys, n_blocks + 1)
            pe.wait_ge(m_sts, n_blocks + 1)
            for r in range(2):
                pe.wait_ge(m_acc, n_blocks * 2 + (r + 1))
                back_to_tokens(r)
            norm_sum("final", KD, SEQ)

        @block.scalar
        def _(act):
            A = nc.scalar.activation
            act.dma_start(c_all, c_in.partition_broadcast(P)).then_inc(inputs_in, 16)
            for i in range(2):
                act.dma_start(ada_w[:, i, :], ada[i, :, :]).then_inc(ada_in[i], 16)
            act.wait_ge(inputs_in, 64)
            seen = [0]

            def link(ins):
                seen[0] += 1
                ins.then_inc(act_chain, 1)
                act.wait_ge(act_chain, seen[0])

            tables = [None]

            def use(which):
                if tables[0] != which:
                    tables[0] = which
                    if isinstance(which, str):
                        act.preload_act_table_set(which)
                    else:
                        act.preload_act_table(which)

            def squares(n, tiles, src, after=None, first=0):
                for m in range(tiles):
                    if after is not None:
                        act.wait_ge(after, m + 1)
                    s = src(m)
                    A(sq[:, first + m, 0:s.shape[1]], s, ACT.Square).then_inc(n_sq, 1)

            def root(n, width, mean, eps, ps=None):
                use("natural_log_exp_and_others")
                act.wait_ge(n_sum, AT[n_sum][n] + 1)
                ps = bank[7] if ps is None else ps
                link(A(rtmp[:, 0:width], ps[:, 0:width], ACT.Ln, scale=1.0 / mean, bias=const(eps)))
                A(rstd[:, 0:width], rtmp[:, 0:width], ACT.Exp, scale=-0.5).then_inc(n_rs, 1)

            def split_piece(at, f, i, it=None):
                slot, n = (at + i) % RING, 0 if it is None else it
                base = f * FFN_PIECES
                act.wait_ge(slot_in[slot], 16 * n + 16 * loads_of(at + i))
                if it is not None or i >= SPLIT_BUFS:
                    act.wait_ge(freed, n * RING + (RING - 1 + at + i - SPLIT_BUFS + 2))
                A(w_hi[:, i % SPLIT_BUFS, :], ring[:, slot, :], ACT.Copy).then_inc(w_high, 1)

            def split_input(f, w, lo):
                for m in range(KD):
                    act.wait_ge(n_out, AT[n_out]["f1_pre" if f == 0 else "f2_pre"] + m + 1)
                    A(x_hi[:, m, lo:TOK], x_all[:, m, 0:w], ACT.Copy).then_inc(x_high, 1)

            def ffn(f, at, w):
                base = f * NF

                def step(j, ready, it=None):
                    split_piece(at, f, j + 2, it)
                    act.wait_ge(up_ready, ready)
                    A(sig[:, j % 2, 0:w], bank[(j % 2) * 2][:, 0:w], ACT.Silu).then_inc(exp_ready, 1)

                def ada_load(i, used, n):
                    act.wait_ge(ada_used, used)
                    src = ada[n, :, :] if isinstance(n, int) else ada[bass.ds(n, 1), :, :].rearrange("o p n -> p (o n)")
                    act.dma_start(ada_w[:, i, :], src).then_inc(ada_in[i], 16)

                with act.Fori(0, NF // RING) as it:
                    for j in range(RING):
                        step(j, it * RING + (base + j + 1), it)
                        for i in range(2 if f == 0 else 0):
                            ada_load(i, it * (2 * RING) + (2 * j + i + 2), it * (2 * RING) + (2 * j + i + 2))
                for j in range(NF // RING * RING, NF):
                    step(j, base + j + 1)
                    for i in range(2 if f == 0 else 0):
                        ada_load(i, 2 * j + i + 2, 2 * j + i + 2)
                if f == 0:
                    for i in range(2):
                        ada_load(i, 2 * NF + i + 2, 2 * NF + i + 2)
                m = 0
                for i in range(NF, FFN_PIECES):
                    if i + 2 < FFN_PIECES:
                        split_piece(at, f, i + 2)
                    while m < KD and (m + 1) * NF <= (i - NF + 1) * BLK:
                        act.wait_ge(down_ready, f * KD + m + 1)
                        b = bank[4 + m % 2][:, 0:w]
                        A(sq[:, m, 0:w], b, ACT.Square).then_inc(n_sq, 1)
                        A(nrm[:, m, 0:w], b, ACT.Copy).then_inc(down_out, 1)
                        m += 1

            squares("f1_pre", KD, lambda m: res[:, m, :])
            split_piece(FFN1_AT, 0, 0)
            root("f1_pre", TOK, D, "eps1")
            use(ACT.Silu)
            split_input(0, TOK, 0)
            split_piece(FFN1_AT, 0, 1)
            A(c_all, c_all, ACT.Silu).then_inc(c_silu, 1)
            ffn(0, FFN1_AT, TOK)
            root("f1_post", TOK, D, "eps1")
            squares("mix_pre", KD, lambda m: res[:, m, :], updated["f1"])
            root("mix_pre", TOK, D, "eps1")
            for i in range(7):
                act.wait_ge(proj, AT[proj]["lat"] + i + 1)
                A(lat[:, i, :], bank[i % 2][:, 0:TOK], ACT.Copy).then_inc(evac["lat"], 1)
            act.wait_ge(evac["lat"], 5)
            for i in range(8):
                act.wait_ge(proj, AT[proj]["qk"] + i + 1)
                if i < 4:
                    A(sb_q[:, i, :], bank[2 + i % 2][:, 0:SEQ], ACT.Copy, scale=0.125).then_inc(evac["qk"], 1)
                else:
                    A(sb_k[:, i - 4, :], bank[2 + i % 2][:, 0:TOK], ACT.Copy).then_inc(evac["qk"], 1)
                if i == 2:
                    squares("cq", 3, lambda m: lat[:, m, META:TOK])
                    squares("ckv", 2, lambda m: lat[:, 3 + m, :], first=4)
            root("cq", SEQ, 384, "eps1")
            act.wait_ge(n_out, AT[n_out]["cq"] + 3)
            root("ckv", TOK, 256, "eps1", bank[0])
            act.wait_ge(proj, AT[proj]["v"] + 1)
            for t, n in enumerate((P, P, META)):
                A(sb_v[0:n, t, :], bank[4 + t][0:n, :], ACT.Copy).then_inc(evac["v"], 1)
            for i in range(8):
                act.wait_ge(proj, AT[proj]["uq"] + i + 1)
                A(uq[:, i, :], bank[2 + i % 2][:, 0:SEQ], ACT.Copy).then_inc(evac["uq"], 1)
            for i in range(4):
                act.wait_ge(proj, AT[proj]["ukv"] + i + 1)
                A(kn[:, i, :], bank[i % 2][:, 0:TOK], ACT.Copy).then_inc(evac["ukv"], 1)
            act.wait_ge(proj, AT[proj]["ukv"] + 5)
            for t, n in enumerate((P, P, META)):
                A(v2[0:n, t, :], bank[4 + t][0:n, :], ACT.Copy).then_inc(evac["ukv"], 1)

            def gate_evac(i, which):
                act.wait_ge(proj, AT[proj][which] + i + 1)
                if which == "gates":
                    A(graw[:, i, :], bank[6 + i % 2][:, 0:SEQ], ACT.Identity,
                      bias=vec("b_gate", i)).then_inc(evac[which], 1)
                else:
                    A(graw2[:, i, :], bank[6 + i % 2][:, 0:SEQ], ACT.Copy).then_inc(evac[which], 1)

            def open_gates(which, gr):
                use(ACT.Sigmoid)
                act.wait_ge(evac[which], 16)
                for m in range(KD):
                    A(gr[:, m, :], gr[:, m, :], ACT.Sigmoid)
                    A(gr[:, 8 + m, :], gr[:, 8 + m, :], ACT.Sigmoid).then_inc(gates_ready, 1)

            def softplus_part(h):
                act.wait_ge(z_ready, h + 1)
                X, Y, e_ = bank[h % 2], bank[2 + h % 2], t_e[:, h % 2, :]
                A(e_[:, 0:384], X[:, 0:384], ACT.Abs)
                link(A(e_[0:META, 384:640], Y[0:META, 0:256], ACT.Abs))
                for func, kw in ((ACT.Exp, dict(scale=-1.0)), (ACT.Ln, dict(bias=const("one")))):
                    A(e_[:, 0:384], e_[:, 0:384], func, **kw)
                    kw = dict(kw, bias=const("one", rows=META)) if "bias" in kw else kw
                    last = A(e_[0:META, 384:640], e_[0:META, 384:640], func, **kw)
                    if func == ACT.Exp:
                        link(last)
                last.then_inc(e_done, 1)

            def attend_exp(h):
                act.wait_ge(la_ready, h + 1)
                act.wait_ge(cap_done, h + 1)
                if h >= 2:
                    act.wait_ge(av_done, h - 1)
                X, Y, e_, t = bank[h % 2], bank[2 + h % 2], t_e[:, h % 2, :], t_a[:, h % 2, :]
                A(t[:, 128:256], X[:, 128:256], ACT.Exp)
                A(t[0:META, 384:640], Y[0:META, 0:256], ACT.Exp)
                A(t[:, 0:128], e_[:, 0:128], ACT.Exp)
                A(t[:, 256:384], e_[:, 256:384], ACT.Exp).then_inc(at_done, 1)

            def y_evac(h, dst, ready, done):
                if h >= 0 and h % 2:
                    act.wait_ge(ready, h + 1)
                    m = h // 2
                    A(dst[:, m, :], bank[4 + m % 2][:, 0:SEQ], ACT.Copy).then_inc(done, 1)

            softplus_part(0)
            for h in range(HEADS):
                if h + 1 < HEADS:
                    softplus_part(h + 1)
                gate_evac(h, "gates")
                attend_exp(h)
                y_evac(h - 1, y_sb, av_done, y_out)
            y_evac(HEADS - 1, y_sb, av_done, y_out)

            def soft_exp(kind, h, p, split):
                s = soft[kind]
                act.wait_ge(s["maxed"], h + 1)
                pp, i = p[:, h % 2, :], h % 2
                A(pp[:, 0:split], pp[:, 0:split], ACT.Exp, bias=smx[:, i, 0:1], accum_out=ssum[:, i, 0:1])
                A(pp[:, split:], pp[:, split:], ACT.Exp, bias=smx[:, i, 1:2],
                  accum_out=ssum[:, i, 1:2]).then_inc(s["exped"], 1)

            soft_exp("mla", 0, p_sb, 144)
            for h in range(HEADS):
                if h + 1 < HEADS:
                    soft_exp("mla", h + 1, p_sb, 144)
                gate_evac(8 + h, "gates")
                act.wait_ge(soft["mla"]["pt"], h + 1)
                if h >= 2:
                    act.wait_ge(soft["mla"]["pv"], h - 1)
                A(pt_sb[0:META, h % 2, 384:640], bank[3][0:META, 0:256], ACT.Copy)\
                    .then_inc(soft["mla"]["pt_a"], 1)
                y_evac(h - 1, y_mla, soft["mla"]["pv"], soft["mla"]["y"])
            y_evac(HEADS - 1, y_mla, soft["mla"]["pv"], soft["mla"]["y"])
            open_gates("gates", graw)
            for m in range(KD):
                act.wait_ge(proj, AT[proj]["w1"] + m + 1)
                b = bank[4 + m % 2][:, 0:SEQ]
                A(sq[:, m, 0:SEQ], b, ACT.Square).then_inc(n_sq, 1)
                A(mix_o[:, m, :], b, ACT.Copy).then_inc(evac["w1"], 1)
            root("mix_post", SEQ, D, "eps1")
            split_piece(FFN2_AT, 1, 0)
            squares("f2_pre", KD, lambda m: real(res[:, m, :]), updated["m1"])
            root("f2_pre", SEQ, D, "eps1")
            use(ACT.Silu)
            split_input(1, SEQ, META)
            split_piece(FFN2_AT, 1, 1)
            ffn(1, FFN2_AT, SEQ)
            root("f2_post", SEQ, D, "eps1")

            squares("n1", KD, lambda m: real(res[:, m, :]), updated["f2"])
            root("n1", SEQ, D, "eps2")
            use(ACT.Sigmoid)
            for m in range(CT):
                act.wait_ge(proj, AT[proj]["conv"] + m + 1)
                if m >= 2:
                    act.wait_ge(evac["conv"], m - 1)
                A(csg[:, m % 2, :], bank[2 * (m % 2) + 1][:, 0:SEQ], ACT.Sigmoid).then_inc(conv_sig, 1)
            use("natural_log_exp_and_others")
            act.wait_ge(proj, AT[proj]["f"] + 1)
            link(A(lf[0:8, :], bank[6][0:8, 0:SEQ], ACT.Identity, bias=vec("b_forget", rows=8)))
            link(A(lft[0:8, :], lf[0:8, :], ACT.Abs))
            link(A(lft[0:8, :], lft[0:8, :], ACT.Exp, scale=-1.0))
            A(lft[0:8, :], lft[0:8, :], ACT.Ln, bias=const("one", rows=8)).then_inc(evac["f"], 1)
            for i in range(8):
                act.wait_ge(proj, AT[proj]["qk2"] + i + 1)
                b = bank[4 + i % 2][:, 0:SEQ]
                if i < 4:
                    A(q2[:, i, :], b, ACT.Copy, scale=0.125).then_inc(evac["qk2"], 1)
                else:
                    A(k2[:, i - 4, :], b, ACT.Copy).then_inc(evac["qk2"], 1)
            act.wait_ge(proj, AT[proj]["v2"] + 1)
            for t in range(2):
                A(w2v[:, t, :], bank[t][:, :], ACT.Copy).then_inc(evac["v2"], 1)
            act.wait_ge(logf_t, 1)
            A(lfn[:, :, :].rearrange("p a b -> p (a b)"), bank[2][:, 0:16], ACT.Copy).then_inc(logf_n, 1)
            act.wait_ge(f_sums, 1)
            A(fcum[:, :, :].rearrange("p a b -> p (a b)"), bank[3][:, 0:16], ACT.Copy).then_inc(f_out, 1)
            A(neg_f[0:8, :], bank[2][0:8, 256:512], ACT.Copy, scale=-1.0).then_inc(f_out, 1)
            soft_exp("fa", 0, p2, P)
            for h in range(HEADS):
                if h + 1 < HEADS:
                    soft_exp("fa", h + 1, p2, P)
                gate_evac(2 * h, "gates2")
                gate_evac(2 * h + 1, "gates2")
                act.wait_ge(soft["fa"]["pt"], h + 1)
                if h >= 2:
                    act.wait_ge(soft["fa"]["pv"], h - 1)
                A(pt2[:, h % 2, :], bank[2][:, 0:384], ACT.Copy).then_inc(soft["fa"]["pt_v"], 1)
                y_evac(h - 1, y2, soft["fa"]["pv"], soft["fa"]["y"])
            y_evac(HEADS - 1, y2, soft["fa"]["pv"], soft["fa"]["y"])
            act.wait_ge(n_sum, AT[n_sum]["ln_mean"] + 1)
            A(lnm, bank[4][:, 0:SEQ], ACT.Copy, scale=1.0 / 512).then_inc(n_rs, 1)
            squares("ln_var", CT, lambda m: cv[:, m, :], ln_in)
            root("ln_var", SEQ, 512, "eps2")
            use(ACT.Silu)
            for m in range(CT):
                act.wait_ge(n_out, AT[n_out]["ln_var"] + m + 1)
                A(cv[:, m, :], cv[:, m, :], ACT.Silu).then_inc(conv_silu, 1)
            open_gates("gates2", graw2)
            use("natural_log_exp_and_others")
            squares("n2", KD, lambda m: real(res[:, m, :]), evac["w2"])
            root("n2", SEQ, D, "eps2")
            act.dma_start(b_all[0:E, :], b_exp).then_inc(bias_in, 16)
            act.wait_ge(top_max, 1)
            for t in range(2):
                A(tope[:, t, 0:TOPK], top[:, t, 0:TOPK], ACT.Exp, bias=tops[:, t, 0:1],
                  accum_out=tops[:, t, 1:2]).then_inc(top_exp, 1)
            act.wait_ge(nat, 1)
            for t in range(2):
                for c in range(2):
                    A(h2n[:, t, c * 512:c * 512 + 512], bank[2 + 2 * t + c][:, :], ACT.Copy)\
                        .then_inc(nat_out, 1)

            act.wait_ge(counts_ready, 1)
            use(ACT.Sigmoid)
            n_blocks = act.value_load(count_i[0:1, E:E + 1], min_val=E, max_val=MAX_BLOCKS)
            act.wait_ge(m_gath, 1)
            A(xg, bank[0][:, :], ACT.Copy).then_inc(m_xg, 1)
            with act.Fori(0, n_blocks) as g:
                act.wait_ge(m_gl, g + 1)
                A(eg, gl, ACT.Sigmoid, scale=1.702).then_inc(m_eg, 1)
                act.wait_ge(m_gath, g + 2)
                act.wait_ge(m_xt, g + 1)
                A(xg, bank[0][:, :], ACT.Copy).then_inc(m_xg, 1)
                act.wait_ge(m_hmt, g + 1)
                A(hmT[:, :, :, :].rearrange("p a b c -> p (a b c)"), bank[4][:, :], ACT.Copy).then_inc(m_hms, 1)
                act.wait_ge(m_xt, g + 2)
                act.wait_ge(m_comb, g * 2 + 2)
                A(ST[:, :, :].rearrange("p a b -> p (a b)"), bank[0][:, 0:256], ACT.Copy).then_inc(m_sts, 1)
                act.wait_ge(m_y, g + 1)
                A(ye, bank[5][:, :], ACT.Copy).then_inc(m_ys, 1)
            for m in range(KD):
                act.wait_ge(fin_x, m + 1)
                A(sq[:, m, 0:SEQ], fin[:, m, :], ACT.Square).then_inc(n_sq, 1)
            root("final", SEQ, D, "eps2")

        @block.gpsimd
        def _(pool):
            def rest(at, i, n):
                pool.wait_ge(w_high, n)
                b, slot = i % SPLIT_BUFS, (at + i) % RING
                nc.gpsimd.tensor_tensor(w_lo[:, b, :], ring[:, slot, :], w_hi[:, b, :].bitcast(f32),
                                        ALU.subtract).then_inc(w_split, 1)

            for f, at in enumerate((FFN1_AT, FFN2_AT)):
                base = f * FFN_PIECES
                with pool.Fori(0, FFN_PIECES // RING) as it:
                    for i in range(RING):
                        rest(at, i, it * RING + (base + i + 1))
                for i in range(FFN_PIECES // RING * RING, FFN_PIECES):
                    rest(at, i, base + i + 1)

        @block.vector
        def _(dve):
            V = nc.vector
            seen = [0]

            def link(ins, *waits):
                seen[0] += 1
                ins.then_inc(dve_chain, 1)
                dve.wait_ge(dve_chain, seen[0])

            def mark(ins):
                seen[0] += 1
                ins.then_inc(dve_chain, 1)

            def settle():
                dve.wait_ge(dve_chain, seen[0])

            def stt(out_, in0, scalar, in1, op0, op1):
                return V.scalar_tensor_tensor(out=out_, in0=in0, scalar=scalar, in1=in1, op0=op0, op1=op1)

            def ts(out_, in0, s1, s2, op0, op1=None):
                if op1 is None:
                    return V.tensor_scalar(out_, in0, s1, None, op0)
                return V.tensor_scalar(out_, in0, s1, s2, op0, op1)

            tt = V.tensor_tensor

            dve.sem_inc(freed, RING - 1)
            dve.sem_inc(hid_ready, 2)
            dve.sem_inc(down_out, 2)
            for s in (ada_used, ada_copied, hid_split, m_acc):
                dve.sem_inc(s, 1)
            dve.wait_ge(inputs_in, 64)
            mark(ts(half_f1, vec("f1_post", 0, 8), 0.5, None, ALU.mult))
            mark(ts(half_f2, vec("f2_post", 0, 8), 0.5, None, ALU.mult))

            def normed(n, tiles, src, gain, dst):
                dve.wait_ge(n_rs, AT[n_rs][n] + 1)
                for m in range(tiles):
                    s = src(m)
                    stt(dst(m), s, gain(m), rstd[:, 0:s.shape[1]], ALU.mult, ALU.mult).then_inc(n_out, 1)

            def residual(n, src, gain, into, upd):
                dve.wait_ge(n_rs, AT[n_rs][n] + 1)
                at = seen[0]
                for m in range(KD):
                    s = src(m)
                    mark(stt(s, s, gain(m), rstd[:, 0:s.shape[1]], ALU.mult, ALU.mult))
                for m in range(KD):
                    dve.wait_ge(dve_chain, at + m + 1)
                    tt(into(m), into(m), src(m), ALU.add).then_inc(upd, 1)

            def split_input(f, w, lo):
                for m in range(KD):
                    dve.wait_ge(x_high, f * KD + m + 1)
                    tt(x_lo[:, m, lo:TOK], x_all[:, m, 0:w], x_hi[:, m, lo:TOK].bitcast(f32), ALU.subtract)\
                        .then_inc(x_split, 1)

            normed("f1_pre", KD, lambda m: res[:, m, :], lambda m: vec("f1_pre", m), lambda m: x_all[:, m, :])
            split_input(0, TOK, 0)
            dve.wait_ge(c_silu, 1)

            def ada_tile(i, n, w, to):
                dve.wait_ge(ada_in[i], w)
                dve.wait_ge(ada_used, n + 1)
                V.tensor_tensor_reduce(out=ada_t, in0=ada_w[:, i, :], in1=c_all, scale=1.0, scalar=0.0,
                                       op0=ALU.mult, op1=ALU.add,
                                       accum_out=to).then_inc(ada_used, 1)

            def ffn(f, w):
                base = f * NF

                def hidden(j, n, at):
                    i = j % 2
                    dve.wait_ge(exp_ready, n)
                    dve.wait_ge(hid_split, n)
                    tt(hid[:, 0:w], sig[:, i, 0:w], bank[2 * i + 1][:, 0:w], ALU.mult).then_inc(hid_ready, 1)
                    dve.wait_ge(hid_ready, n + 2)
                    hi, lo = hid_hi[:, at, 0:w], hid_lo[:, at, 0:w]
                    if not isinstance(at, int):
                        hi, lo = (v.rearrange("p o t -> p (o t)") for v in (hi, lo))
                    V.tensor_copy(hi, hid[:, 0:w]).then_inc(hid_high, 1)
                    dve.wait_ge(hid_high, n)
                    tt(lo, hid[:, 0:w], hi.bitcast(f32), ALU.subtract).then_inc(hid_split, 1)

                with dve.Fori(0, NF // 2) as it:
                    if f == 0:
                        dve.wait_ge(ada_copied, it + 1)
                    for j in range(2):
                        hidden(j, it * 2 + (base + j + 1), bass.ds(it * 2 + j, 1))
                        if f == 0:
                            for i in range(2):
                                ada_tile(i, it * 4 + (2 * j + i), it * 32 + 16 * (j + 1),
                                         ada_acc[:, 2 * j + i:2 * j + i + 1])
                    if f == 0:
                        dve.wait_ge(ada_used, it * 4 + 5)
                        V.tensor_copy(mod[:, bass.ds(it * 4, 4)], ada_acc).then_inc(ada_copied, 1)

            ffn(0, TOK)
            for n in range(2 * NF, 48):
                ada_tile(n % 2, n, 16 * (n // 2 + 1), mod[:, n:n + 1])
            dve.wait_ge(ada_copied, NF // 2 + 1)
            dve.wait_ge(ada_used, 49)
            link(tt(mod, mod, vec("b_ada", 0, 48), ALU.add))
            link(ts(g1s, mod[:, 8:16], 1.0, None, ALU.add))
            link(ts(g2s, mod[:, 32:40], 1.0, None, ALU.add))
            mark(tt(g1s, g1s, vec("n1_g", 0, 8), ALU.mult))
            mark(tt(g2s, g2s, vec("n2_g", 0, 8), ALU.mult))
            residual("f1_post", lambda m: nrm[:, m, :], lambda m: half_f1[:, m:m + 1], lambda m: res[:, m, :],
                     updated["f1"])
            dve.wait_ge(updated["f1"], KD)
            normed("mix_pre", KD, lambda m: res[:, m, :], lambda m: vec("mix_pre", m), lambda m: nrm[:, m, :])
            normed("cq", 3, lambda m: lat[:, m, META:TOK], lambda m: vec("q_g", m), lambda m: lat[:, m, META:TOK])
            normed("ckv", 2, lambda m: lat[:, 3 + m, :], lambda m: vec("kv_g", m), lambda m: lat[:, 3 + m, :])
            mark(tt(lat[:, 5, :], lat[:, 5, :], const("cos"), ALU.mult))
            mark(tt(lat[:, 6, :], lat[:, 6, :], const("sin"), ALU.mult))
            settle()
            tt(lat[:, 5, :], lat[:, 5, :], lat[:, 6, :], ALU.add).then_inc(roped, 1)
            dve.wait_ge(evac["uq"], 8)
            for m in range(2):
                mark(tt(uq[:, 4 + m, :], uq[:, 4 + m, :], const("cos", META), ALU.mult))
                mark(tt(uq[:, 6 + m, :], uq[:, 6 + m, :], const("sin", META), ALU.mult))
            settle()
            tt(uq[:, 4:6, :], uq[:, 4:6, :], uq[:, 6:8, :], ALU.add).then_inc(roped, 1)

            def softplus(h):
                dve.wait_ge(e_done, h + 1)
                X, Y = bank[h % 2], bank[2 + h % 2]
                e_, s = t_e[:, h % 2, :], t_sp[:, h % 2, :]
                mark(stt(s[:, 0:384], X[:, 0:384], 0.0, e_[:, 0:384], ALU.max, ALU.add))
                mark(stt(s[0:META, 384:640], Y[0:META, 0:256], 0.0, e_[0:META, 384:640], ALU.max, ALU.add))
                settle()
                tt(s[:, 0:128], s[:, 0:128], const("strict"), ALU.mult)
                tt(s[:, 256:384], s[:, 256:384], const("strict"), ALU.mult).then_inc(sp_done, 1)

            def cap_diagonal(h):
                dve.wait_ge(la_ready, h + 1)
                X, e_ = bank[h % 2], t_e[:, h % 2, :]
                tt(e_[:, 0:128], X[:, 0:128], const("cap"), ALU.min)
                tt(e_[:, 256:384], X[:, 256:384], const("cap"), ALU.min).then_inc(cap_done, 1)

            softplus(0)
            for h in range(HEADS):
                if h + 1 < HEADS:
                    softplus(h + 1)
                cap_diagonal(h)

            def soft_norm(kind, h, p, split):
                s = soft[kind]
                dve.wait_ge(s["exped"], h + 1)
                pp, i = p[:, h % 2, :], h % 2
                link(V.reciprocal(srec[:, i, :], ssum[:, i, :]))
                ts(pp[:, 0:split], pp[:, 0:split], srec[:, i, 0:1], None, ALU.mult)
                ts(pp[:, split:], pp[:, split:], srec[:, i, 1:2], None, ALU.mult).then_inc(s["normed"], 1)

            def soft_max(kind, h, p, split):
                pp, i = p[:, h % 2, :], h % 2
                mark(V.reduce_max(smx[:, i, 0:1], pp[:, 0:split], AX.X))
                mark(V.reduce_max(smx[:, i, 1:2], pp[:, split:], AX.X))
                settle()
                ts(smx[:, i, :], smx[:, i, :], -1.0, None, ALU.mult).then_inc(soft[kind]["maxed"], 1)

            def mla_scores(h):
                dve.wait_ge(soft["mla"]["scores"], h + 1)
                if h >= 2:
                    dve.wait_ge(soft["mla"]["pt"], h - 1)
                link(stt(p_sb[:, h % 2, :], bank[h % 2][:, 0:416], MLA_SCALE, const("mla_mask"),
                         ALU.mult, ALU.add))
                soft_max("mla", h, p_sb, 144)

            dve.wait_ge(av_done, HEADS)
            mla_scores(0)
            for h in range(HEADS):
                soft_norm("mla", h, p_sb, 144)
                if h + 1 < HEADS:
                    mla_scores(h + 1)
                dve.wait_ge(soft["mla"]["pt"], h + 1)
                if h >= 2:
                    dve.wait_ge(soft["mla"]["pv"], h - 1)
                V.tensor_copy(pt_sb[:, h % 2, 0:384], bank[2][:, 0:384]).then_inc(soft["mla"]["pt_v"], 1)

            def gated(n, gr, tmp):
                for m in range(KD):
                    dve.wait_ge(proj, AT[proj][n] + m + 1)
                    dve.wait_ge(gates_ready, (KD if n == "o2" else 0) + m + 1)
                    if m:
                        dve.wait_ge(evac[n], m)
                    b0 = 2 * (m % 2)
                    mark(tt(tmp[:, 0, :], bank[b0][:, 0:SEQ], gr[:, m, :], ALU.mult))
                    mark(tt(tmp[:, 1, :], bank[b0 + 1][:, 0:SEQ], gr[:, 8 + m, :], ALU.mult))
                    settle()
                    tt(nrm[:, m, 0:SEQ], tmp[:, 0, :], tmp[:, 1, :], ALU.add).then_inc(evac[n], 1)

            gated("o1", graw, mtmp)
            residual("mix_post", lambda m: mix_o[:, m, :], lambda m: vec("mix_post", m),
                     lambda m: real(res[:, m, :]), updated["m1"])
            dve.wait_ge(updated["m1"], KD)
            normed("f2_pre", KD, lambda m: real(res[:, m, :]), lambda m: vec("f2_pre", m),
                   lambda m: x_all[:, m, 0:SEQ])
            split_input(1, SEQ, META)
            ffn(1, SEQ)
            residual("f2_post", lambda m: nrm[:, m, 0:SEQ], lambda m: half_f2[:, m:m + 1],
                     lambda m: real(res[:, m, :]), updated["f2"])
            dve.wait_ge(updated["f2"], KD)

            def modulated(n, gains, shift):
                dve.wait_ge(n_rs, AT[n_rs][n] + 1)
                at = seen[0]
                for m in range(KD):
                    mark(stt(nrm[:, m, 0:SEQ], real(res[:, m, :]), gains[:, m:m + 1], rstd[:, 0:SEQ],
                             ALU.mult, ALU.mult))
                for m in range(KD):
                    dve.wait_ge(dve_chain, at + m + 1)
                    ts(nrm[:, m, 0:SEQ], nrm[:, m, 0:SEQ], mod[:, shift + m:shift + m + 1], None, ALU.add)\
                        .then_inc(n_out, 1)

            mark(V.memset(ca[:, :, 0:CONV_K - 1], 0.0))
            modulated("n1", g1s, 0)
            for m in range(CT):
                dve.wait_ge(conv_sig, m + 1)
                tt(ca[:, m, CONV_K - 1:], bank[2 * (m % 2)][:, 0:SEQ], csg[:, m % 2, :], ALU.mult)\
                    .then_inc(evac["conv"], 1)
            dve.wait_ge(evac["f"], 1)
            stt(lf[0:8, :], lf[0:8, :], 0.0, lft[0:8, :], ALU.min, ALU.subtract).then_inc(logf_ready, 1)
            dve.wait_ge(evac["conv"], CT)

            taps = [(m, k) for m in range(CT) for k in range(CONV_K)]

            def conv_taps(n):
                for _ in range(n):
                    if not taps:
                        return
                    m, k = taps.pop(0)
                    w = vec("conv_w", m * CONV_K + k)
                    x = ca[:, m, k:k + SEQ]
                    if k == 0:
                        link(ts(cv[:, m, :], x, w, vec("conv_b", m), ALU.mult, ALU.add))
                    elif k < CONV_K - 1:
                        link(stt(cv[:, m, :], x, w, cv[:, m, :], ALU.mult, ALU.add))
                    else:
                        stt(cv[:, m, :], x, w, cv[:, m, :], ALU.mult, ALU.add).then_inc(conv_done, 1)

            conv_taps(40)

            def fa_scores(h):
                dve.wait_ge(soft["fa"]["scores"], h + 1)
                if h >= 2:
                    dve.wait_ge(soft["fa"]["pt"], h - 1)
                p, b_ = p2[:, h % 2, :], bank[h % 2]
                mark(stt(p[:, 0:P], b_[:, 0:P], fcum[:, 0, h:h + 1], const("causal"), ALU.add, ALU.add))
                mark(ts(p[:, P:256], b_[:, P:256], fcum[:, 1, h:h + 1], None, ALU.add))
                mark(stt(p[:, 256:384], b_[:, 256:384], fcum[:, 1, h:h + 1], const("causal"), ALU.add, ALU.add))
                settle()
                soft_max("fa", h, p2, P)

            fa_scores(0)
            for h in range(HEADS):
                soft_norm("fa", h, p2, P)
                if h + 1 < HEADS:
                    fa_scores(h + 1)
                conv_taps(11)
            conv_taps(len(taps))
            dve.wait_ge(conv_done, CT)
            dve.wait_ge(n_rs, AT[n_rs]["ln_mean"] + 1)
            for m in range(CT):
                tt(cv[:, m, :], cv[:, m, :], lnm, ALU.subtract).then_inc(ln_in, 1)
            dve.wait_ge(n_rs, AT[n_rs]["ln_var"] + 1)
            dve.wait_ge(ln_in, CT)
            at = seen[0]
            for m in range(CT):
                mark(tt(cv[:, m, :], cv[:, m, :], rstd[:, 0:SEQ], ALU.mult))
            for m in range(CT):
                dve.wait_ge(dve_chain, at + m + 1)
                ts(cv[:, m, :], cv[:, m, :], vec("ln_g", m), vec("ln_b", m), ALU.mult, ALU.add)\
                    .then_inc(n_out, 1)
            gated("o2", graw2, mt2)
            for m in range(KD):
                dve.wait_ge(proj, AT[proj]["w2"] + m + 1)
                r = real(res[:, m, :])
                stt(r, bank[4 + m % 2][:, 0:SEQ], mod[:, 16 + m:17 + m], r, ALU.mult, ALU.add)\
                    .then_inc(evac["w2"], 1)
            dve.wait_ge(evac["w2"], KD)
            modulated("n2", g2s, 24)

            mark(V.memset(acc, 0.0))
            dve.wait_ge(logits, 1)
            for t in range(2):
                mark(tt(lgt[:, t, :], bank[t][:, 0:E], vec("b_router", 0, E), ALU.add))
            settle()
            for t in range(2):
                mark(V.max(top[:, t, :], lgt[:, t, :]))
            settle()
            for t in range(2):
                mark(V.max_index(idx_u[:, t, :], top[:, t, :], lgt[:, t, :]))
            settle()
            mark(V.tensor_copy(topi[:, :, :], idx_u[:, :, :]))
            for t in range(2):
                last = ts(tops[:, t, 0:1], top[:, t, 0:1], -1.0, None, ALU.mult)
            last.then_inc(top_max, 1)
            settle()
            for t in range(2):
                mark(ts(msk[:, t, :], const("iota", 0, E), topi[:, t, 0:1], None, ALU.is_equal))
            for j in range(1, TOPK):
                settle()
                for t in range(2):
                    last = stt(msk[:, t, :], const("iota", 0, E), topi[:, t, j:j + 1], msk[:, t, :],
                               ALU.is_equal, ALU.add)
                    if j < TOPK - 1:
                        mark(last)
            last.then_inc(masked, 1)
            dve.wait_ge(top_exp, 2)
            mark(V.reciprocal(tops[:, :, 1:2], tops[:, :, 1:2]))
            settle()
            for t in range(2):
                mark(ts(tope[:, t, 0:TOPK], tope[:, t, 0:TOPK], tops[:, t, 1:2], None, ALU.mult))
            settle()
            for t in range(2):
                mark(ts(gate[:, t, :], const("iota", 0, E), topi[:, t, 0:1], tope[:, t, 0:1],
                        ALU.is_equal, ALU.mult))
            for j in range(1, TOPK):
                settle()
                dve.wait_ge(masked, 1)
                for t, tmp in enumerate((ctmp, csum)):
                    mark(ts(tmp, const("iota", 0, E), topi[:, t, j:j + 1], tope[:, t, j:j + 1],
                            ALU.is_equal, ALU.mult))
                settle()
                for t, tmp in enumerate((ctmp, csum)):
                    mark(tt(gate[:, t, :], gate[:, t, :], tmp, ALU.add))
            settle()
            dve.wait_ge(counted, 1)
            for t in range(2):
                mark(stt(slot[:, t, :], bank[6][:, t * E:t * E + E], 1.0, msk[:, t, :], ALU.add, ALU.mult))

            def blocks_of(to, counts):
                settle()
                mark(ts(to, counts, float(SLOT_TOK), 1.0, ALU.is_gt, ALU.add))
                for lim in (2, 3):
                    settle()
                    mark(stt(to, counts, float(lim * SLOT_TOK), to, ALU.is_gt, ALU.add))
                settle()

            blocks_of(ctmp[0:1, :], bank[6][0:1, 2 * E:3 * E])
            mark(V.tensor_copy(count_i[:, 0:E], ctmp[0:1, :]))
            for t in range(2):
                mark(ts(slot[:, t, :], slot[:, t, :], 1.0, None, ALU.subtract))
            dve.wait_ge(nb_ready, 1)
            blocks_of(nb_col[0:E, :], bank[0][0:E, 0:1])
            dve.sem_inc(nb_ready, 1)
            dve.wait_ge(cum_ready, 1)
            link(V.tensor_copy(cum_col[0:E, :], bank[1][0:E, 0:1]))
            ts(past[0:E, :], const("iota", 0, MAX_BLOCKS + 1, E), cum_col[0:E, :], None, ALU.is_ge)\
                .then_inc(past_ready, 1)
            dve.wait_ge(table_sums, 1)
            width = MAX_BLOCKS + 1
            link(tt(table[0:1, 1, :], const("iota", 0, width, 1), bank[0][0:1, width:2 * width], ALU.subtract))
            link(ts(table[0:1, 1, :], table[0:1, 1, :], 3.0, None, ALU.min))
            link(ts(table[0:1, 0, :], bank[0][0:1, 0:width], float(E - 1), None, ALU.min))
            link(V.tensor_copy(block_i[:, :], table[0:1, :, :].rearrange("p a b -> p (a b)")))
            link(V.tensor_copy(count_i[:, E:E + 1], bank[0][0:1, 2 * width:2 * width + 1]))
            mark(V.memset(ye, 0.0))
            mark(V.memset(ST, 0.0))
            settle()
            dve.sem_inc(m_ys, 1)
            dve.sem_inc(m_sts, 1)
            dve.sem_inc(counts_ready, 1)

            def where(g):
                e_ = dve.value_load(block_i[0:1, bass.ds(g, 1)], min_val=0, max_val=E - 1)
                b_ = dve.value_load(block_i[0:1, bass.ds(g + width, 1)], min_val=0, max_val=3)
                return e_, b_

            def slots(b_):
                return cst[:, bass.ds(b_ * SLOT_TOK + CONST["iota"][0], SLOT_TOK)]

            def select(e_, b_):
                for t in range(2):
                    last = V.tensor_scalar(S[:, t, :], slots(b_), slot[:, t, bass.ds(e_, 1)], None, ALU.is_equal)
                return last

            def one_hot(to, e_):
                return V.tensor_scalar(to[0:E, :], const("ones", 0, SLOT_TOK, E),
                                       cst[0:E, bass.ds(e_ + CONST["ident"][0], 1)], None, ALU.mult)

            def add_up(r):
                for j in range(2):
                    a_ = acc[:, 4 * j + 2 * r:4 * j + 2 * r + 2, :]
                    last = tt(a_, a_, bank[6 + j][:, :].rearrange("p (a b) -> p a b", a=2), ALU.add)
                last.then_inc(m_acc, 1)

            n_blocks = dve.value_load(count_i[0:1, E:E + 1], min_val=E, max_val=MAX_BLOCKS)
            e0, b0 = where(0)
            select(e0, b0).then_inc(m_S, 1)
            one_hot(onehot1, e0).then_inc(m_oh1, 1)
            dve.wait_ge(m_xt, 1)
            V.tensor_copy(xT[:, :, :, :].rearrange("p a b c -> p (a b c)"), bank[1][:, :]).then_inc(m_xts, 1)
            with dve.Fori(0, n_blocks) as g:
                e, b = where(g)
                e_next, b_next = where(g + 1)
                select(e_next, b_next).then_inc(m_S, 1)
                for t in range(2):
                    place, weight = slot[:, t, bass.ds(e, 1)], gate[:, t, bass.ds(e, 1)]
                    for i in range(2):
                        V.tensor_scalar(SG[:, t, i, :], slots(b), place, weight, ALU.is_equal, ALU.mult)
                dve.wait_ge(m_comb, g * 2 + 1)
                one_hot(onehot2, e).then_inc(m_SG, 1)
                dve.wait_ge(m_acc, g * 2 + 1)
                add_up(0)
                dve.wait_ge(m_hc, g + 1)
                ts(gl, bank[2][:, :], 7.0, None, ALU.min).then_inc(m_gl, 1)
                ts(ul, bank[3][:, :], 7.0, -7.0, ALU.min, ALU.max).then_inc(moe_dve, 1)
                dve.wait_ge(m_gl, g + 1)
                dve.wait_ge(moe_dve, g * 2 + 1)
                stt(ul, ul, 1.0, gl, ALU.add, ALU.mult).then_inc(moe_dve, 1)
                dve.wait_ge(m_eg, g + 1)
                dve.wait_ge(moe_dve, g * 2 + 2)
                tt(gl, ul, eg, ALU.mult).then_inc(m_hm, 1)
                one_hot(onehot1, e_next).then_inc(m_oh1, 1)
                dve.wait_ge(m_comb, g * 2 + 2)
                add_up(1)
                dve.wait_ge(m_xt, g + 2)
                V.tensor_copy(xT[:, :, :, :].rearrange("p a b c -> p (a b c)"), bank[1][:, :]).then_inc(m_xts, 1)
            for r in range(2):
                dve.wait_ge(m_comb, n_blocks * 2 + (r + 1))
                dve.wait_ge(m_acc, n_blocks * 2 + (r + 1))
                add_up(r)
            dve.wait_ge(m_acc, n_blocks * 2 + 3)
            for m in range(KD):
                stt(fin[:, m, :], acc[:, m, :], mod[:, 40 + m:41 + m], real(res[:, m, :]),
                    ALU.mult, ALU.add).then_inc(fin_x, 1)
            dve.wait_ge(n_rs, AT[n_rs]["final"] + 1)
            dve.wait_ge(fin_x, KD)
            for m in range(KD):
                stt(fin[:, m, :], fin[:, m, :], vec("final_g", m), rstd[:, 0:SEQ], ALU.mult, ALU.mult)\
                    .then_inc(fin_ready, 1)


def block_stream(mats):
    parts = []
    for w, kind in mats:
        k, n = w.shape
        if kind == "tiles":
            parts.append(w.reshape(k // P, P, n // P, P).transpose(1, 2, 0, 3).reshape(P, -1))
        else:
            parts.append(w.reshape(k // P, P, n).transpose(1, 0, 2).reshape(P, -1))
    s = np.concatenate(parts, axis=1)
    return s.reshape(P, -1, PIECE).transpose(1, 0, 2)


def interleave(a, b):
    k = a.shape[0]
    return np.stack([a.reshape(k, -1, P), b.reshape(k, -1, P)], axis=2).reshape(k, -1)


def column(v):
    return np.asarray(v).reshape(-1, P).T


def kernel(**inputs):
    from concourse import bacc
    from concourse.bass_utils import run_bass_kernel_spmd

    x = {k: np.asarray(v) for k, v in inputs.items()}
    w_in = x["w_in"][0]
    at = np.cumsum([0, 512, 512, 512, 384, 256, 32, 2048])
    sq_, sk_, sv_, cq_, ckv_, kr_, gt_ = [w_in[:, at[i]:at[i + 1]] for i in range(7)]

    def swap(w):
        return np.concatenate([w[..., 16:], w[..., :16]], axis=-1)

    uq = x["w_uq"][0]
    ukv = x["w_ukv"][0]
    krs = np.tile(kr_, (1, 4)), np.tile(swap(kr_), (1, 4))
    mix1 = block_stream([
        (np.concatenate([cq_, ckv_, krs[0], krs[1], sq_, sk_], axis=1), "tiles"), (sv_, "rows"),
        (np.concatenate([uq[..., :64].reshape(384, 512), uq[..., 64:].reshape(384, 256),
                         swap(uq[..., 64:]).reshape(384, 256)], axis=1), "tiles"),
        (ukv[..., :64].reshape(256, 512), "tiles"), (ukv[..., 64:].reshape(256, 512), "rows"),
        (gt_, "tiles"), (interleave(x["w_sb_o"][0], x["w_mla_o"][0]), "tiles"), (x["w_out"][0], "tiles")])
    w2 = x["w_in_2"][0]
    at = np.cumsum([0, 512, 512, 512, 512, 512, 8, 1024, 1024])
    val, gat, q2, k2, v2, wf, gc, ga = [w2[:, at[i]:at[i + 1]] for i in range(8)]
    mix2 = block_stream([
        (np.concatenate([interleave(val, gat), q2, k2], axis=1), "tiles"), (v2, "rows"),
        (np.concatenate([gc, ga], axis=1), "tiles"),
        (interleave(x["w_conv_out_2"][0], x["w_attn_out_2"][0]), "tiles"), (x["w_out_2"][0], "tiles")])

    def ffn(n):
        return block_stream([(interleave(x[f"{n}_w_gate"][0], x[f"{n}_w_up"][0]), "tiles"),
                             (x[f"{n}_w_down"][0], "tiles")])

    stream = np.ascontiguousarray(np.concatenate([ffn("ffn1"), mix1, ffn("ffn2"), mix2]))
    cols = {
        "f1_pre": column(x["ffn1_pre_g"]), "f1_post": column(x["ffn1_post_g"]), "mix_pre": column(x["mix_pre_g"]),
        "b_gate": column(x["b_gate"]), "q_g": column(x["q_norm_g"]), "kv_g": column(x["kv_norm_g"]),
        "mix_post": column(x["mix_post_g"]), "f2_pre": column(x["ffn2_pre_g"]),
        "f2_post": column(x["ffn2_post_g"]), "b_ada": column(x["b_ada_2"]), "n1_g": column(x["norm1_g_2"]),
        "conv_b": column(x["conv_b_2"]), "ln_g": column(x["conv_ln_g_2"]), "ln_b": column(x["conv_ln_b_2"]),
        "n2_g": column(x["norm2_g_2"]), "final_g": column(x["final_g_2"]),
        "conv_w": x["conv_w_2"][0].reshape(CONV_K, CT, P).transpose(2, 1, 0).reshape(P, -1),
        "w_f": wf.reshape(KD, P, HEADS).transpose(1, 0, 2).reshape(P, -1),
        "w_router": x["w_router_2"][0].reshape(KD, P, E).transpose(1, 0, 2).reshape(P, -1),
        "b_router": np.tile(x["b_router_2"], (P, 1)),
        "b_forget": np.concatenate([x["b_forget_2"][0], np.zeros(P - HEADS, np.float32)])[:, None],
    }
    arrays = {
        "xT_in": np.ascontiguousarray(np.concatenate([x["meta_tokens"], x["x"][0]]).T),
        "stream": stream,
        "ada": np.ascontiguousarray(x["w_ada_2"][0].T.reshape(48, P, D)),
        "c_in": np.ascontiguousarray(x["c_2"][0]),
        "cols_in": np.ascontiguousarray(np.concatenate([cols[k] for k in COLS], axis=1)),
        "const_in": shape_constants(),
        "w_exp_in": np.ascontiguousarray(x["w_exp_in_2"][0]).reshape(E * 8, P, 2 * D),
        "w_exp_out": np.ascontiguousarray(x["w_exp_out_2"][0]).reshape(E * 8, P, D),
        "b_exp": np.ascontiguousarray(np.concatenate([x["b_exp_in_2"][0], x["b_exp_out_2"][0]], axis=1)),
    }
    nc = bacc.Bacc("TRN2", target_bir_lowering=False, num_devices=1)
    args = {n: nc.dram_tensor(n, a.shape, mybir.dt.from_np(a.dtype), kind="ExternalInput").ap()
            for n, a in arrays.items()}
    out = nc.dram_tensor("outT", (D, SEQ), mybir.dt.float32, kind="ExternalOutput").ap()
    build(nc, out=out, **args)
    r = run_bass_kernel_spmd(nc, [arrays], core_ids=[0])
    return np.ascontiguousarray(r.results[0]["outT"].T)[None]
```

```python
import concourse.bass as bass
from concourse import mybir
from concourse.alu_op_type import AluOpType as ALU
from contextlib import ExitStack
import numpy as np

P = 128
D = 1024
KD = D // P
SEQ = 256
META = 16
TOK = SEQ + META
FF = 2816
NF = FF // P
HEADS = 8
E = 32
TOPK = 4
EPS1 = 1e-6
EPS2 = 1e-5
MLA_SCALE = 96 ** -0.5
CONV_K = 31
CT = 4
PIECE = 2048
BLK = 16
RING = 6
SLOTS = 12
SPLIT_BUFS = 3
SLOT_TOK = 64
MAX_BLOCKS = E + SEQ * TOPK // SLOT_TOK
NEG = -1e30

FFN_PIECES = NF + NF // 2
MIX1_BLOCKS = 448
MIX2_BLOCKS = 416
MIX1_PIECES = MIX1_BLOCKS // BLK
MIX2_PIECES = MIX2_BLOCKS // BLK


FFN1_AT = 0
MIX1_AT = FFN_PIECES
FFN2_AT = MIX1_AT + MIX1_PIECES
MIX2_AT = FFN2_AT + FFN_PIECES
DENSE = MIX2_AT + MIX2_PIECES
ROUNDS = DENSE // RING
assert DENSE % RING == 0 and FFN_PIECES % SPLIT_BUFS == 0 and RING % SPLIT_BUFS == 0 and RING % 2 == 0


MIX1_PROJ = 10
MIX1_GATES = range(MIX1_AT + 12, MIX1_AT + 20)
SPLIT_PIECES = (list(range(0, MIX1_AT + MIX1_PROJ)) + list(MIX1_GATES)
                + list(range(FFN2_AT, DENSE)))
ORDER = {p: n for n, p in enumerate(SPLIT_PIECES)}
BUF = {}
for _start, _n in ((FFN1_AT, FFN_PIECES), (MIX1_AT, MIX1_PROJ), (FFN2_AT, FFN_PIECES), (MIX2_AT, MIX2_PIECES)):
    for _i in range(_n):
        BUF[_start + _i] = _i % SPLIT_BUFS
for _p in MIX1_GATES:
    BUF[_p] = (_p - MIX1_GATES[0] + 1) % 2


def last_user(p):
    return max((q for q in SPLIT_PIECES if q < p and BUF[q] == BUF[p]), default=None)


def loads_of(p):
    return p // RING + 1


COLS = {}


def _columns():
    at = 0
    for name, n in (("f1_pre", 8), ("f1_post", 8), ("mix_pre", 8), ("b_gate", 16), ("q_g", 3), ("kv_g", 2),
                    ("mix_post", 8), ("f2_pre", 8), ("f2_post", 8), ("b_ada", 48), ("n1_g", 8),
                    ("conv_b", 4), ("ln_g", 4), ("ln_b", 4), ("n2_g", 8), ("final_g", 8),
                    ("conv_w", CT * CONV_K), ("w_f", KD * HEADS), ("w_router", KD * E),
                    ("b_router", E), ("b_forget", 1)):
        COLS[name] = (at, n)
        at += n
    return at


NCOLS = _columns()

CONST = {}


def _const_columns():
    at = 0
    for name, n in (("ones", 128), ("eps1", 1), ("eps2", 1), ("one", 1), ("ident", 128), ("neg_ones", 128), ("neg_tri_ge", 128), ("tri_le", 128),
                    ("strict", 128), ("cap", 128), ("mla_mask", 416), ("causal", 128), ("iota", 256),
                    ("cos", TOK), ("sin", TOK), ("sel", HEADS * 128)):
        CONST[name] = (at, n)
        at += n
    return at


NCONST = _const_columns()
NFIRST = 131


def shape_constants():
    c = np.zeros((P, NCONST), np.float32)

    def put(name, a):
        at, n = CONST[name]
        c[: a.shape[0], at:at + n] = a

    i, j = np.arange(128)[:, None], np.arange(128)[None, :]
    put("ident", np.eye(128))
    put("ones", np.ones((128, 128)))
    put("neg_ones", -np.ones((128, 128)))
    put("neg_tri_ge", -(i >= j).astype(np.float32))
    put("tri_le", (i <= j).astype(np.float32))
    put("strict", (i < j).astype(np.float32))
    put("cap", np.where(i < j, 3e38, NEG))
    later = np.where((i < 64) & (np.arange(64)[None, :] >= 0), NEG, 0.0)
    mask = np.zeros((128, 416))
    mask[:, META + 64:144] = later
    mask[:, 144 + META + 192:] = later
    put("mla_mask", mask)
    put("causal", np.where(j <= i, 0.0, NEG))
    put("iota", np.tile(np.arange(256), (128, 1)))
    inv = 10000.0 ** (-np.arange(16, dtype=np.float32) / 16)
    ang = (np.arange(TOK, dtype=np.float32)[None, :] * inv.astype(np.float32)[:, None]).astype(np.float32)
    put("cos", np.tile(np.concatenate([np.cos(ang), np.cos(ang)]), (4, 1)))
    put("sin", np.tile(np.concatenate([-np.sin(ang), np.sin(ang)]), (4, 1)))
    sel = np.zeros((HEADS, HEADS * 128))
    for h in range(HEADS):
        sel[h, h * 128:(h + 1) * 128] = 1.0
    put("sel", sel)
    put("eps1", np.full((128, 1), EPS1))
    put("eps2", np.full((128, 1), EPS2))
    put("one", np.ones((128, 1)))
    return c


def build(nc, xT_in, stream, ada, c_in, cols_in, const_in, w_exp_in, w_exp_out, b_exp, out):
    ENG = mybir.EngineType
    f32, f32r, i32, u32 = mybir.dt.float32, mybir.dt.float32r, mybir.dt.int32, mybir.dt.uint32
    ACT = mybir.ActivationFunctionType
    AX = mybir.AxisListType
    PE_, ACT_, DVE_, SP_ = (ENG.PE, ENG.Activation, ENG.DVE, ENG.SP)
    ctx = ExitStack()
    with ctx:
        def sb(name, shape, dt=f32):
            return ctx.enter_context(nc.sbuf_tensor(name, shape, dt))

        def sem(name):
            return ctx.enter_context(nc.semaphore(name))

        place = [-(-nc.sbuf_base // 64) * 64]

        def at_place(name, shape, dt=f32, over=None):
            size = int(np.prod(shape[1:])) * 4
            offset = place[0] if over is None else over
            if over is None:
                place[0] += size
            return nc.alloc_sbuf_tensor_at(name, shape, dt, offset=offset), offset

        ring, ring_at = at_place("ring", [P, SLOTS, PIECE])
        res, _ = at_place("res", [P, KD, TOK])
        nrm, nrm_at = at_place("nrm", [P, KD, TOK])
        sq, sq_at = at_place("sq", [P, KD, TOK])
        ARENA = 16896
        arena, arena_at = at_place("arena", [P, ARENA])
        slot_bytes = PIECE * 4
        w_hi, _ = at_place("w_hi", [P, SPLIT_BUFS, PIECE], f32r, over=ring_at + RING * slot_bytes)
        w_lo, _ = at_place("w_lo", [P, SPLIT_BUFS, PIECE], f32r, over=ring_at + (RING + SPLIT_BUFS) * slot_bytes)
        x_hi, _ = at_place("x_hi", [P, KD, TOK], f32r, over=nrm_at)
        x_lo, _ = at_place("x_lo", [P, KD, TOK], f32r, over=sq_at)
        hid_hi, _ = at_place("hid_hi", [P, NF, TOK], f32r, over=arena_at)
        hid_lo, _ = at_place("hid_lo", [P, NF, TOK], f32r, over=arena_at + NF * TOK * 4)
        nc.bump_sbuf(place[0] - nc.sbuf_base)
        cst = sb("cst", [P, NCONST])
        col = sb("col", [P, NCOLS])
        small = sb("small", [P, 512])
        rstd = sb("rstd", [P, TOK])
        rtmp = sb("rtmp", [P, TOK])
        count_i = sb("count_i", [1, E + 1], i32)
        block_i = sb("block_i", [1, 2 * (MAX_BLOCKS + 1)], i32)
        idx_u = sb("idx_u", [P, 2, 8], u32)
        bank = [ctx.enter_context(nc.psum_tensor(f"bank{i}", [P, 512], f32)) for i in range(8)]

        def const(name, lo=0, hi=None, rows=P):
            at, n = CONST[name]
            return cst[0:rows, at + lo:at + (n if hi is None else hi)]

        def vec(name, i=0, n=1, rows=P):
            at, _ = COLS[name]
            return col[0:rows, at + i:at + i + n]

        class Area:

            def __init__(self, whole, at=0):
                self.whole, self.at = whole, at

            def take(self, *shape):
                n = int(np.prod(shape))
                v = self.whole[:, self.at:self.at + n]
                self.at += n
                assert self.at <= self.whole.shape[1], (self.at, self.whole.shape)
                if len(shape) == 2:
                    v = v.rearrange("p (a b) -> p a b", a=shape[0])
                if len(shape) == 3:
                    v = v.rearrange("p (a b c) -> p a b c", a=shape[0], b=shape[1])
                return v

        sm_area = Area(small)
        half_f1 = sm_area.take(8)
        half_f2 = sm_area.take(8)
        mod = sm_area.take(48)
        ada_acc = sm_area.take(4)
        g1s = sm_area.take(8)
        g2s = sm_area.take(8)
        c_col = sm_area.take(8)
        top = sm_area.take(2, 8)
        topi = sm_area.take(2, 8)
        tope = sm_area.take(2, 8)
        tops = sm_area.take(2, 2)
        smx = sm_area.take(2, 2)
        ssum = sm_area.take(2, 2)
        srec = sm_area.take(2, 2)
        gate = sm_area.take(2, E)
        slot = sm_area.take(2, E)
        csum = sm_area.take(E)
        ctmp = sm_area.take(E)
        nb_col = sm_area.take(1)
        cum_col = sm_area.take(1)

        a = Area(arena)
        x_all = arena[:, 0:KD * TOK].rearrange("p (a b) -> p a b", a=KD)
        a.take(2, NF, TOK)
        sig = a.take(2, TOK)
        hid = a.take(TOK)
        ada_w = a.take(2, D)
        c_all = a.take(D)
        ada_t = a.take(D)

        a = Area(arena)
        lat = a.take(7, TOK)
        sb_q = a.take(4, SEQ)
        sb_k = a.take(4, TOK)
        sb_v = a.take(3, 512)
        x_mix1 = arena[:, a.at:a.at + KD * TOK].rearrange("p (a b) -> p a b", a=KD)
        lat_sq = arena[:, a.at:a.at + 5 * TOK].rearrange("p (a b) -> p a b", a=5)
        graw = a.take(16, SEQ)
        uq = a.take(8, SEQ)
        kn = a.take(4, TOK)
        v2 = a.take(3, 512)
        t_e = a.take(2, 640)
        t_sp = a.take(2, 640)
        spare = ring[:, RING + SPLIT_BUFS - 1, :]
        t_a = spare[:, 0:1280].rearrange("p (a b) -> p a b", a=2)
        qr = uq[:, 4:6, :]
        kr = lat[:, 5, :]
        a2 = Area(arena, a.at - 2560)
        p_sb = a2.take(2, 416)
        pt_sb = a2.take(2, 640)
        y_area = ring[:, SLOTS - 1, :]
        y_sb = y_area[:, 0:1024].rearrange("p (a b) -> p a b", a=4)
        y_mla = y_area[:, 1024:2048].rearrange("p (a b) -> p a b", a=4)
        mix_o = graw[:, 0:8, :]
        mtmp = spare[:, 1280:1792].rearrange("p (a b) -> p a b", a=2)

        a = Area(arena)
        ca = a.take(CT, SEQ + CONV_K - 1)
        conv_s = ca[:, :, 0:SEQ]
        cv = a.take(CT, SEQ)
        csg = a.take(2, SEQ)
        q2 = a.take(4, SEQ)
        k2 = a.take(4, SEQ)
        w2v = a.take(2, 512)
        lf = a.take(SEQ)
        lft = a.take(SEQ)
        lfn = a.take(2, HEADS)
        fcum = a.take(2, HEADS)
        neg_f = a.take(SEQ)
        x_mix2 = arena[:, a.at:a.at + KD * SEQ].rearrange("p (a b) -> p a b", a=KD)
        graw2 = a.take(16, SEQ)
        p2 = a.take(2, 384)
        pt2 = a.take(2, 384)
        y2 = a.take(4, SEQ)
        mt2 = a.take(2, SEQ)
        x_out2 = graw2[:, 0:8, :]
        sq_n2 = graw2[:, 8:16, :]
        o_hi, _ = at_place("o_hi", [P, 8, SEQ], f32r, over=arena_at + a.at * 4)
        o_lo, _ = at_place("o_lo", [P, 8, SEQ], f32r, over=arena_at + (CT * (SEQ + CONV_K - 1) + 6 * SEQ) * 4)
        assert a.at + 8 * SEQ <= ARENA and CT == 4

        a = Area(arena)
        h2n = a.take(2, D)
        acc = a.take(KD, SEQ)
        lgt = a.take(2, E)
        msk = a.take(2, E)
        b_all = a.take(3 * D)
        S = a.take(2, SLOT_TOK)
        SG = a.take(2, 2, SLOT_TOK)
        onehot1 = a.take(SLOT_TOK)
        onehot2 = a.take(SLOT_TOK)
        past = a.take(MAX_BLOCKS + 1)
        table = a.take(2, MAX_BLOCKS + 1)
        xg = a.take(512)
        xT = a.take(4, 2, SLOT_TOK)
        ST = a.take(2, P)
        gl = a.take(512)
        ul = a.take(512)
        eg = a.take(512)
        hmT = a.take(4, 2, SLOT_TOK)
        ye = a.take(512)
        fin = a.take(KD, SEQ)

        LAST_BANKS = (2, 3)
        FIN_ORDER = (0, 1, 4, 5, 2, 3, 6, 7)

        x_in = sem("x_in")
        const_sem = sem("const_in")
        const_rest = sem("const_rest")
        cols_sem = sem("cols_in")
        c_sem = sem("c_in")
        slot_in = [sem(f"slot_in{s}") for s in range(SLOTS)]
        freed = sem("freed")
        ada_in = [sem(f"ada_in{i}") for i in range(2)]
        ada_used = sem("ada_used")
        ada_copied = sem("ada_copied")
        bias_in = sem("bias_in")
        stored_out = sem("stored_out")
        act_chain = sem("act_chain")
        dve_chain = sem("dve_chain")
        n_sq = sem("norm_squares")
        n_sum = sem("norm_sum")
        n_rs = sem("norm_rstd")
        n_out = sem("normed")
        x_high = sem("x_high")
        x_split = sem("x_split")
        x_whole = sem("x_whole")
        o_high = sem("o_high")
        o_split = sem("o_split")
        proj = sem("projected")

        def bases(*parts):
            at, found = 0, {}
            for name, n in parts:
                found[name] = at
                at += n
            return found

        AT = {
            n_sq: bases(("f1_pre", 8), ("f1_post", 8), ("mix_pre", 8), ("cq", 3), ("ckv", 2), ("mix_post", 8),
                        ("f2_pre", 8), ("f2_post", 8), ("n1", 8), ("ln_var", 4), ("n2", 8), ("final", 8)),
            n_sum: bases(*((n, 1) for n in ("f1_pre", "f1_post", "mix_pre", "cq", "ckv", "mix_post", "f2_pre",
                                            "f2_post", "n1", "ln_mean", "ln_var", "n2", "final"))),
            n_out: bases(("f1_pre", 8), ("mix_pre", 8), ("cq", 3), ("ckv", 2), ("f2_pre", 8), ("n1", 8),
                         ("ln_var", 4), ("n2", 8)),
            proj: bases(("lat", 7), ("qk", 8), ("v", 1), ("uq", 8), ("ukv", 5), ("gates", 16), ("o1", 8),
                        ("w1", 8), ("conv", 4), ("f", 1), ("qk2", 8), ("v2", 1), ("gates2", 16), ("o2", 8),
                        ("w2", 8)),
        }
        AT[n_rs] = {n: v - (v > AT[n_sum]["ln_mean"]) for n, v in AT[n_sum].items() if n != "ln_mean"}
        AT[x_split] = bases(("f1_pre", KD), ("mix_pre", KD), ("f2_pre", KD), ("n1", KD), ("w2", KD))
        updated = {n: sem(f"residual_{n}") for n in ("f1", "m1", "f2", "m2")}
        up_ready = sem("up_ready")
        exp_ready = sem("exp_ready")
        c_silu = sem("c_silu")
        fin_x = sem("fin_x")
        hid_ready = sem("hid_ready")
        hid_high = sem("hid_high")
        hid_split = sem("hid_split")
        w_high = sem("w_high")
        w_split = sem("w_split")
        down_ready = sem("down_ready")
        down_out = sem("down_out")
        evac = {n: sem(f"evac_{n}") for n in ("lat", "qk", "v", "uq", "ukv", "gates", "o1", "w1",
                                              "conv", "qk2", "v2", "f", "gates2", "o2", "w2")}
        roped = sem("roped")
        z_ready = sem("z_ready")
        e_done = sem("e_done")
        sp_done = sem("sp_done")
        la_ready = sem("la_ready")
        cap_done = sem("cap_done")
        at_done = sem("at_done")
        av_done = sem("av_done")
        y_out = sem("y_out")
        soft = {k: {n: sem(f"{n}_{k}") for n in ("scores", "maxed", "exped", "normed", "pt", "pt_v", "pt_a",
                                                 "pv", "y")} for k in ("mla", "fa")}
        gates_ready = sem("gates_ready")
        conv_sig = sem("conv_sig")
        conv_in = sem("conv_in")
        conv_done = sem("conv_done")
        ln_in = sem("ln_in")
        ln_sigmoid = sem("ln_sigmoid")
        conv_out = sem("conv_out")
        logf_ready = sem("logf_ready")
        logf_t = sem("logf_t")
        logf_n = sem("logf_n")
        f_sums = sem("f_sums")
        f_out = sem("f_out")
        logits = sem("logits")
        top_max = sem("top_max")
        top_exp = sem("top_exp")
        masked = sem("masked")
        counted = sem("counted")
        counts_ready = sem("counts_ready")
        nat = sem("nat")
        nat_out = sem("nat_out")
        nb_ready = sem("nb_ready")
        cum_ready = sem("cum_ready")
        past_ready = sem("past_ready")
        table_sums = sem("table_sums")
        m_S = sem("m_S")
        m_SG = sem("m_SG")
        m_oh1 = sem("m_oh1")
        m_gath = sem("m_gath")
        m_xg = sem("m_xg")
        m_xt = sem("m_xt")
        m_xts = sem("m_xts")
        m_sts = sem("m_sts")
        m_hc = sem("m_hc")
        m_gl = sem("m_gl")
        m_eg = sem("m_eg")
        m_hm = sem("m_hm")
        m_hmt = sem("m_hmt")
        m_hms = sem("m_hms")
        m_y = sem("m_y")
        m_ys = sem("m_ys")
        m_comb = sem("m_comb")
        m_acc = sem("m_acc")
        moe_dve = sem("moe_dve")
        fin_ready = sem("fin_ready")

        def real(x):
            return x[:, META:TOK]

        block = ctx.enter_context(nc.Block())

        @block.sync
        def _(sp):
            sp.dma_start(res[:, :, :], xT_in.rearrange("(k p) t -> p k t", p=P)).then_inc(x_in, 16)

            def load_piece(p, it=None):
                n = p if it is None else it * RING + p
                sp.wait_ge(freed, n + 1)
                src = stream[n, :, :] if it is None else \
                    stream[bass.ds(n, 1), :, :].rearrange("o p n -> p (o n)")
                sp.dma_start(ring[:, p % RING, :], src).then_inc(slot_in[p % RING], 16)

            def load_ada(p, it=None):
                for i in range(2):
                    n = 2 * (p - RING + 1) + i
                    if it is not None:
                        n = it * (2 * RING) + n
                    sp.wait_ge(ada_used, n)
                    src = ada[n, :, :] if it is None else \
                        ada[bass.ds(n, 1), :, :].rearrange("o p n -> p (o n)")
                    sp.dma_start(ada_w[:, i, :], src).then_inc(ada_in[i], 16)

            for p in range(RING):
                load_piece(p)
                if p == 0:
                    sp.dma_start(col[:, :], cols_in).then_inc(cols_sem, 16)
                if p == 1:
                    sp.dma_start(c_all, c_in.partition_broadcast(P)).then_inc(c_sem, 16)
                if p == 2:
                    for i in range(2):
                        sp.dma_start(ada_w[:, i, :], ada[i, :, :]).then_inc(ada_in[i], 16)
                if p == 3:
                    sp.dma_start(cst[:, NFIRST:], const_in[:, NFIRST:]).then_inc(const_rest, 16)
            ada_last = RING - 1 + KD * 6 // 2 - 1
            with sp.Fori(1, ada_last // RING) as it:
                for j in range(RING):
                    load_piece(j, it)
                    load_ada(j, it)
            for p in range(ada_last // RING * RING, (ada_last // RING + 1) * RING):
                load_piece(p)
                if p <= ada_last:
                    load_ada(p)

            def expert_piece(e, j):
                if j < 8:
                    return ring[:, j, :], w_exp_in[bass.ds(e * 8 + j, 1), :, :].rearrange("o p n -> p (o n)")
                return (ring[:, j, :].rearrange("p (t n) -> p t n", t=2),
                        w_exp_out[bass.ds(e * 8 + (j - 8) * 2, 2), :, :].rearrange("t p n -> p t n"))

            with sp.Fori(ada_last // RING + 1, ROUNDS - 1) as it:
                for j in range(RING):
                    load_piece(j, it)
            for p in range(DENSE - RING, DENSE):
                load_piece(p)
            for j in range(SLOTS):
                if j < RING - 1:
                    sp.wait_ge(freed, DENSE + j + 1)
                if j == RING - 1:
                    sp.wait_ge(n_sum, AT[n_sum]["n2"] + 1)
                dst, src = expert_piece(0, j)
                sp.dma_start(dst, src).then_inc(slot_in[j], 16)
            sp.wait_ge(counts_ready, 1)
            cum = sp.alloc_register("sp_cum")
            n0 = sp.value_load(count_i[0:1, 0:1], min_val=1, max_val=4)
            sp.reg_mov(cum, 0)
            sp.reg_add(cum, cum, n0)
            with sp.Fori(1, E) as e:
                before = nc.snap(cum, engines=[SP_])
                for j in range(SLOTS):
                    sp.wait_ge(freed, before * SLOTS + (DENSE + RING + 1 - SLOTS + j))
                    dst, src = expert_piece(e, j)
                    sp.dma_start(dst, src).then_inc(slot_in[j], 16)
                n = sp.value_load(count_i[0:1, bass.ds(e, 1)], min_val=1, max_val=4)
                sp.reg_add(cum, cum, n)
            for half in range(2):
                k0, k1 = half * KD // 2, (half + 1) * KD // 2
                sp.wait_ge(fin_ready, k1)
                sp.dma_start(out.rearrange("(k p) t -> p k t", p=P)[:, k0:k1, :], fin[:, k0:k1, :])\
                    .then_inc(stored_out, 16)
            sp.wait_ge(stored_out, 32)

        @block.tensor
        def _(pe):
            mm = nc.tensor.matmul
            pe.wait_ge(const_sem, 16)

            def norm_sum(n, tiles, width, squares=sq):
                for m in range(tiles):
                    pe.wait_ge(n_sq, AT[n_sq][n] + m + 1)
                    last = mm(bank[7][:, 0:width], const("ones"), squares[:, m, 0:width],
                              start=(m == 0), stop=(m == tiles - 1))
                last.then_inc(n_sum, 1)

            def three(out_, wh, wl, xh, xl, start, stop):
                begin = mm(out_, wh, xh, start=start, stop=False)
                mm(out_, wh, xl, start=False, stop=False)
                return begin, mm(out_, wl, xh, start=False, stop=stop)

            def ffn(f, at, lo):
                w = TOK - lo
                base = f * NF

                def up_tile(j, piece, hid_at, first=False):
                    pe.wait_ge(w_split, piece)
                    pe.wait_ge(hid_ready, hid_at)
                    for g in range(2):
                        for k in range(KD):
                            c0 = (g * KD + k) * P
                            b = j % SPLIT_BUFS
                            if first and g == 0:
                                pe.wait_ge(x_split, AT[x_split]["f1_pre" if f == 0 else "f2_pre"] + k + 1)
                            begin, last = three(bank[2 * (j % 2) + g][:, 0:w], w_hi[:, b, c0:c0 + P],
                                                w_lo[:, b, c0:c0 + P], x_hi[:, k, lo:TOK], x_lo[:, k, lo:TOK],
                                                k == 0, k == KD - 1)
                            if g == 0 and k == 0:
                                begin.then_inc(freed, 1)
                    last.then_inc(up_ready, 1)

                ahead = NF % RING
                for j in range(ahead):
                    up_tile(j, ORDER[at] + j + 1, base + j + 1, first=(j == 0))
                with pe.Fori(0, NF // RING) as it:
                    for j in range(ahead, ahead + RING):
                        up_tile(j, it * RING + (ORDER[at] + j + 1), it * RING + (base + j + 1))
                at_block = NF * BLK
                for m in range(KD):
                    pe.wait_ge(down_out, f * KD + m + 1)
                    for k in range(NF):
                        p, c0 = at_block // BLK, at_block % BLK * P
                        if c0 == 0:
                            pe.wait_ge(w_split, ORDER[at] + p + 1)
                        if m == 0:
                            pe.wait_ge(hid_split, base + k + 2)
                        b = p % SPLIT_BUFS
                        begin, last = three(bank[4 + m % 2][:, 0:w], w_hi[:, b, c0:c0 + P], w_lo[:, b, c0:c0 + P],
                                            hid_hi[:, k, 0:w], hid_lo[:, k, 0:w], k == 0, k == NF - 1)
                        if c0 == 0:
                            begin.then_inc(freed, 1)
                        at_block += 1
                    last.then_inc(down_ready, 1)

            class Cursor:

                def __init__(self, piece):
                    self.b = piece * BLK
                    self.owed = 0

                def take(self, n=1):
                    p, c = self.b // BLK, (self.b % BLK) * P
                    begins = self.b % BLK == 0
                    parts = None
                    if p in ORDER:
                        b = BUF[p]
                        parts = w_hi[:, b, c:c + n * P], w_lo[:, b, c:c + n * P]
                    if begins:
                        if p in ORDER:
                            pe.wait_ge(w_split, ORDER[p] + 1)
                        else:
                            pe.wait_ge(slot_in[p % RING], 16 * loads_of(p))
                    self.b += n
                    return ring[:, p % RING, c:c + n * P], parts, int(begins)

            def tile(cur, out_, rhs, n_k, ready=None):
                for k in range(n_k):
                    w, parts, back = cur.take()
                    x = rhs(k)
                    flags = (k == 0, k == n_k - 1)
                    if isinstance(x, tuple):
                        begin, last = three(out_, *parts, *x, *flags)
                    else:
                        begin = last = mm(out_, w, x, start=flags[0], stop=flags[1])
                    cur.owed += back
                    if cur.owed and k < n_k - 1:
                        begin.then_inc(freed, cur.owed)
                        cur.owed = 0
                if ready is not None:
                    last.then_inc(ready, 1)

            def natural(cur, n_k, parts, ready):
                for k in range(n_k):
                    w, w_parts, back = cur.take(4)
                    for n, (o, lhs) in enumerate(parts):
                        x = lhs(k)
                        flags = (k == 0, k == n_k - 1)
                        if isinstance(x, tuple):
                            begin, last = three(o, *x, *w_parts, *flags)
                        else:
                            begin = last = mm(o, x, w, start=flags[0], stop=flags[1])
                        if n == 0 and back + cur.owed:
                            begin.then_inc(freed, back + cur.owed)
                            cur.owed = 0
                last.then_inc(ready, 1)

            def split_x(k, lo, hi):
                return x_hi[:, k, lo:hi], x_lo[:, k, lo:hi]

            def split_x_first(n, k, lo, hi):
                pe.wait_ge(x_split, AT[x_split][n] + k + 1)
                return split_x(k, lo, hi)

            norm_sum("f1_pre", KD, TOK)
            ffn(0, FFN1_AT, 0)
            norm_sum("f1_post", KD, TOK)
            norm_sum("mix_pre", KD, TOK)
            pe.wait_ge(const_rest, 16)
            cur = Cursor(MIX1_AT)
            for i in range(7):
                if i >= 2:
                    pe.wait_ge(evac["lat"], i - 1)
                tile(cur, bank[i % 2][:, 0:TOK], lambda k: split_x_first("mix_pre", k, 0, TOK) if i == 0
                     else split_x(k, 0, TOK), KD, proj)
            for i in range(8):
                if i >= 2:
                    pe.wait_ge(evac["qk"], i - 1)
                lo = META if i < 4 else 0
                tile(cur, bank[2 + i % 2][:, 0:TOK - lo], lambda k: split_x(k, lo, TOK), KD, proj)
            pe.wait_ge(evac["lat"], 7)
            v_parts = ((META, P), (META + P, P), (0, META))
            natural(cur, KD, [(bank[4 + t][0:n, :], lambda k, c0=c0, n=n: split_x(k, c0, c0 + n))
                              for t, (c0, n) in enumerate(v_parts)], proj)
            norm_sum("cq", 3, SEQ, lat_sq)
            for m in range(2):
                pe.wait_ge(n_sq, AT[n_sq]["ckv"] + m + 1)
                last = mm(bank[0][:, 0:TOK], const("ones"), lat_sq[:, 3 + m, :], start=(m == 0), stop=(m == 1))
            last.then_inc(n_sum, 1)
            pe.wait_ge(n_out, AT[n_out]["cq"] + 3)
            pe.wait_ge(evac["qk"], 8)
            for i in range(8):
                if i >= 2:
                    pe.wait_ge(evac["uq"], i - 1)
                tile(cur, bank[2 + i % 2][:, 0:SEQ], lambda k: lat[:, k, META:TOK], 3, proj)
            pe.wait_ge(n_out, AT[n_out]["ckv"] + 2)
            for i in range(4):
                if i >= 2:
                    pe.wait_ge(evac["ukv"], i - 1)
                tile(cur, bank[i % 2][:, 0:TOK], lambda k: lat[:, 3 + k, :], 2, proj)
            pe.wait_ge(evac["v"], 3)
            natural(cur, 2, [(bank[4 + t][0:n, :], lambda k, c0=c0, n=n: lat[:, 3 + k, c0:c0 + n])
                             for t, (c0, n) in enumerate(v_parts)], proj)
            pe.wait_ge(evac["uq"], 8)
            pe.wait_ge(evac["ukv"], 7)

            def gate_tile(i, which):
                if i >= 2:
                    pe.wait_ge(evac[which], i - 1)
                tile(cur, bank[6 + i % 2][:, 0:SEQ], lambda k: split_x(k, META, TOK) if which == "gates"
                     else split_x(k, 0, SEQ), KD, proj)

            def rows(x, j, n=64):
                return x[64 * j:64 * j + n]

            def z(h):
                m, j = h // 2, h % 2
                if h >= 2:
                    pe.wait_ge(at_done, h - 1)
                X, Y = bank[h % 2], bank[2 + h % 2]
                pos = (64 * j, 0)
                kk, qq = rows(sb_k[:, m, :], j), rows(sb_q[:, m, :], j)
                mm(X[:, 0:256], kk[:, META:META + P], qq, start=True, stop=False, tile_position=pos,
                   skip_group_check=True)
                mm(X[:, 256:384], kk[:, META + P:TOK], qq[:, P:SEQ], start=False, stop=False, tile_position=pos,
                   skip_group_check=True)
                mm(Y[0:META, 0:256], kk[:, 0:META], qq, start=True, stop=False, tile_position=pos,
                   skip_group_check=True).then_inc(z_ready, 1)

            def suffix(h):
                pe.wait_ge(sp_done, h + 1)
                X, Y, sp_ = bank[h % 2], bank[2 + h % 2], t_sp[:, h % 2, :]
                tri, no = const("neg_tri_ge"), const("neg_ones")
                kw = dict(start=False, skip_group_check=True)
                mm(X[:, 0:256], tri, sp_[:, 0:256], stop=False, **kw)
                mm(X[:, 128:256], no, sp_[:, 256:384], stop=False, **kw)
                mm(X[:, 256:384], tri, sp_[:, 256:384], stop=True, **kw)
                mm(Y[0:META, 0:256], no[:, 0:META], sp_[:, 0:256], stop=False, **kw)
                mm(Y[0:META, 128:256], no[:, 0:META], sp_[:, 256:384], stop=False, **kw)
                mm(Y[0:META, 0:256], const("neg_tri_ge", 0, META, META), sp_[0:META, 384:640], stop=True,
                   **kw).then_inc(la_ready, 1)

            def pv(h, v, ready, parts):
                j = h % 2
                pos = (0, 64 * j)
                o = bank[4 + h // 2 % 2][64 * j:64 * j + 64, 0:SEQ]
                for n, (vt, n_rows, ap, lo) in enumerate(parts):
                    last = mm(o[:, lo:SEQ], v[0:n_rows, vt, 64 * h:64 * h + 64], ap,
                              start=(n == 0), stop=(n == len(parts) - 1), tile_position=pos,
                              skip_group_check=True)
                last.then_inc(ready, 1)

            def av(h):
                pe.wait_ge(at_done, h + 1)
                if h % 2 == 0 and h >= 4:
                    pe.wait_ge(y_out, h // 2 - 1)
                t = t_a[:, h % 2, :]
                pv(h, sb_v, av_done,
                   ((0, P, t[:, 0:256], 0), (1, P, t[:, 256:384], P), (2, META, t[0:META, 384:640], 0)))

            gi = 0
            z(0)
            for h in range(HEADS):
                if h + 1 < HEADS:
                    z(h + 1)
                gate_tile(gi, "gates")
                gi += 1
                suffix(h)
                if h:
                    av(h - 1)
            av(HEADS - 1)

            def scores_mla(h):
                m, j = h // 2, h % 2
                if h >= 2:
                    pe.wait_ge(soft["mla"]["maxed"], h - 1)
                if h == 0:
                    pe.wait_ge(at_done, HEADS)
                    pe.wait_ge(roped, 2)
                Bk = bank[h % 2]
                r, g = h // 4, 32 * (h % 4)
                qn_, kn_ = rows(uq[:, m, :], j), rows(kn[:, m, :], j)
                qr_, kr_ = qr[g:g + 32, r, :], kr[g:g + 32, :]
                for t, (c0, n) in enumerate(((0, 144), (144, TOK))):
                    mm(Bk[:, c0:c0 + n], qn_[:, t * P:t * P + P], kn_[:, 0:n], start=True, stop=False,
                       tile_position=(64 * j, 0), skip_group_check=True)
                    last = mm(Bk[:, c0:c0 + n], qr_[:, t * P:t * P + P], kr_[:, 0:n], start=False, stop=True,
                              tile_position=(g, 0), skip_group_check=True)
                last.then_inc(soft["mla"]["scores"], 1)

            def transposes(kind, h, p, parts):
                s = soft[kind]
                pe.wait_ge(s["normed"], h + 1)
                if h:
                    pe.wait_ge(s["pt_v"], h)
                    if kind == "mla":
                        pe.wait_ge(s["pt_a"], h)
                for o, i in parts:
                    last = nc.tensor.transpose(o, i, const("ident"))
                last.then_inc(s["pt"], 1)

            def pt_mla(h):
                p = p_sb[:, h % 2, :]
                b2, b3 = bank[2], bank[3]
                transposes("mla", h, p, ((b3[0:META, 0:P], p[:, 0:META]), (b2[:, 0:P], p[:, META:144]),
                                         (b3[0:META, P:256], p[:, 144:160]), (b2[:, P:256], p[:, 160:288]),
                                         (b2[:, 256:384], p[:, 288:416])))

            def pv_mla(h):
                s = soft["mla"]
                pe.wait_ge(s["pt_v"], h + 1)
                pe.wait_ge(s["pt_a"], h + 1)
                if h in (0, 2):
                    pe.wait_ge(y_out, 3 + h // 2)
                if h % 2 == 0 and h >= 4:
                    pe.wait_ge(s["y"], h // 2 - 1)
                t = pt_sb[:, h % 2, :]
                pv(h, v2, s["pv"],
                   ((0, P, t[:, 0:256], 0), (1, P, t[:, 256:384], P), (2, META, t[0:META, 384:640], 0)))

            scores_mla(0)
            for h in range(HEADS):
                if h + 1 < HEADS:
                    scores_mla(h + 1)
                gate_tile(gi, "gates")
                gi += 1
                pt_mla(h)
                if h:
                    pv_mla(h - 1)
            pv_mla(HEADS - 1)

            def out_proj(n, ya, yb_, ready_a, ready_b):
                ready_a()
                for m in range(KD):
                    if m >= 2:
                        pe.wait_ge(evac[n], m - 1)
                    b0 = 2 * (m % 2)
                    tile(cur, bank[b0][:, 0:SEQ], ya, 4)
                    if m == 0:
                        ready_b()
                    tile(cur, bank[b0 + 1][:, 0:SEQ], yb_, 4, proj)

            out_proj("o1", lambda k: y_sb[:, k, :], lambda k: y_mla[:, k, :], lambda: pe.wait_ge(y_out, 4),
                     lambda: (pe.wait_ge(soft["mla"]["y"], 4)))
            pe.wait_ge(evac["o1"], KD)
            for m in range(KD):
                if m >= 2:
                    pe.wait_ge(evac["w1"], m - 1)
                tile(cur, bank[4 + m % 2][:, 0:SEQ], lambda k: nrm[:, k, 0:SEQ], KD, proj)
            norm_sum("mix_post", KD, SEQ)
            norm_sum("f2_pre", KD, SEQ)
            ffn(1, FFN2_AT, META)
            norm_sum("f2_post", KD, SEQ)

            norm_sum("n1", KD, SEQ)
            cur = Cursor(MIX2_AT)
            x2 = lambda k: split_x(k, 0, SEQ)
            for m in range(CT):
                if m >= 2:
                    pe.wait_ge(evac["conv"], m - 1)
                tile(cur, bank[2 * (m % 2)][:, 0:SEQ], x2 if m else lambda k: split_x_first("n1", k, 0, SEQ), KD)
                tile(cur, bank[2 * (m % 2) + 1][:, 0:SEQ], x2, KD, proj)
            pe.wait_ge(x_whole, KD)
            for k in range(KD):
                last = mm(bank[6][0:HEADS, 0:SEQ], vec("w_f", k * HEADS, HEADS), x_mix2[:, k, :],
                          start=(k == 0), stop=(k == KD - 1))
            last.then_inc(proj, 1)
            for i in range(8):
                if i >= 2:
                    pe.wait_ge(evac["qk2"], i - 1)
                tile(cur, bank[4 + i % 2][:, 0:SEQ], x2, KD, proj)
            pe.wait_ge(evac["conv"], CT)
            natural(cur, KD, [(bank[t][:, :], lambda k, t=t: split_x(k, t * P, t * P + P)) for t in range(2)],
                    proj)
            pe.wait_ge(logf_ready, 1)
            for t in range(2):
                last = nc.tensor.transpose(bank[2][:, t * 8:t * 8 + 8], lf[0:8, t * P:t * P + P],
                                           const("ident", 0, 8, 8))
            last.then_inc(logf_t, 1)
            pe.wait_ge(logf_n, 1)
            kw = dict(skip_group_check=True)
            mm(bank[3][:, 0:8], const("tri_le"), lfn[:, 0, :], start=True, stop=False, **kw)
            mm(bank[3][:, 8:16], const("ones"), lfn[:, 0, :], start=False, stop=False, **kw)
            mm(bank[3][:, 8:16], const("tri_le"), lfn[:, 1, :], start=False, stop=True, **kw)
            mm(bank[2][0:8, 256:384], lfn[:, 0, :], const("tri_le"), start=True, stop=False, **kw)
            mm(bank[2][0:8, 384:512], lfn[:, 0, :], const("ones"), start=False, stop=False, **kw)
            mm(bank[2][0:8, 384:512], lfn[:, 1, :], const("tri_le"), start=False, stop=True,
               **kw).then_inc(f_sums, 1)
            pe.wait_ge(evac["qk2"], 8)
            pe.wait_ge(evac["v2"], 2)
            pe.wait_ge(f_out, 2)

            def scores_fa(h):
                m, j = h // 2, h % 2
                if h >= 2:
                    pe.wait_ge(soft["fa"]["maxed"], h - 1)
                Bk = bank[h % 2]
                q_, k_ = rows(q2[:, m, :], j), rows(k2[:, m, :], j)
                for t, (c0, n) in enumerate(((0, P), (P, SEQ))):
                    mm(Bk[:, c0:c0 + n], q_[:, t * P:t * P + P], k_[:, 0:n], start=True, stop=False,
                       tile_position=(64 * j, 0), skip_group_check=True)
                    last = mm(Bk[:, c0:c0 + n], const("sel", h * P, h * P + P, HEADS), neg_f[0:8, 0:n],
                              start=False, stop=True, skip_group_check=True)
                last.then_inc(soft["fa"]["scores"], 1)

            def pt_fa(h):
                p = p2[:, h % 2, :]
                b2 = bank[2]
                transposes("fa", h, p, ((b2[:, 0:P], p[:, 0:P]), (b2[:, P:256], p[:, P:256]),
                                        (b2[:, 256:384], p[:, 256:384])))

            def pv_fa(h):
                s = soft["fa"]
                pe.wait_ge(s["pt_v"], h + 1)
                if h % 2 == 0 and h >= 4:
                    pe.wait_ge(s["y"], h // 2 - 1)
                t = pt2[:, h % 2, :]
                pv(h, w2v, s["pv"], ((0, P, t[:, 0:256], 0), (1, P, t[:, 256:384], P)))

            pe.wait_ge(evac["f"], 1)
            scores_fa(0)
            for h in range(HEADS):
                if h + 1 < HEADS:
                    scores_fa(h + 1)
                gate_tile(2 * h, "gates2")
                gate_tile(2 * h + 1, "gates2")
                pt_fa(h)
                if h:
                    pv_fa(h - 1)
            pv_fa(HEADS - 1)
            pe.wait_ge(soft["fa"]["y"], 3)
            for m in range(CT):
                pe.wait_ge(conv_done, m + 1)
                last = mm(bank[4][:, 0:SEQ], const("ones"), cv[:, m, :], start=(m == 0), stop=(m == CT - 1))
            last.then_inc(n_sum, 1)
            pe.wait_ge(evac["gates2"], 16)
            norm_sum("ln_var", CT, SEQ)
            out_proj("o2", lambda k: (o_hi[:, k, :], o_lo[:, k, :]), lambda k: (o_hi[:, 4 + k, :], o_lo[:, 4 + k, :]),
                     lambda: pe.wait_ge(o_split, 8), lambda: None)
            for m in range(KD):
                if m >= 2:
                    pe.wait_ge(evac["w2"], m - 1)
                tile(cur, bank[4 + m % 2][:, 0:SEQ], x2 if m else lambda k: split_x_first("w2", k, 0, SEQ), KD, proj)
            norm_sum("n2", KD, SEQ, sq_n2)

            pe.wait_ge(x_whole, 2 * KD)
            for t in range(2):
                for k in range(KD):
                    last = mm(bank[t][:, 0:E], nrm[:, k, t * P:t * P + P], vec("w_router", k * E, E),
                              start=(k == 0), stop=(k == KD - 1))
            last.then_inc(logits, 1)
            for t in range(2):
                for k in range(KD):
                    b = bank[2 + 2 * t + k // 4]
                    last = nc.tensor.transpose(b[:, (k % 4) * P:(k % 4 + 1) * P], nrm[:, k, t * P:t * P + P],
                                               const("ident"))
            last.then_inc(nat, 1)
            pe.wait_ge(masked, 1)
            mm(bank[6][:, 0:E], const("strict"), msk[:, 0, :], start=True, stop=False, **kw)
            mm(bank[6][:, E:2 * E], const("ones"), msk[:, 0, :], start=False, stop=False, **kw)
            mm(bank[6][:, E:2 * E], const("strict"), msk[:, 1, :], start=False, stop=False, **kw)
            mm(bank[6][:, 2 * E:3 * E], const("ones"), msk[:, 0, :], start=False, stop=False, **kw)
            mm(bank[6][:, 2 * E:3 * E], const("ones"), msk[:, 1, :], start=False, stop=True,
               **kw).then_inc(counted, 1)

            for t in range(2):
                last = mm(bank[0][0:E, 0:1], msk[:, t, :], const("ones", 0, 1), start=(t == 0), stop=(t == 1))
            last.then_inc(nb_ready, 1)
            pe.wait_ge(nb_ready, 2)
            mm(bank[1][0:E, 0:1], const("tri_le", 0, E, E), nb_col[0:E, :], start=True, stop=True)\
                .then_inc(cum_ready, 1)
            pe.wait_ge(past_ready, 1)
            width = MAX_BLOCKS + 1
            mm(bank[0][0:1, 0:width], const("ones", 0, 1, E), past[0:E, :], start=True, stop=False, **kw)
            mm(bank[0][0:1, width:2 * width], nb_col[0:E, :], past[0:E, :], start=False, stop=False, **kw)
            mm(bank[0][0:1, 2 * width:2 * width + 1], nb_col[0:E, :], const("ones", 0, 1, E),
               start=False, stop=True, **kw).then_inc(table_sums, 1)

            pe.wait_ge(nat_out, 4)
            halves = [(j, (0, 64 * j), slice(64 * j, 64 * j + 64)) for j in range(2)]
            loaded = [16 * ROUNDS if s < RING else 0 for s in range(SLOTS)]

            def gather(n, to=bank[0]):
                pe.wait_ge(m_S, n)
                for t in range(2):
                    for j, pos, pr in halves:
                        last = mm(to[pr, :], S[:, t, :], h2n[:, t, 512 * j:512 * j + 512],
                                  start=(t == 0), stop=(t == 1), tile_position=pos)
                last.then_inc(m_gath, 1)

            def turn_rows():
                for c in range(4):
                    last = nc.tensor.transpose(bank[1][:, c * P:c * P + P], xg[:, c * P:c * P + P], const("ident"))
                return last

            def first(e, ks):
                for k in ks:
                    pe.wait_ge(slot_in[k], e * 16 + (loaded[k] + 16))
                    for gu in range(2):
                        for j, pos, pr in halves:
                            c0 = gu * D + j * 512
                            last = mm(bank[2 + gu][pr, :], xT[:, k % 4, k // 4, :], ring[:, k, c0:c0 + 512],
                                      start=False, stop=(k == KD - 1), tile_position=pos)
                            if gu == 0 and j == 0:
                                last.then_inc(freed, 1)
                return last

            def back_to_tokens(r, banks=(6, 7)):
                for mp in range(2):
                    for j, _, pr in halves:
                        mt = 2 * r + mp
                        last = mm(bank[banks[j]][:, mp * 256:mp * 256 + 256], ye[pr, mt * P:mt * P + P],
                                  ST[pr, :, :].rearrange("p a b -> p (a b)"),
                                  start=True, stop=True, tile_position=(64 * j, 0))
                last.then_inc(m_comb, 1)

            gather(1, bank[7])
            pe.wait_ge(m_xg, 1)
            turn_rows().then_inc(m_xt, 1)
            pe.wait_ge(bias_in, 16)
            pe.wait_ge(counts_ready, 1)
            n_blocks = pe.value_load(count_i[0:1, E:E + 1], min_val=E, max_val=MAX_BLOCKS)
            with pe.Fori(0, n_blocks) as g:
                e = pe.value_load(block_i[0:1, bass.ds(g, 1)], min_val=0, max_val=E - 1)
                pe.wait_ge(m_oh1, g + 1)
                for gu in range(2):
                    for j, pos, pr in halves:
                        c0 = gu * D + j * 512
                        mm(bank[2 + gu][pr, :], onehot1[0:E, :], b_all[0:E, c0:c0 + 512],
                           start=True, stop=False, tile_position=pos)
                pe.wait_ge(m_xts, g + 1)
                first(e, range(0, 4))
                pe.wait_ge(m_ys, g + 1)
                pe.wait_ge(m_sts, g + 1)
                pe.wait_ge(m_acc, g * 2 + 1)
                back_to_tokens(0)
                first(e, range(4, KD)).then_inc(m_hc, 1)
                pe.wait_ge(m_acc, g * 2 + 2)
                back_to_tokens(1)
                gather(g + 2)
                pe.wait_ge(m_hm, g + 1)
                for c in range(4):
                    last = nc.tensor.transpose(bank[4][:, c * P:c * P + P], gl[:, c * P:c * P + P],
                                               const("ident"))
                last.then_inc(m_hmt, 1)
                pe.wait_ge(m_xg, g + 2)
                turn_rows()
                pe.wait_ge(m_SG, g + 1)
                for t in range(2):
                    last = nc.tensor.transpose(bank[0][:, t * P:t * P + P],
                                               SG[:, t, :, :].rearrange("p a b -> p (a b)"), const("ident"))
                last.then_inc(m_xt, 1)
                for j, pos, pr in halves:
                    mm(bank[5][pr, :], onehot2[0:E, :], b_all[0:E, 2 * D + 512 * j:2 * D + 512 * j + 512],
                       start=True, stop=False, tile_position=pos)
                pe.wait_ge(m_hms, g + 1)
                for k in range(KD):
                    s = 8 + k // 2
                    if k % 2 == 0:
                        pe.wait_ge(slot_in[s], e * 16 + (loaded[s] + 16))
                    for j, pos, pr in halves:
                        c0 = (k % 2) * D + j * 512
                        last = mm(bank[5][pr, :], hmT[:, k % 4, k // 4, :], ring[:, s, c0:c0 + 512],
                                  start=False, stop=(k == KD - 1), tile_position=pos)
                        if k % 2 == 0 and j == 0:
                            last.then_inc(freed, 1)
                last.then_inc(m_y, 1)
            pe.wait_ge(m_ys, n_blocks + 1)
            pe.wait_ge(m_sts, n_blocks + 1)
            pe.wait_ge(m_acc, n_blocks * 2 + 1)
            back_to_tokens(0)
            back_to_tokens(1, LAST_BANKS)
            norm_sum("final", KD, SEQ)

        @block.scalar
        def _(act):
            A = nc.scalar.activation
            act.dma_start(cst[:, 0:NFIRST], const_in[:, 0:NFIRST]).then_inc(const_sem, 16)
            seen = [0]

            def link(ins):
                seen[0] += 1
                ins.then_inc(act_chain, 1)
                act.wait_ge(act_chain, seen[0])

            tables = [None]

            def use(which):
                if tables[0] != which:
                    tables[0] = which
                    if isinstance(which, str):
                        act.preload_act_table_set(which)
                    else:
                        act.preload_act_table(which)

            def squares(n, tiles, src, after=None, first=0):
                for m in range(tiles):
                    if after is not None:
                        act.wait_ge(after, m + 1)
                    s = src(m)
                    A(sq[:, first + m, 0:s.shape[1]], s, ACT.Square).then_inc(n_sq, 1)

            def root(n, width, mean, eps, ps=None):
                use("natural_log_exp_and_others")
                act.wait_ge(n_sum, AT[n_sum][n] + 1)
                ps = bank[7] if ps is None else ps
                link(A(rtmp[:, 0:width], ps[:, 0:width], ACT.Ln, scale=1.0 / mean, bias=const(eps)))
                A(rstd[:, 0:width], rtmp[:, 0:width], ACT.Exp, scale=-0.5).then_inc(n_rs, 1)

            def split_piece(p, it=None):
                n = 0 if it is None else it
                act.wait_ge(slot_in[p % RING], 16 * n + 16 * loads_of(p))
                if last_user(p) is not None:
                    act.wait_ge(freed, n * RING + (RING - 1 + last_user(p) + 2))
                A(w_hi[:, BUF[p], :], ring[:, p % RING, :], ACT.Copy).then_inc(w_high, 1)

            def split_input(n, x, width, lo=0):
                for m in range(KD):
                    act.wait_ge(n_out, AT[n_out][n] + m + 1)
                    A(x_hi[:, m, lo:lo + width], x[:, m, 0:width], ACT.Copy).then_inc(x_high, 1)

            def shifted(n, shift, to, x, done):
                for m in range(KD):
                    act.wait_ge(n_out, AT[n_out][n] + m + 1)
                    A(to(m), x[:, m, 0:SEQ], ACT.Identity, bias=mod[:, shift + m:shift + m + 1]).then_inc(done, 1)

            def ffn(f, at, w):
                base = f * NF

                def step(j, ready, it=None):
                    split_piece(at + j + 2, it)
                    act.wait_ge(up_ready, ready)
                    A(sig[:, j % 2, 0:w], bank[(j % 2) * 2][:, 0:w], ACT.Silu).then_inc(exp_ready, 1)

                with act.Fori(0, NF // RING) as it:
                    for j in range(RING):
                        step(j, it * RING + (base + j + 1), it)
                for j in range(NF // RING * RING, NF):
                    step(j, base + j + 1)
                m = 0
                for i in range(NF, FFN_PIECES):
                    split_piece(at + i + 2)
                    while m < KD and (m + 1) * NF <= (i - NF + 1) * BLK:
                        act.wait_ge(down_ready, f * KD + m + 1)
                        b = bank[4 + m % 2][:, 0:w]
                        A(sq[:, m, 0:w], b, ACT.Square).then_inc(n_sq, 1)
                        A(nrm[:, m, 0:w], b, ACT.Copy).then_inc(down_out, 1)
                        m += 1

            act.wait_ge(x_in, 16)
            squares("f1_pre", KD, lambda m: res[:, m, :])
            use("natural_log_exp_and_others")
            split_piece(FFN1_AT)
            act.wait_ge(const_sem, 16)
            root("f1_pre", TOK, D, "eps1")
            split_input("f1_pre", x_all, TOK)
            split_piece(FFN1_AT + 1)
            use(ACT.Silu)
            act.wait_ge(c_sem, 16)
            A(c_all, c_all, ACT.Silu).then_inc(c_silu, 1)
            ffn(0, FFN1_AT, TOK)
            root("f1_post", TOK, D, "eps1")
            squares("mix_pre", KD, lambda m: res[:, m, :], updated["f1"])
            root("mix_pre", TOK, D, "eps1")
            split_input("mix_pre", x_mix1, TOK)

            act.wait_ge(const_rest, 16)

            def two_ahead(i, at, last):
                if i % 2 == 0 and at + i // 2 + 2 <= last:
                    split_piece(at + i // 2 + 2)

            for i in range(7):
                two_ahead(i, MIX1_AT, MIX1_AT + MIX1_PROJ - 1)
                act.wait_ge(proj, AT[proj]["lat"] + i + 1)
                A(lat[:, i, :], bank[i % 2][:, 0:TOK], ACT.Copy).then_inc(evac["lat"], 1)
            act.wait_ge(evac["lat"], 5)
            for i in range(8):
                two_ahead(7 + i, MIX1_AT, MIX1_AT + MIX1_PROJ - 1)
                act.wait_ge(proj, AT[proj]["qk"] + i + 1)
                if i < 4:
                    A(sb_q[:, i, :], bank[2 + i % 2][:, 0:SEQ], ACT.Copy, scale=0.125).then_inc(evac["qk"], 1)
                else:
                    A(sb_k[:, i - 4, :], bank[2 + i % 2][:, 0:TOK], ACT.Copy).then_inc(evac["qk"], 1)
                if i == 2:
                    for m in range(5):
                        lo = META if m < 3 else 0
                        A(lat_sq[:, m, 0:TOK - lo], lat[:, m, lo:TOK], ACT.Square).then_inc(n_sq, 1)
            split_piece(MIX1_GATES[0])
            root("cq", SEQ, 384, "eps1")
            act.wait_ge(n_out, AT[n_out]["cq"] + 3)
            root("ckv", TOK, 256, "eps1", bank[0])
            act.wait_ge(proj, AT[proj]["v"] + 1)
            for t, n in enumerate((P, P, META)):
                A(sb_v[0:n, t, :], bank[4 + t][0:n, :], ACT.Copy).then_inc(evac["v"], 1)
            for i in range(8):
                act.wait_ge(proj, AT[proj]["uq"] + i + 1)
                A(uq[:, i, :], bank[2 + i % 2][:, 0:SEQ], ACT.Copy).then_inc(evac["uq"], 1)
            split_piece(MIX1_GATES[1])
            for i in range(4):
                act.wait_ge(proj, AT[proj]["ukv"] + i + 1)
                A(kn[:, i, :], bank[i % 2][:, 0:TOK], ACT.Copy).then_inc(evac["ukv"], 1)
            act.wait_ge(proj, AT[proj]["ukv"] + 5)
            for t, n in enumerate((P, P, META)):
                A(v2[0:n, t, :], bank[4 + t][0:n, :], ACT.Copy).then_inc(evac["ukv"], 1)

            def gate_evac(i, which):
                act.wait_ge(proj, AT[proj][which] + i + 1)
                if which == "gates":
                    A(graw[:, i, :], bank[6 + i % 2][:, 0:SEQ], ACT.Identity,
                      bias=vec("b_gate", i)).then_inc(evac[which], 1)
                else:
                    A(graw2[:, i, :], bank[6 + i % 2][:, 0:SEQ], ACT.Copy).then_inc(evac[which], 1)

            def open_gates(which, gr, tiles=range(KD)):
                use(ACT.Sigmoid)
                act.wait_ge(evac[which], 16)
                for m in tiles:
                    A(gr[:, m, :], gr[:, m, :], ACT.Sigmoid)
                    A(gr[:, 8 + m, :], gr[:, 8 + m, :], ACT.Sigmoid).then_inc(gates_ready, 1)

            def softplus_part(h):
                act.wait_ge(z_ready, h + 1)
                X, Y, e_ = bank[h % 2], bank[2 + h % 2], t_e[:, h % 2, :]
                A(e_[:, 0:384], X[:, 0:384], ACT.Abs)
                link(A(e_[0:META, 384:640], Y[0:META, 0:256], ACT.Abs))
                for func, kw in ((ACT.Exp, dict(scale=-1.0)), (ACT.Ln, dict(bias=const("one")))):
                    A(e_[:, 0:384], e_[:, 0:384], func, **kw)
                    kw = dict(kw, bias=const("one", rows=META)) if "bias" in kw else kw
                    last = A(e_[0:META, 384:640], e_[0:META, 384:640], func, **kw)
                    if func == ACT.Exp:
                        link(last)
                last.then_inc(e_done, 1)

            def attend_exp(h):
                act.wait_ge(la_ready, h + 1)
                act.wait_ge(cap_done, h + 1)
                if h >= 2:
                    act.wait_ge(av_done, h - 1)
                X, Y, e_, t = bank[h % 2], bank[2 + h % 2], t_e[:, h % 2, :], t_a[:, h % 2, :]
                A(t[:, 128:256], X[:, 128:256], ACT.Exp)
                A(t[0:META, 384:640], Y[0:META, 0:256], ACT.Exp)
                A(t[:, 0:128], e_[:, 0:128], ACT.Exp)
                A(t[:, 256:384], e_[:, 256:384], ACT.Exp).then_inc(at_done, 1)

            def y_evac(h, dst, ready, done, upper=None):
                if h >= 0 and h % 2:
                    act.wait_ge(ready, h + 1)
                    m = h // 2
                    last = A(dst[:, m, :], bank[4 + m % 2][:, 0:SEQ], ACT.Copy)
                    if upper is not None:
                        last = A(upper[:, 4 + m, :], bank[4 + m % 2][:, 0:SEQ], ACT.Copy)
                    last.then_inc(done, 1)

            def split_gates(i):
                if i % 2 == 0 and 2 <= i <= 12:
                    split_piece(MIX1_GATES[i // 2 + 1])

            softplus_part(0)
            for h in range(HEADS):
                if h + 1 < HEADS:
                    softplus_part(h + 1)
                split_gates(h)
                gate_evac(h, "gates")
                attend_exp(h)
                y_evac(h - 1, y_sb, av_done, y_out)
            y_evac(HEADS - 1, y_sb, av_done, y_out)

            def soft_exp(kind, h, p, split):
                s = soft[kind]
                act.wait_ge(s["maxed"], h + 1)
                pp, i = p[:, h % 2, :], h % 2
                A(pp[:, 0:split], pp[:, 0:split], ACT.Exp, bias=smx[:, i, 0:1], accum_out=ssum[:, i, 0:1])
                A(pp[:, split:], pp[:, split:], ACT.Exp, bias=smx[:, i, 1:2],
                  accum_out=ssum[:, i, 1:2]).then_inc(s["exped"], 1)

            soft_exp("mla", 0, p_sb, 144)
            for h in range(HEADS):
                if h + 1 < HEADS:
                    soft_exp("mla", h + 1, p_sb, 144)
                split_gates(8 + h)
                gate_evac(8 + h, "gates")
                act.wait_ge(soft["mla"]["pt"], h + 1)
                if h >= 2:
                    act.wait_ge(soft["mla"]["pv"], h - 1)
                A(pt_sb[0:META, h % 2, 384:640], bank[3][0:META, 0:256], ACT.Copy)\
                    .then_inc(soft["mla"]["pt_a"], 1)
                y_evac(h - 1, y_mla, soft["mla"]["pv"], soft["mla"]["y"])
            y_evac(HEADS - 1, y_mla, soft["mla"]["pv"], soft["mla"]["y"])
            open_gates("gates", graw)
            for m in range(KD):
                if m in (4, 6):
                    split_piece(FFN2_AT + (m - 4) // 2)
                act.wait_ge(proj, AT[proj]["w1"] + m + 1)
                b = bank[4 + m % 2][:, 0:SEQ]
                A(sq[:, m, 0:SEQ], b, ACT.Square).then_inc(n_sq, 1)
                A(mix_o[:, m, :], b, ACT.Copy).then_inc(evac["w1"], 1)
            root("mix_post", SEQ, D, "eps1")
            squares("f2_pre", KD, lambda m: real(res[:, m, :]), updated["m1"])
            root("f2_pre", SEQ, D, "eps1")
            split_input("f2_pre", x_all, SEQ, META)
            use(ACT.Silu)
            ffn(1, FFN2_AT, SEQ)
            root("f2_post", SEQ, D, "eps1")

            squares("n1", KD, lambda m: real(res[:, m, :]), updated["f2"])
            root("n1", SEQ, D, "eps2")
            shifted("n1", 0, lambda m: x_hi[:, m, 0:SEQ], x_mix2, x_high)
            for m in range(KD):
                act.wait_ge(x_split, AT[x_split]["n1"] + m + 1)
                A(x_mix2[:, m, 0:SEQ], x_mix2[:, m, 0:SEQ], ACT.Identity, bias=mod[:, m:m + 1])\
                    .then_inc(x_whole, 1)
            use(ACT.Sigmoid)
            for m in range(CT):
                split_piece(MIX2_AT + m + 2)
                act.wait_ge(proj, AT[proj]["conv"] + m + 1)
                if m >= 2:
                    act.wait_ge(evac["conv"], m - 1)
                A(csg[:, m % 2, :], bank[2 * (m % 2) + 1][:, 0:SEQ], ACT.Sigmoid).then_inc(conv_sig, 1)
            use("natural_log_exp_and_others")
            act.wait_ge(proj, AT[proj]["f"] + 1)
            link(A(lf[0:8, :], bank[6][0:8, 0:SEQ], ACT.Identity, bias=vec("b_forget", rows=8)))
            link(A(lft[0:8, :], lf[0:8, :], ACT.Abs))
            link(A(lft[0:8, :], lft[0:8, :], ACT.Exp, scale=-1.0))
            A(lft[0:8, :], lft[0:8, :], ACT.Ln, bias=const("one", rows=8)).then_inc(evac["f"], 1)
            for i in range(8):
                two_ahead(i, MIX2_AT + CT, DENSE)
                act.wait_ge(proj, AT[proj]["qk2"] + i + 1)
                b = bank[4 + i % 2][:, 0:SEQ]
                if i < 4:
                    A(q2[:, i, :], b, ACT.Copy, scale=0.125).then_inc(evac["qk2"], 1)
                else:
                    A(k2[:, i - 4, :], b, ACT.Copy).then_inc(evac["qk2"], 1)
            for p in range(2):
                split_piece(MIX2_AT + CT + 6 + p)
            act.wait_ge(proj, AT[proj]["v2"] + 1)
            for t in range(2):
                A(w2v[:, t, :], bank[t][:, :], ACT.Copy).then_inc(evac["v2"], 1)
            act.wait_ge(logf_t, 1)
            A(lfn[:, :, :].rearrange("p a b -> p (a b)"), bank[2][:, 0:16], ACT.Copy).then_inc(logf_n, 1)
            act.wait_ge(f_sums, 1)
            A(fcum[:, :, :].rearrange("p a b -> p (a b)"), bank[3][:, 0:16], ACT.Copy).then_inc(f_out, 1)
            A(neg_f[0:8, :], bank[2][0:8, 256:512], ACT.Copy, scale=-1.0).then_inc(f_out, 1)
            soft_exp("fa", 0, p2, P)
            for h in range(HEADS):
                if h + 1 < HEADS:
                    soft_exp("fa", h + 1, p2, P)
                gate_evac(2 * h, "gates2")
                gate_evac(2 * h + 1, "gates2")
                act.wait_ge(soft["fa"]["pt"], h + 1)
                if h >= 2:
                    act.wait_ge(soft["fa"]["pv"], h - 1)
                A(pt2[:, h % 2, :], bank[2][:, 0:384], ACT.Copy).then_inc(soft["fa"]["pt_v"], 1)
                split_piece(MIX2_AT + CT + 6 + h + 2)
                y_evac(h - 1, y2, soft["fa"]["pv"], soft["fa"]["y"], o_hi)
            y_evac(HEADS - 1, y2, soft["fa"]["pv"], soft["fa"]["y"], o_hi)
            squares("ln_var", CT, lambda m: cv[:, m, :], ln_in)
            root("ln_var", SEQ, 512, "eps2")
            use(ACT.Sigmoid)
            for m in range(CT):
                act.wait_ge(n_out, AT[n_out]["ln_var"] + m + 1)
                A(conv_s[:, m, :], cv[:, m, :], ACT.Sigmoid).then_inc(ln_sigmoid, 1)
            for m in range(CT):
                act.wait_ge(conv_out, m + 1)
                A(o_hi[:, m, :], cv[:, m, :], ACT.Copy).then_inc(o_high, 1)
            at_piece = MIX2_AT + CT + 6 + HEADS
            open_gates("gates2", graw2, range(0, 3))
            split_piece(at_piece + 2)
            open_gates("gates2", graw2, range(3, KD))
            use("natural_log_exp_and_others")
            for m in range(KD):
                if m % 2 == 0 and m:
                    split_piece(at_piece + m // 2 + 2)
                act.wait_ge(evac["o2"], m + 1)
                A(x_hi[:, m, 0:SEQ], x_out2[:, m, :], ACT.Copy).then_inc(x_high, 1)
            for m in range(KD):
                if m in (0, 2):
                    split_piece(at_piece + 6 + m // 2)
                act.wait_ge(evac["w2"], m + 1)
                A(sq_n2[:, m, :], real(res[:, m, :]), ACT.Square).then_inc(n_sq, 1)
            root("n2", SEQ, D, "eps2")
            shifted("n2", 24, lambda m: nrm[:, m, 0:SEQ], nrm, x_whole)
            act.dma_start(b_all[0:E, :], b_exp).then_inc(bias_in, 16)
            act.wait_ge(top_max, 1)
            for t in range(2):
                A(tope[:, t, 0:TOPK], top[:, t, 0:TOPK], ACT.Exp, bias=tops[:, t, 0:1],
                  accum_out=tops[:, t, 1:2]).then_inc(top_exp, 1)
            act.wait_ge(nat, 1)
            for t in range(2):
                for c in range(2):
                    A(h2n[:, t, c * 512:c * 512 + 512], bank[2 + 2 * t + c][:, :], ACT.Copy)\
                        .then_inc(nat_out, 1)

            use(ACT.Sigmoid)
            act.wait_ge(m_gath, 1)
            A(xg, bank[7][:, :], ACT.Copy).then_inc(m_xg, 1)
            act.wait_ge(counts_ready, 1)
            n_blocks = act.value_load(count_i[0:1, E:E + 1], min_val=E, max_val=MAX_BLOCKS)
            with act.Fori(0, n_blocks) as g:
                act.wait_ge(m_gl, g + 1)
                A(eg, gl, ACT.Sigmoid, scale=1.702).then_inc(m_eg, 1)
                act.wait_ge(m_gath, g + 2)
                act.wait_ge(m_xt, g + 1)
                A(xg, bank[0][:, :], ACT.Copy).then_inc(m_xg, 1)
                act.wait_ge(m_hmt, g + 1)
                A(hmT[:, :, :, :].rearrange("p a b c -> p (a b c)"), bank[4][:, :], ACT.Copy).then_inc(m_hms, 1)
                act.wait_ge(m_xt, g + 2)
                act.wait_ge(m_comb, g * 2 + 2)
                A(ST[:, :, :].rearrange("p a b -> p (a b)"), bank[0][:, 0:256], ACT.Copy).then_inc(m_sts, 1)
                act.wait_ge(m_y, g + 1)
                A(ye, bank[5][:, :], ACT.Copy).then_inc(m_ys, 1)
            use("natural_log_exp_and_others")
            for n, m in enumerate(FIN_ORDER):
                act.wait_ge(fin_x, n + 1)
                A(sq[:, n, 0:SEQ], fin[:, m, :], ACT.Square).then_inc(n_sq, 1)
            root("final", SEQ, D, "eps2")

        @block.gpsimd
        def _(pool):
            def rest(p, n):
                pool.wait_ge(w_high, n)
                nc.gpsimd.tensor_tensor(w_lo[:, BUF[p], :], ring[:, p % RING, :], w_hi[:, BUF[p], :].bitcast(f32),
                                        ALU.subtract).then_inc(w_split, 1)

            for at, mixer in ((FFN1_AT, range(MIX1_AT, FFN2_AT)), (FFN2_AT, range(MIX2_AT, DENSE))):
                whole = FFN_PIECES // RING
                with pool.Fori(0, whole) as it:
                    for i in range(RING):
                        rest(at + i, it * RING + (ORDER[at] + i + 1))
                for p in [*range(at + whole * RING, at + FFN_PIECES), *mixer]:
                    if p in ORDER:
                        rest(p, ORDER[p] + 1)

        @block.vector
        def _(dve):
            V = nc.vector
            seen = [0]

            def link(ins, *waits):
                seen[0] += 1
                ins.then_inc(dve_chain, 1)
                dve.wait_ge(dve_chain, seen[0])

            def mark(ins):
                seen[0] += 1
                ins.then_inc(dve_chain, 1)

            def settle():
                dve.wait_ge(dve_chain, seen[0])

            def stt(out_, in0, scalar, in1, op0, op1):
                return V.scalar_tensor_tensor(out=out_, in0=in0, scalar=scalar, in1=in1, op0=op0, op1=op1)

            def ts(out_, in0, s1, s2, op0, op1=None):
                if op1 is None:
                    return V.tensor_scalar(out_, in0, s1, None, op0)
                return V.tensor_scalar(out_, in0, s1, s2, op0, op1)

            tt = V.tensor_tensor

            dve.sem_inc(freed, RING - 1)
            dve.sem_inc(hid_ready, 2)
            dve.sem_inc(down_out, 2)
            for s in (ada_used, ada_copied, hid_split, m_acc):
                dve.sem_inc(s, 1)
            dve.wait_ge(cols_sem, 16)
            mark(ts(half_f1, vec("f1_post", 0, 8), 0.5, None, ALU.mult))
            mark(ts(half_f2, vec("f2_post", 0, 8), 0.5, None, ALU.mult))

            def normed(n, tiles, src, gain, dst, then=lambda m: None):
                dve.wait_ge(n_rs, AT[n_rs][n] + 1)
                for m in range(tiles):
                    s = src(m)
                    stt(dst(m), s, gain(m), rstd[:, 0:s.shape[1]], ALU.mult, ALU.mult).then_inc(n_out, 1)
                    if m:
                        then(m - 1)
                then(tiles - 1)

            def residual(n, src, gain, into, upd):
                dve.wait_ge(n_rs, AT[n_rs][n] + 1)
                at = seen[0]

                def add(m):
                    dve.wait_ge(dve_chain, at + m + 1)
                    tt(into(m), into(m), src(m), ALU.add).then_inc(upd, 1)

                for m in range(KD):
                    s = src(m)
                    mark(stt(s, s, gain(m), rstd[:, 0:s.shape[1]], ALU.mult, ALU.mult))
                    if m:
                        add(m - 1)
                add(KD - 1)

            def lower(n, x, width, lo=0):
                def of(m):
                    dve.wait_ge(x_high, AT[x_split][n] + m + 1)
                    tt(x_lo[:, m, lo:lo + width], x[:, m, 0:width], x_hi[:, m, lo:lo + width].bitcast(f32),
                       ALU.subtract).then_inc(x_split, 1)
                return of

            normed("f1_pre", KD, lambda m: res[:, m, :], lambda m: vec("f1_pre", m), lambda m: x_all[:, m, :],
                   lower("f1_pre", x_all, TOK))
            dve.wait_ge(c_silu, 1)

            def ada_tile(i, n, w, to):
                dve.wait_ge(ada_in[i], w)
                dve.wait_ge(ada_used, n + 1)
                V.tensor_tensor_reduce(out=ada_t, in0=ada_w[:, i, :], in1=c_all, scale=1.0, scalar=0.0,
                                       op0=ALU.mult, op1=ALU.add,
                                       accum_out=to).then_inc(ada_used, 1)

            def ffn(f, w):
                base = f * NF

                def hidden(j, n, at):
                    i = j % 2
                    dve.wait_ge(exp_ready, n)
                    dve.wait_ge(hid_split, n)
                    tt(hid[:, 0:w], sig[:, i, 0:w], bank[2 * i + 1][:, 0:w], ALU.mult).then_inc(hid_ready, 1)
                    dve.wait_ge(hid_ready, n + 2)
                    hi, lo = hid_hi[:, at, 0:w], hid_lo[:, at, 0:w]
                    if not isinstance(at, int):
                        hi, lo = (v.rearrange("p o t -> p (o t)") for v in (hi, lo))
                    V.tensor_copy(hi, hid[:, 0:w]).then_inc(hid_high, 1)
                    dve.wait_ge(hid_high, n)
                    tt(lo, hid[:, 0:w], hi.bitcast(f32), ALU.subtract).then_inc(hid_split, 1)

                with dve.Fori(0, NF // 2) as it:
                    if f == 0:
                        dve.wait_ge(ada_copied, it + 1)
                    for j in range(2):
                        hidden(j, it * 2 + (base + j + 1), bass.ds(it * 2 + j, 1))
                        if f == 0:
                            for i in range(2):
                                ada_tile(i, it * 4 + (2 * j + i), it * 32 + 16 * (j + 1),
                                         ada_acc[:, 2 * j + i:2 * j + i + 1])
                    if f == 0:
                        dve.wait_ge(ada_used, it * 4 + 5)
                        V.tensor_copy(mod[:, bass.ds(it * 4, 4)], ada_acc).then_inc(ada_copied, 1)

            ffn(0, TOK)
            for n in range(2 * NF, 48):
                ada_tile(n % 2, n, 16 * (n // 2 + 1), mod[:, n:n + 1])
            dve.wait_ge(ada_copied, NF // 2 + 1)
            dve.wait_ge(ada_used, 49)
            link(tt(mod, mod, vec("b_ada", 0, 48), ALU.add))
            link(ts(g1s, mod[:, 8:16], 1.0, None, ALU.add))
            link(ts(g2s, mod[:, 32:40], 1.0, None, ALU.add))
            mark(tt(g1s, g1s, vec("n1_g", 0, 8), ALU.mult))
            mark(tt(g2s, g2s, vec("n2_g", 0, 8), ALU.mult))
            residual("f1_post", lambda m: nrm[:, m, :], lambda m: half_f1[:, m:m + 1], lambda m: res[:, m, :],
                     updated["f1"])
            dve.wait_ge(updated["f1"], KD)
            normed("mix_pre", KD, lambda m: res[:, m, :], lambda m: vec("mix_pre", m), lambda m: x_mix1[:, m, :],
                   lower("mix_pre", x_mix1, TOK))
            normed("cq", 3, lambda m: lat[:, m, META:TOK], lambda m: vec("q_g", m), lambda m: lat[:, m, META:TOK])
            normed("ckv", 2, lambda m: lat[:, 3 + m, :], lambda m: vec("kv_g", m), lambda m: lat[:, 3 + m, :])
            dve.wait_ge(const_rest, 16)
            mark(tt(lat[:, 5, :], lat[:, 5, :], const("cos"), ALU.mult))
            mark(tt(lat[:, 6, :], lat[:, 6, :], const("sin"), ALU.mult))
            settle()
            tt(lat[:, 5, :], lat[:, 5, :], lat[:, 6, :], ALU.add).then_inc(roped, 1)
            dve.wait_ge(evac["uq"], 8)
            for m in range(2):
                mark(tt(uq[:, 4 + m, :], uq[:, 4 + m, :], const("cos", META), ALU.mult))
                mark(tt(uq[:, 6 + m, :], uq[:, 6 + m, :], const("sin", META), ALU.mult))
            settle()
            tt(uq[:, 4:6, :], uq[:, 4:6, :], uq[:, 6:8, :], ALU.add).then_inc(roped, 1)

            def softplus(h):
                dve.wait_ge(e_done, h + 1)
                X, Y = bank[h % 2], bank[2 + h % 2]
                e_, s = t_e[:, h % 2, :], t_sp[:, h % 2, :]
                mark(stt(s[:, 0:384], X[:, 0:384], 0.0, e_[:, 0:384], ALU.max, ALU.add))
                mark(stt(s[0:META, 384:640], Y[0:META, 0:256], 0.0, e_[0:META, 384:640], ALU.max, ALU.add))
                settle()
                tt(s[:, 0:128], s[:, 0:128], const("strict"), ALU.mult)
                tt(s[:, 256:384], s[:, 256:384], const("strict"), ALU.mult).then_inc(sp_done, 1)

            def cap_diagonal(h):
                dve.wait_ge(la_ready, h + 1)
                X, e_ = bank[h % 2], t_e[:, h % 2, :]
                tt(e_[:, 0:128], X[:, 0:128], const("cap"), ALU.min)
                tt(e_[:, 256:384], X[:, 256:384], const("cap"), ALU.min).then_inc(cap_done, 1)

            softplus(0)
            for h in range(HEADS):
                if h + 1 < HEADS:
                    softplus(h + 1)
                cap_diagonal(h)

            def soft_norm(kind, h, p, split):
                s = soft[kind]
                dve.wait_ge(s["exped"], h + 1)
                pp, i = p[:, h % 2, :], h % 2
                link(V.reciprocal(srec[:, i, :], ssum[:, i, :]))
                ts(pp[:, 0:split], pp[:, 0:split], srec[:, i, 0:1], None, ALU.mult)
                ts(pp[:, split:], pp[:, split:], srec[:, i, 1:2], None, ALU.mult).then_inc(s["normed"], 1)

            def soft_max(kind, h, p, split):
                pp, i = p[:, h % 2, :], h % 2
                mark(V.reduce_max(smx[:, i, 0:1], pp[:, 0:split], AX.X))
                mark(V.reduce_max(smx[:, i, 1:2], pp[:, split:], AX.X))
                settle()
                ts(smx[:, i, :], smx[:, i, :], -1.0, None, ALU.mult).then_inc(soft[kind]["maxed"], 1)

            def mla_scores(h):
                dve.wait_ge(soft["mla"]["scores"], h + 1)
                if h >= 2:
                    dve.wait_ge(soft["mla"]["pt"], h - 1)
                link(stt(p_sb[:, h % 2, :], bank[h % 2][:, 0:416], MLA_SCALE, const("mla_mask"),
                         ALU.mult, ALU.add))
                soft_max("mla", h, p_sb, 144)

            dve.wait_ge(av_done, HEADS)
            mla_scores(0)
            for h in range(HEADS):
                soft_norm("mla", h, p_sb, 144)
                if h + 1 < HEADS:
                    mla_scores(h + 1)
                dve.wait_ge(soft["mla"]["pt"], h + 1)
                if h >= 2:
                    dve.wait_ge(soft["mla"]["pv"], h - 1)
                V.tensor_copy(pt_sb[:, h % 2, 0:384], bank[2][:, 0:384]).then_inc(soft["mla"]["pt_v"], 1)

            def gated(n, gr, tmp, to, then=lambda m: None):
                for m in range(KD):
                    dve.wait_ge(proj, AT[proj][n] + m + 1)
                    dve.wait_ge(gates_ready, (KD if n == "o2" else 0) + m + 1)
                    if m:
                        dve.wait_ge(evac[n], m)
                    b0 = 2 * (m % 2)
                    mark(tt(tmp[:, 0, :], bank[b0][:, 0:SEQ], gr[:, m, :], ALU.mult))
                    mark(tt(tmp[:, 1, :], bank[b0 + 1][:, 0:SEQ], gr[:, 8 + m, :], ALU.mult))
                    settle()
                    tt(to[:, m, 0:SEQ], tmp[:, 0, :], tmp[:, 1, :], ALU.add).then_inc(evac[n], 1)
                    if m:
                        then(m - 1)
                then(KD - 1)

            gated("o1", graw, mtmp, nrm)
            residual("mix_post", lambda m: mix_o[:, m, :], lambda m: vec("mix_post", m),
                     lambda m: real(res[:, m, :]), updated["m1"])
            dve.wait_ge(updated["m1"], KD)
            normed("f2_pre", KD, lambda m: real(res[:, m, :]), lambda m: vec("f2_pre", m),
                   lambda m: x_all[:, m, 0:SEQ], lower("f2_pre", x_all, SEQ, META))
            ffn(1, SEQ)
            residual("f2_post", lambda m: nrm[:, m, 0:SEQ], lambda m: half_f2[:, m:m + 1],
                     lambda m: real(res[:, m, :]), updated["f2"])
            dve.wait_ge(updated["f2"], KD)

            mark(V.memset(ca[:, :, 0:CONV_K - 1], 0.0))

            def shifted_lower(m):
                dve.wait_ge(x_high, AT[x_split]["n1"] + m + 1)
                stt(x_lo[:, m, 0:SEQ], x_mix2[:, m, :], mod[:, m:m + 1], x_hi[:, m, 0:SEQ].bitcast(f32),
                    ALU.add, ALU.subtract).then_inc(x_split, 1)

            normed("n1", KD, lambda m: real(res[:, m, :]), lambda m: g1s[:, m:m + 1], lambda m: x_mix2[:, m, :],
                   shifted_lower)
            for m in range(CT):
                dve.wait_ge(conv_sig, m + 1)
                tt(ca[:, m, CONV_K - 1:], bank[2 * (m % 2)][:, 0:SEQ], csg[:, m % 2, :], ALU.mult)\
                    .then_inc(evac["conv"], 1)
            dve.wait_ge(evac["f"], 1)
            stt(lf[0:8, :], lf[0:8, :], 0.0, lft[0:8, :], ALU.min, ALU.subtract).then_inc(logf_ready, 1)
            dve.wait_ge(evac["conv"], CT)

            taps = [(m, k) for m in range(CT) for k in range(CONV_K)]

            def conv_taps(n):
                for _ in range(n):
                    if not taps:
                        return
                    m, k = taps.pop(0)
                    w = vec("conv_w", m * CONV_K + k)
                    x = ca[:, m, k:k + SEQ]
                    if k == 0:
                        link(ts(cv[:, m, :], x, w, vec("conv_b", m), ALU.mult, ALU.add))
                    elif k < CONV_K - 1:
                        link(stt(cv[:, m, :], x, w, cv[:, m, :], ALU.mult, ALU.add))
                    else:
                        stt(cv[:, m, :], x, w, cv[:, m, :], ALU.mult, ALU.add).then_inc(conv_done, 1)

            conv_taps(40)

            def fa_scores(h):
                dve.wait_ge(soft["fa"]["scores"], h + 1)
                if h >= 2:
                    dve.wait_ge(soft["fa"]["pt"], h - 1)
                p, b_ = p2[:, h % 2, :], bank[h % 2]
                mark(stt(p[:, 0:P], b_[:, 0:P], fcum[:, 0, h:h + 1], const("causal"), ALU.add, ALU.add))
                mark(ts(p[:, P:256], b_[:, P:256], fcum[:, 1, h:h + 1], None, ALU.add))
                mark(stt(p[:, 256:384], b_[:, 256:384], fcum[:, 1, h:h + 1], const("causal"), ALU.add, ALU.add))
                settle()
                soft_max("fa", h, p2, P)

            fa_scores(0)
            for h in range(HEADS):
                soft_norm("fa", h, p2, P)
                if h + 1 < HEADS:
                    fa_scores(h + 1)
                conv_taps(11)
            conv_taps(len(taps))
            dve.wait_ge(conv_done, CT)
            for m in range(4):
                dve.wait_ge(soft["fa"]["y"], m + 1)
                tt(o_lo[:, 4 + m, :], y2[:, m, :], o_hi[:, 4 + m, :].bitcast(f32), ALU.subtract)\
                    .then_inc(o_split, 1)
            dve.wait_ge(n_sum, AT[n_sum]["ln_mean"] + 1)
            for m in range(CT):
                stt(cv[:, m, :], bank[4][:, 0:SEQ], -1.0 / 512, cv[:, m, :], ALU.mult, ALU.add).then_inc(ln_in, 1)
            dve.wait_ge(n_rs, AT[n_rs]["ln_var"] + 1)
            dve.wait_ge(ln_in, CT)
            at = seen[0]
            for m in range(CT):
                mark(tt(cv[:, m, :], cv[:, m, :], rstd[:, 0:SEQ], ALU.mult))
            for m in range(CT):
                dve.wait_ge(dve_chain, at + m + 1)
                ts(cv[:, m, :], cv[:, m, :], vec("ln_g", m), vec("ln_b", m), ALU.mult, ALU.add)\
                    .then_inc(n_out, 1)
            for m in range(CT):
                dve.wait_ge(ln_sigmoid, m + 1)
                tt(cv[:, m, :], cv[:, m, :], conv_s[:, m, :], ALU.mult).then_inc(conv_out, 1)
            for m in range(CT):
                dve.wait_ge(o_high, m + 1)
                tt(o_lo[:, m, :], cv[:, m, :], o_hi[:, m, :].bitcast(f32), ALU.subtract).then_inc(o_split, 1)
            gated("o2", graw2, mt2, x_out2, lower("w2", x_out2, SEQ))
            for m in range(KD):
                dve.wait_ge(proj, AT[proj]["w2"] + m + 1)
                r = real(res[:, m, :])
                stt(r, bank[4 + m % 2][:, 0:SEQ], mod[:, 16 + m:17 + m], r, ALU.mult, ALU.add)\
                    .then_inc(evac["w2"], 1)
            dve.wait_ge(evac["w2"], KD)
            normed("n2", KD, lambda m: real(res[:, m, :]), lambda m: g2s[:, m:m + 1],
                   lambda m: nrm[:, m, 0:SEQ])

            mark(V.memset(acc, 0.0))
            mark(V.memset(ye, 0.0))
            mark(V.memset(ST, 0.0))
            dve.wait_ge(logits, 1)
            for t in range(2):
                mark(tt(lgt[:, t, :], bank[t][:, 0:E], vec("b_router", 0, E), ALU.add))
            settle()
            for t in range(2):
                mark(V.max(top[:, t, :], lgt[:, t, :]))
            settle()
            for t in range(2):
                mark(V.max_index(idx_u[:, t, :], top[:, t, :], lgt[:, t, :]))
            settle()
            mark(V.tensor_copy(topi[:, :, :], idx_u[:, :, :]))
            for t in range(2):
                last = ts(tops[:, t, 0:1], top[:, t, 0:1], -1.0, None, ALU.mult)
            last.then_inc(top_max, 1)
            settle()
            for t in range(2):
                mark(ts(msk[:, t, :], const("iota", 0, E), topi[:, t, 0:1], None, ALU.is_equal))
            for j in range(1, TOPK):
                settle()
                for t in range(2):
                    last = stt(msk[:, t, :], const("iota", 0, E), topi[:, t, j:j + 1], msk[:, t, :],
                               ALU.is_equal, ALU.add)
                    if j < TOPK - 1:
                        mark(last)
            last.then_inc(masked, 1)
            dve.wait_ge(counted, 1)

            def router_weights():
                dve.wait_ge(top_exp, 2)
                mark(V.reciprocal(tops[:, :, 1:2], tops[:, :, 1:2]))
                settle()
                for t in range(2):
                    mark(ts(tope[:, t, 0:TOPK], tope[:, t, 0:TOPK], tops[:, t, 1:2], None, ALU.mult))
                settle()
                for t in range(2):
                    mark(ts(gate[:, t, :], const("iota", 0, E), topi[:, t, 0:1], tope[:, t, 0:1],
                            ALU.is_equal, ALU.mult))
                for j in range(1, TOPK):
                    settle()
                    dve.wait_ge(masked, 1)
                    for t, tmp in enumerate((ctmp, csum)):
                        mark(ts(tmp, const("iota", 0, E), topi[:, t, j:j + 1], tope[:, t, j:j + 1],
                                ALU.is_equal, ALU.mult))
                    settle()
                    for t, tmp in enumerate((ctmp, csum)):
                        mark(tt(gate[:, t, :], gate[:, t, :], tmp, ALU.add))
                settle()

            for t in range(2):
                mark(stt(slot[:, t, :], bank[6][:, t * E:t * E + E], 1.0, msk[:, t, :], ALU.add, ALU.mult))

            def blocks_of(to, counts):
                settle()
                mark(ts(to, counts, float(SLOT_TOK), 1.0, ALU.is_gt, ALU.add))
                for lim in (2, 3):
                    settle()
                    mark(stt(to, counts, float(lim * SLOT_TOK), to, ALU.is_gt, ALU.add))
                settle()

            blocks_of(ctmp[0:1, :], bank[6][0:1, 2 * E:3 * E])
            mark(V.tensor_copy(count_i[:, 0:E], ctmp[0:1, :]))
            for t in range(2):
                mark(ts(slot[:, t, :], slot[:, t, :], 1.0, None, ALU.subtract))
            dve.wait_ge(nb_ready, 1)
            blocks_of(nb_col[0:E, :], bank[0][0:E, 0:1])
            dve.sem_inc(nb_ready, 1)
            dve.wait_ge(cum_ready, 1)
            link(V.tensor_copy(cum_col[0:E, :], bank[1][0:E, 0:1]))
            ts(past[0:E, :], const("iota", 0, MAX_BLOCKS + 1, E), cum_col[0:E, :], None, ALU.is_ge)\
                .then_inc(past_ready, 1)
            def where(g):
                e_ = dve.value_load(block_i[0:1, bass.ds(g, 1)], min_val=0, max_val=E - 1)
                b_ = dve.value_load(block_i[0:1, bass.ds(g + width, 1)], min_val=0, max_val=3)
                return e_, b_

            def slots(b_):
                return cst[:, bass.ds(b_ * SLOT_TOK + CONST["iota"][0], SLOT_TOK)]

            def select(e_, b_):
                for t in range(2):
                    last = V.tensor_scalar(S[:, t, :], slots(b_), slot[:, t, bass.ds(e_, 1)], None, ALU.is_equal)
                return last

            def one_hot(to, e_):
                return V.tensor_scalar(to[0:E, :], const("ones", 0, SLOT_TOK, E),
                                       cst[0:E, bass.ds(e_ + CONST["ident"][0], 1)], None, ALU.mult)

            def add_up(r, banks=(6, 7)):
                for j in range(2):
                    a_ = acc[:, 4 * j + 2 * r:4 * j + 2 * r + 2, :]
                    last = tt(a_, a_, bank[banks[j]][:, :].rearrange("p (a b) -> p a b", a=2), ALU.add)
                last.then_inc(m_acc, 1)

            for t in range(2):
                last = V.tensor_scalar(S[:, t, :], const("iota", 0, SLOT_TOK), slot[:, t, 0:1], None, ALU.is_equal)
            last.then_inc(m_S, 1)
            V.tensor_scalar(onehot1[0:E, :], const("ones", 0, SLOT_TOK, E), const("ident", 0, 1, E), None,
                            ALU.mult).then_inc(m_oh1, 1)
            width = MAX_BLOCKS + 1
            dve.wait_ge(table_sums, 1)
            link(tt(table[0:1, 1, :], const("iota", 0, width, 1), bank[0][0:1, width:2 * width], ALU.subtract))
            link(ts(table[0:1, 1, :], table[0:1, 1, :], 3.0, None, ALU.min))
            link(ts(table[0:1, 0, :], bank[0][0:1, 0:width], float(E - 1), None, ALU.min))
            link(V.tensor_copy(block_i[:, :], table[0:1, :, :].rearrange("p a b -> p (a b)")))
            link(V.tensor_copy(count_i[:, E:E + 1], bank[0][0:1, 2 * width:2 * width + 1]))
            dve.sem_inc(m_ys, 1)
            dve.sem_inc(m_sts, 1)
            dve.sem_inc(counts_ready, 1)
            n_blocks = dve.value_load(count_i[0:1, E:E + 1], min_val=E, max_val=MAX_BLOCKS)
            dve.wait_ge(m_xt, 1)
            V.tensor_copy(xT[:, :, :, :].rearrange("p a b c -> p (a b c)"), bank[1][:, :]).then_inc(m_xts, 1)
            router_weights()
            with dve.Fori(0, n_blocks) as g:
                e, b = where(g)
                e_next, b_next = where(g + 1)
                select(e_next, b_next).then_inc(m_S, 1)
                for t in range(2):
                    place, weight = slot[:, t, bass.ds(e, 1)], gate[:, t, bass.ds(e, 1)]
                    for i in range(2):
                        V.tensor_scalar(SG[:, t, i, :], slots(b), place, weight, ALU.is_equal, ALU.mult)
                dve.wait_ge(m_comb, g * 2 + 1)
                one_hot(onehot2, e).then_inc(m_SG, 1)
                dve.wait_ge(m_acc, g * 2 + 1)
                add_up(0)
                dve.wait_ge(m_hc, g + 1)
                ts(gl, bank[2][:, :], 7.0, None, ALU.min).then_inc(m_gl, 1)
                ts(ul, bank[3][:, :], 7.0, -7.0, ALU.min, ALU.max).then_inc(moe_dve, 1)
                dve.wait_ge(m_gl, g + 1)
                dve.wait_ge(moe_dve, g * 2 + 1)
                stt(ul, ul, 1.0, gl, ALU.add, ALU.mult).then_inc(moe_dve, 1)
                dve.wait_ge(m_eg, g + 1)
                dve.wait_ge(moe_dve, g * 2 + 2)
                tt(gl, ul, eg, ALU.mult).then_inc(m_hm, 1)
                one_hot(onehot1, e_next).then_inc(m_oh1, 1)
                dve.wait_ge(m_comb, g * 2 + 2)
                add_up(1)
                dve.wait_ge(m_xt, g + 2)
                V.tensor_copy(xT[:, :, :, :].rearrange("p a b c -> p (a b c)"), bank[1][:, :]).then_inc(m_xts, 1)
            for r in range(2):
                dve.wait_ge(m_comb, n_blocks * 2 + (r + 1))
                dve.wait_ge(m_acc, n_blocks * 2 + (r + 1))
                add_up(r, LAST_BANKS if r else (6, 7))
                dve.wait_ge(m_acc, n_blocks * 2 + (r + 2))
                for m in FIN_ORDER[4 * r:4 * r + 4]:
                    stt(fin[:, m, :], acc[:, m, :], mod[:, 40 + m:41 + m], real(res[:, m, :]),
                        ALU.mult, ALU.add).then_inc(fin_x, 1)
            dve.wait_ge(n_rs, AT[n_rs]["final"] + 1)
            dve.wait_ge(fin_x, KD)
            for m in range(KD):
                stt(fin[:, m, :], fin[:, m, :], vec("final_g", m), rstd[:, 0:SEQ], ALU.mult, ALU.mult)\
                    .then_inc(fin_ready, 1)


def block_stream(mats):
    parts = []
    for w, kind in mats:
        k, n = w.shape
        if kind == "tiles":
            parts.append(w.reshape(k // P, P, n // P, P).transpose(1, 2, 0, 3).reshape(P, -1))
        else:
            parts.append(w.reshape(k // P, P, n).transpose(1, 0, 2).reshape(P, -1))
    s = np.concatenate(parts, axis=1)
    return s.reshape(P, -1, PIECE).transpose(1, 0, 2)


def interleave(a, b):
    k = a.shape[0]
    return np.stack([a.reshape(k, -1, P), b.reshape(k, -1, P)], axis=2).reshape(k, -1)


def column(v):
    return np.asarray(v).reshape(-1, P).T


def kernel(**inputs):
    from concourse import bacc
    from concourse.bass_utils import run_bass_kernel_spmd

    x = {k: np.asarray(v) for k, v in inputs.items()}
    w_in = x["w_in"][0]
    at = np.cumsum([0, 512, 512, 512, 384, 256, 32, 2048])
    sq_, sk_, sv_, cq_, ckv_, kr_, gt_ = [w_in[:, at[i]:at[i + 1]] for i in range(7)]

    def swap(w):
        return np.concatenate([w[..., 16:], w[..., :16]], axis=-1)

    uq = x["w_uq"][0]
    ukv = x["w_ukv"][0]
    krs = np.tile(kr_, (1, 4)), np.tile(swap(kr_), (1, 4))
    mix1 = block_stream([
        (np.concatenate([cq_, ckv_, krs[0], krs[1], sq_, sk_], axis=1), "tiles"), (sv_, "rows"),
        (np.concatenate([uq[..., :64].reshape(384, 512), uq[..., 64:].reshape(384, 256),
                         swap(uq[..., 64:]).reshape(384, 256)], axis=1), "tiles"),
        (ukv[..., :64].reshape(256, 512), "tiles"), (ukv[..., 64:].reshape(256, 512), "rows"),
        (gt_, "tiles"), (interleave(x["w_sb_o"][0], x["w_mla_o"][0]), "tiles"), (x["w_out"][0], "tiles")])
    w2 = x["w_in_2"][0]
    at = np.cumsum([0, 512, 512, 512, 512, 512, 8, 1024, 1024])
    val, gat, q2, k2, v2, wf, gc, ga = [w2[:, at[i]:at[i + 1]] for i in range(8)]
    mix2 = block_stream([
        (np.concatenate([interleave(val, gat), q2, k2], axis=1), "tiles"), (v2, "rows"),
        (np.concatenate([gc, ga], axis=1), "tiles"),
        (interleave(x["w_conv_out_2"][0], x["w_attn_out_2"][0]), "tiles"), (x["w_out_2"][0], "tiles")])

    def ffn(n):
        return block_stream([(interleave(x[f"{n}_w_gate"][0], x[f"{n}_w_up"][0]), "tiles"),
                             (x[f"{n}_w_down"][0], "tiles")])

    stream = np.ascontiguousarray(np.concatenate([ffn("ffn1"), mix1, ffn("ffn2"), mix2]))
    cols = {
        "f1_pre": column(x["ffn1_pre_g"]), "f1_post": column(x["ffn1_post_g"]), "mix_pre": column(x["mix_pre_g"]),
        "b_gate": column(x["b_gate"]), "q_g": column(x["q_norm_g"]), "kv_g": column(x["kv_norm_g"]),
        "mix_post": column(x["mix_post_g"]), "f2_pre": column(x["ffn2_pre_g"]),
        "f2_post": column(x["ffn2_post_g"]), "b_ada": column(x["b_ada_2"]), "n1_g": column(x["norm1_g_2"]),
        "conv_b": column(x["conv_b_2"]), "ln_g": column(x["conv_ln_g_2"]), "ln_b": column(x["conv_ln_b_2"]),
        "n2_g": column(x["norm2_g_2"]), "final_g": column(x["final_g_2"]),
        "conv_w": x["conv_w_2"][0].reshape(CONV_K, CT, P).transpose(2, 1, 0).reshape(P, -1),
        "w_f": wf.reshape(KD, P, HEADS).transpose(1, 0, 2).reshape(P, -1),
        "w_router": x["w_router_2"][0].reshape(KD, P, E).transpose(1, 0, 2).reshape(P, -1),
        "b_router": np.tile(x["b_router_2"], (P, 1)),
        "b_forget": np.concatenate([x["b_forget_2"][0], np.zeros(P - HEADS, np.float32)])[:, None],
    }
    arrays = {
        "xT_in": np.ascontiguousarray(np.concatenate([x["meta_tokens"], x["x"][0]]).T),
        "stream": stream,
        "ada": np.ascontiguousarray(x["w_ada_2"][0].T.reshape(48, P, D)),
        "c_in": np.ascontiguousarray(x["c_2"][0]),
        "cols_in": np.ascontiguousarray(np.concatenate([cols[k] for k in COLS], axis=1)),
        "const_in": shape_constants(),
        "w_exp_in": np.ascontiguousarray(x["w_exp_in_2"][0]).reshape(E * 8, P, 2 * D),
        "w_exp_out": np.ascontiguousarray(x["w_exp_out_2"][0]).reshape(E * 8, P, D),
        "b_exp": np.ascontiguousarray(np.concatenate([x["b_exp_in_2"][0], x["b_exp_out_2"][0]], axis=1)),
    }
    nc = bacc.Bacc("TRN2", target_bir_lowering=False, num_devices=1)
    args = {n: nc.dram_tensor(n, a.shape, mybir.dt.from_np(a.dtype), kind="ExternalInput").ap()
            for n, a in arrays.items()}
    out = nc.dram_tensor("outT", (D, SEQ), mybir.dt.float32, kind="ExternalOutput").ap()
    build(nc, out=out, **args)
    r = run_bass_kernel_spmd(nc, [arrays], core_ids=[0])
    return np.ascontiguousarray(r.results[0]["outT"].T)[None]
```
